# Optimizing a Trainium2 kernel written in Bass

```python
import jax
import jax.numpy as jnp
from jax import lax
import numpy as np

D_MODEL = 2048
BATCH = 1
SEQ = 256
DEPTH = 2
DEC_BATCH = 8
DEC_SEQ = 1
PAST_LEN = 2048
PAGE_SIZE = 128

N_EVEN = (DEPTH + 1) // 2
N_ODD = DEPTH // 2
MIX_W = D_MODEL
GLA_HEADS = 4
GLA_W = MIX_W // 2
GLA_DV = GLA_W // GLA_HEADS
GLA_KEY_W = GLA_W // 2
GLA_DK = GLA_KEY_W // GLA_HEADS
GLA_GATE_RANK = 16
GLA_GATE_TEMP = 16.0
POOL_W = MIX_W - GLA_W
POOL_WINDOWS = (2, 4, 8, 16)
POOL_GROUPS = len(POOL_WINDOWS)
POOL_GC = POOL_W // POOL_GROUPS
POOL_PAST = max(POOL_WINDOWS) - 1
EVEN_IN = 2 * GLA_KEY_W + 2 * GLA_W + GLA_GATE_RANK + POOL_W
HGRN_W = MIX_W // 2
HGRN_DK = 128
HGRN_HEADS = HGRN_W // HGRN_DK
HGRN_DV = HGRN_W // HGRN_HEADS
CONF_W = MIX_W - HGRN_W
CONV_W = 31
CONV_PAST = CONV_W - 1
ODD_IN = 4 * HGRN_W + 2 * CONF_W
D_FF = 4 * D_MODEL
LA_CHUNK = 64
EPS = 1e-6
MIN_GATE = 1e-30

kernel_name = 'hybrid_gla_pool_hgrn2_conformer_decode_step'

def split_cols(z, widths):
    out, start = [], 0
    for w in widths:
        out.append(z[..., start:start + w])
        start += w
    return out

def rms_norm(x, g):
    xf = x.astype(jnp.float32)
    y = xf * lax.rsqrt(jnp.mean(xf * xf, axis=-1, keepdims=True) + EPS)
    return (y * g.astype(jnp.float32)).astype(x.dtype)

def layer_norm(x, g, b):
    xf = x.astype(jnp.float32)
    mu = jnp.mean(xf, axis=-1, keepdims=True)
    var = jnp.mean(jnp.square(xf - mu), axis=-1, keepdims=True)
    return ((xf - mu) * lax.rsqrt(var + EPS) * g.astype(jnp.float32) + b.astype(jnp.float32)).astype(x.dtype)

def gated_linear_recurrence(q, k, v, log_a, s0):
    out_dtype = v.dtype
    B, T, H, _ = q.shape
    Dv = v.shape[-1]
    C = min(LA_CHUNK, T)
    n = -(-T // C)
    pad = n * C - T

    def blocks(a):
        a = jnp.pad(a.astype(jnp.float32), ((0, 0), (0, pad), (0, 0), (0, 0)))
        return a.reshape(B, n, C, H, a.shape[-1]).transpose(1, 0, 3, 2, 4)

    causal = jnp.tril(jnp.ones((C, C), dtype=bool))[:, :, None]

    def step(S, blk):
        qc, kc, vc, gc = blk
        b = jnp.cumsum(gc, axis=2)
        o_inter = jnp.einsum('bhtd,bhde->bhte', qc * jnp.exp(b), S)
        diff = b[:, :, :, None, :] - b[:, :, None, :, :]
        decay = jnp.where(causal, jnp.exp(jnp.where(causal, diff, 0.0)), 0.0)
        scores = jnp.einsum('bhtd,bhtsd,bhsd->bhts', qc, decay, kc)
        o_intra = jnp.einsum('bhts,bhse->bhte', scores, vc)
        b_end = b[:, :, -1:, :]
        S_new = jnp.exp(b_end[:, :, 0, :, None]) * S + jnp.einsum('bhsd,bhse->bhde', kc * jnp.exp(b_end - b), vc)
        return S_new, o_inter + o_intra

    s_fin, o = lax.scan(step, s0.astype(jnp.float32), (blocks(q), blocks(k), blocks(v), blocks(log_a)))
    o = o.transpose(1, 0, 3, 2, 4).reshape(B, n * C, H, Dv)[:, :T]
    return o.astype(out_dtype), s_fin.astype(s0.dtype)

def multiscale_pool(u, prefix, pos0, pool_w, pool_scale):
    B, T, _ = u.shape
    uf = jnp.concatenate([prefix.astype(jnp.float32), u.astype(jnp.float32)], axis=1)
    cs = jnp.pad(jnp.cumsum(uf, axis=1), ((0, 0), (1, 0), (0, 0)))
    cur = uf[:, POOL_PAST:]
    pos = jnp.arange(T, dtype=jnp.int32) + pos0
    groups = []
    for g, w in enumerate(POOL_WINDOWS):
        c0, c1 = g * POOL_GC, (g + 1) * POOL_GC
        win = cs[:, POOL_PAST + 1:, c0:c1] - cs[:, POOL_PAST + 1 - w:POOL_PAST + 1 - w + T, c0:c1]
        cnt = jnp.minimum(pos + 1, w).astype(jnp.float32)[None, :, None]
        groups.append(win / cnt - cur[:, :, c0:c1])
    d = jnp.stack(groups, axis=2)
    y = jnp.einsum('btgc,gce->btge', d, pool_w.astype(jnp.float32)).reshape(B, T, POOL_W)
    y = y * pool_scale.astype(jnp.float32)
    return y.astype(u.dtype), uf[:, -POOL_PAST:].astype(prefix.dtype)

def even_mixer(h, pos0, s_gla, s_pool, w_in, w_gate_up, b_gate, gla_norm, pool_w, pool_scale, w_out):
    B, T, _ = h.shape
    z = h @ w_in
    q, k, v, r, a_lr, u = split_cols(z, [GLA_KEY_W, GLA_KEY_W, GLA_W, GLA_W, GLA_GATE_RANK, POOL_W])
    q = q.reshape(B, T, GLA_HEADS, GLA_DK) * (GLA_DK ** -0.5)
    k = k.reshape(B, T, GLA_HEADS, GLA_DK)
    v = v.reshape(B, T, GLA_HEADS, GLA_DV)
    log_a = jax.nn.log_sigmoid((a_lr @ w_gate_up + b_gate).astype(jnp.float32)) / GLA_GATE_TEMP
    log_a = log_a.reshape(B, T, GLA_HEADS, GLA_DK)
    o, s_gla_new = gated_linear_recurrence(q, k, v, log_a, s_gla)
    o = rms_norm(o, gla_norm) * jax.nn.silu(r.reshape(B, T, GLA_HEADS, GLA_DV))
    o = o.reshape(B, T, GLA_W)
    p, s_pool_new = multiscale_pool(u, s_pool, pos0, pool_w, pool_scale)
    y = jnp.concatenate([o, p.astype(o.dtype)], axis=-1) @ w_out
    return y, s_gla_new, s_pool_new

def odd_mixer(h, s_hgrn, s_conv, lb, w_in, hgrn_norm, conv_w, conv_b, ln_g, ln_b, w_out):
    B, T, _ = h.shape
    z = h @ w_in
    q, fz, i, g, glu = split_cols(z, [HGRN_W, HGRN_W, HGRN_W, HGRN_W, 2 * CONF_W])
    fz32 = fz.astype(jnp.float32)
    f = lb + (1.0 - lb) * jax.nn.sigmoid(fz32)
    log_f = jnp.log(jnp.maximum(f, MIN_GATE))
    k = (1.0 - lb) * jax.nn.sigmoid(-fz32)
    o, s_hgrn_new = gated_linear_recurrence(
        q.reshape(B, T, HGRN_HEADS, HGRN_DK), k.reshape(B, T, HGRN_HEADS, HGRN_DK),
        i.reshape(B, T, HGRN_HEADS, HGRN_DV), log_f.reshape(B, T, HGRN_HEADS, HGRN_DK), s_hgrn)
    o = rms_norm(o, hgrn_norm) * jax.nn.silu(g.reshape(B, T, HGRN_HEADS, HGRN_DV))
    o = o.reshape(B, T, HGRN_W)
    ga, gb = split_cols(glu, [CONF_W, CONF_W])
    cv_in = ga * jax.nn.sigmoid(gb)
    cvf = jnp.concatenate([s_conv.astype(cv_in.dtype), cv_in], axis=1)
    cv = lax.conv_general_dilated(cvf, conv_w[:, None, :].astype(cvf.dtype), (1,), 'VALID',
                                  dimension_numbers=('NWC', 'WIO', 'NWC'), feature_group_count=CONF_W)
    cv = jax.nn.silu(layer_norm(cv + conv_b.astype(cv.dtype), ln_g, ln_b))
    y = jnp.concatenate([o, cv.astype(o.dtype)], axis=-1) @ w_out
    return y, s_hgrn_new, cvf[:, -CONV_PAST:].astype(s_conv.dtype)

def sq_relu_mlp(h, w_up, w_down):
    return jnp.square(jax.nn.relu(h @ w_up)) @ w_down

def trunk(x, c, pos0, st_gla, st_pool, st_hgrn, st_conv, p):
    new_gla, new_pool, new_hgrn, new_conv = [], [], [], []
    c_act = jax.nn.silu(c)
    for l in range(DEPTH):
        mod = (c_act @ p['w_ada'][l] + p['b_ada'][l])[:, None, :]
        sh1, sc1, g1, sh2, sc2, g2 = split_cols(mod, [D_MODEL] * 6)
        h = rms_norm(x, p['norm_mix'][l]) * (1.0 + sc1) + sh1
        if l % 2 == 0:
            e = l // 2
            y, sg, sp = even_mixer(h, pos0, st_gla[e], st_pool[e], p['ev_w_in'][e], p['ev_w_gate_up'][e],
                                   p['ev_b_gate'][e], p['ev_gla_norm'][e], p['ev_pool_w'][e],
                                   p['ev_pool_scale'][e], p['ev_w_out'][e])
            new_gla.append(sg)
            new_pool.append(sp)
        else:
            o = l // 2
            y, shg, scv = odd_mixer(h, st_hgrn[o], st_conv[o], p['lower_bounds'][o], p['od_w_in'][o],
                                    p['od_hgrn_norm'][o], p['od_conv_w'][o], p['od_conv_b'][o],
                                    p['od_ln_g'][o], p['od_ln_b'][o], p['od_w_out'][o])
            new_hgrn.append(shg)
            new_conv.append(scv)
        x = x + g1 * y
        h = rms_norm(x, p['norm_mlp'][l]) * (1.0 + sc2) + sh2
        x = x + g2 * sq_relu_mlp(h, p['mlp_w_up'][l], p['mlp_w_down'][l])
    y = rms_norm(x, p['norm_final'])
    return y, jnp.stack(new_gla), jnp.stack(new_pool), jnp.stack(new_hgrn), jnp.stack(new_conv)

def setup_inputs(seed: int = 0) -> dict:
    key = jax.random.key(seed)
    ks = iter(jax.random.split(key, 40))

    def nrm(shape, s):
        return jax.random.normal(next(ks), shape, jnp.float32) * s

    def gain(shape):
        return 1.0 + nrm(shape, 0.1)

    return {
        'x_prompt': nrm((BATCH, SEQ, D_MODEL), 1.0),
        'x_sample': nrm((DEC_BATCH, DEC_SEQ, D_MODEL), 1.0),
        'c_prompt': nrm((BATCH, D_MODEL), 1.0),
        'c_sample': nrm((DEC_BATCH, D_MODEL), 1.0),
        'state_gla': nrm((N_EVEN, DEC_BATCH, GLA_HEADS, GLA_DK, GLA_DV), 0.5),
        'state_pool': nrm((N_EVEN, DEC_BATCH, POOL_PAST, POOL_W), 1.0),
        'state_hgrn': nrm((N_ODD, DEC_BATCH, HGRN_HEADS, HGRN_DK, HGRN_DV), 0.5),
        'state_conv': nrm((N_ODD, DEC_BATCH, CONV_PAST, CONF_W), 0.5),
        'w_ada': nrm((DEPTH, D_MODEL, 6 * D_MODEL), 0.5 * D_MODEL ** -0.5),
        'b_ada': nrm((DEPTH, 6 * D_MODEL), 0.02),
        'norm_mix': gain((DEPTH, D_MODEL)),
        'norm_mlp': gain((DEPTH, D_MODEL)),
        'norm_final': gain((D_MODEL,)),
        'ev_w_in': nrm((N_EVEN, D_MODEL, EVEN_IN), D_MODEL ** -0.5),
        'ev_w_gate_up': nrm((N_EVEN, GLA_GATE_RANK, GLA_KEY_W), GLA_GATE_RANK ** -0.5),
        'ev_b_gate': nrm((N_EVEN, GLA_KEY_W), 0.1),
        'ev_gla_norm': gain((N_EVEN, GLA_DV)),
        'ev_pool_w': nrm((N_EVEN, POOL_GROUPS, POOL_GC, POOL_GC), POOL_GC ** -0.5),
        'ev_pool_scale': gain((N_EVEN, POOL_W)),
        'ev_w_out': nrm((N_EVEN, MIX_W, D_MODEL), MIX_W ** -0.5),
        'od_w_in': nrm((N_ODD, D_MODEL, ODD_IN), D_MODEL ** -0.5),
        'od_lb_raw': nrm((N_ODD, HGRN_W), 0.5),
        'od_hgrn_norm': gain((N_ODD, HGRN_DV)),
        'od_conv_w': nrm((N_ODD, CONV_W, CONF_W), CONV_W ** -0.5),
        'od_conv_b': nrm((N_ODD, CONF_W), 0.02),
        'od_ln_g': gain((N_ODD, CONF_W)),
        'od_ln_b': nrm((N_ODD, CONF_W), 0.02),
        'od_w_out': nrm((N_ODD, MIX_W, D_MODEL), MIX_W ** -0.5),
        'mlp_w_up': nrm((DEPTH, D_MODEL, D_FF), D_MODEL ** -0.5),
        'mlp_w_down': nrm((DEPTH, D_FF, D_MODEL), D_FF ** -0.5),
    }

def reference(x_prompt, x_sample, c_prompt, c_sample, state_gla, state_pool, state_hgrn, state_conv,
              w_ada, b_ada, norm_mix, norm_mlp, norm_final,
              ev_w_in, ev_w_gate_up, ev_b_gate, ev_gla_norm, ev_pool_w, ev_pool_scale, ev_w_out,
              od_w_in, od_lb_raw, od_hgrn_norm, od_conv_w, od_conv_b, od_ln_g, od_ln_b, od_w_out,
              mlp_w_up, mlp_w_down):
    sm = jax.nn.softmax(od_lb_raw.astype(jnp.float32), axis=0)
    lower_bounds = jnp.cumsum(sm, axis=0) - sm[0:1]
    p = dict(w_ada=w_ada, b_ada=b_ada, norm_mix=norm_mix, norm_mlp=norm_mlp, norm_final=norm_final,
             ev_w_in=ev_w_in, ev_w_gate_up=ev_w_gate_up, ev_b_gate=ev_b_gate, ev_gla_norm=ev_gla_norm,
             ev_pool_w=ev_pool_w, ev_pool_scale=ev_pool_scale, ev_w_out=ev_w_out,
             od_w_in=od_w_in, lower_bounds=lower_bounds, od_hgrn_norm=od_hgrn_norm, od_conv_w=od_conv_w,
             od_conv_b=od_conv_b, od_ln_g=od_ln_g, od_ln_b=od_ln_b, od_w_out=od_w_out,
             mlp_w_up=mlp_w_up, mlp_w_down=mlp_w_down)
    bp = x_prompt.shape[0]
    zero_gla = jnp.zeros((N_EVEN, bp, GLA_HEADS, GLA_DK, GLA_DV), state_gla.dtype)
    zero_pool = jnp.zeros((N_EVEN, bp, POOL_PAST, POOL_W), state_pool.dtype)
    zero_hgrn = jnp.zeros((N_ODD, bp, HGRN_HEADS, HGRN_DK, HGRN_DV), state_hgrn.dtype)
    zero_conv = jnp.zeros((N_ODD, bp, CONV_PAST, CONF_W), state_conv.dtype)
    y_prompt, gla_p, pool_p, hgrn_p, conv_p = trunk(x_prompt, c_prompt, 0, zero_gla, zero_pool,
                                                     zero_hgrn, zero_conv, p)
    y_sample, gla_s, pool_s, hgrn_s, conv_s = trunk(x_sample, c_sample, PAST_LEN, state_gla, state_pool,
                                                     state_hgrn, state_conv, p)
    return (y_prompt, y_sample, gla_p, pool_p, hgrn_p, conv_p, gla_s, pool_s, hgrn_s, conv_s)


_drawn_inputs = setup_inputs


def setup_inputs(seed=0):
    import zlib

    import numpy as np

    out = dict(_drawn_inputs(seed))
    spreads = {}
    factors = {'ev_gla_norm': 3.482,
     'ev_pool_scale': 2.801,
     'od_hgrn_norm': 4.909,
     'od_conv_b': 8.0,
     'od_ln_g': 4.042,
     'od_ln_b': 29.901}
    for name, (base, spread) in spreads.items():
        noise = np.random.default_rng([zlib.crc32(name.encode()), seed]).standard_normal(out[name].shape)
        drawn = base * np.exp(spread * noise) if base else spread * noise
        out[name] = jnp.asarray(drawn.astype(out[name].dtype))
    for name, factor in factors.items():
        out[name] = (out[name] * factor).astype(out[name].dtype)
    return out
```

```python
from contextlib import ExitStack

import numpy as np

import concourse.bass as bass
from concourse import mybir

F32 = mybir.dt.float32
F32R = mybir.dt.float32r
I32 = mybir.dt.int32
ALU = mybir.AluOpType
ACT = mybir.ActivationFunctionType
AX = mybir.AxisListType

P = 128
D = 2048
KT = D // P
TP = 256
NS = 8
T = TP + NS
NC = NS + 1
GC = 256
MT = GC // P
UK = 4
NU = KT // UK
UW = UK * GC
CH = 128
NCH = TP // CH
LEVELS = 7
HG = 4
DK = 128
WINDOWS = (2, 4, 8, 16)
POOL_PAST = 15
TAPS = 31
CONV_PAST = 30
EPS = 1e-6
MIN_GATE = 1e-30
TWO60 = float(2 ** 60)
FF_CHUNKS = 4
POOL_TAIL = POOL_PAST + NS
CONV_TAIL = CONV_PAST + NS

VA = {"norm_mix": 0, "norm_mlp": 32, "norm_final": 64}
VB = {"ev_b_gate": 0, "ev_gla_norm": 4, "ev_pool_scale": 6, "od_lb_raw": 14, "od_hgrn_norm": 22,
      "od_conv_b": 23, "od_ln_g": 31, "od_ln_b": 39}
VB_ROWS = 47
SH1, SC1, G1, SH2, SC2, G2 = range(0, 96, 16)


def make_plan():
    order = [("ada0a", "ada", 16), ("in0", "gemm", 16), ("ada0b", "ada", 32), ("out0", "gemm", 8)]
    for f in range(FF_CHUNKS):
        order += [(f"ada1u{f}", "ada", 2), (f"up0_{f}", "gemm", 8),
                  (f"ada1d{f}", "ada", 2), (f"down0_{f}", "gemm", 8)]
    order += [("glu", "gemm", 8), ("in1", "gemm", 16), ("ada1b", "ada", 32), ("out1", "gemm", 8)]
    for f in range(FF_CHUNKS):
        order += [(f"up1_{f}", "gemm", 8), (f"down1_{f}", "gemm", 8)]
    plan, g, n, a = {}, 0, 0, 0
    for name, kind, count in order:
        plan[name] = (kind, count, g, n, a)
        g += count
        n += count if kind == "gemm" else 0
        a += count if kind == "ada" else 0
    return plan, g, n, a


PLAN, GROUPS, GEMMS, ADAS = make_plan()


def constants():
    s, t = np.arange(CH)[:, None], np.arange(CH)[None, :]
    masks = np.zeros((CH, LEVELS, CH), np.int32)
    for lv in range(LEVELS):
        h = 1 << lv
        masks[:, lv, :] = (s // (2 * h) == t // (2 * h)) & (s % (2 * h) < h) & (t % (2 * h) >= h)
    inv = np.zeros((P, len(WINDOWS), 16), np.float32)
    for g, w in enumerate(WINDOWS):
        inv[:, g, :] = 1.0 / np.minimum(np.arange(16) + 1, w).astype(np.float32)
    return {"ident": np.eye(P, dtype=np.float32), "masks": masks.reshape(CH, LEVELS * CH),
            "inv_count": inv.reshape(P, -1)}


START_BANKS = 2 + KT
CONSTS = 1 + len(VA) + len(VB) + 3
SMALL_OUTS = 9
OPAIRS = [0, 4, 6, 8]


class Count:
    def __init__(self):
        self.n = 0

    def next(self):
        self.n += 1
        return self.n


def build(nc, io, out):
    stack = ExitStack()
    with stack:
        used = [(nc.sbuf_base + 31) // 32 * 32]

        def at(name, shape, dt, offset):
            return nc.alloc_sbuf_tensor_at(name, shape, dt, offset=offset)

        def sb(name, shape, dt=F32):
            size = int(np.prod(shape[1:])) * 4
            offset = used[0]
            used[0] += (size + 31) // 32 * 32
            assert used[0] <= nc.sbuf_top, (name, used[0], nc.sbuf_top)
            return at(name, shape, dt, offset)

        def arena(size):
            offset = used[0]
            used[0] += (size + 31) // 32 * 32
            assert used[0] <= nc.sbuf_top
            return offset

        def sem(name):
            return stack.enter_context(nc.semaphore(name))

        x = sb("x", [P, KT, T])
        raw = sb("raw", [P, 2, NU, UW])
        w_hi = sb("w_hi", [P, NU, UW], F32R)
        w_lo = sb("w_lo", [P, NU, UW], F32R)
        mod = sb("mod", [P, 2, 96, NC])
        amod = sb("amod", [P, KT, NC])
        cT = sb("cT", [P, KT, NC])
        bada = sb("bada", [P, 2, 96])
        va = sb("va", [P, 80])
        vb = sb("vb", [P, VB_ROWS])
        ident = sb("ident", [P, P])
        ones = sb("ones", [P, P])
        zeros = sb("zeros", [P, T])
        masks = sb("masks", [P, LEVELS, CH], I32)
        inv_count = sb("inv_count", [P, len(WINDOWS), 16])
        lb = sb("lb", [P, 8])
        oml = sb("oml", [P, 8])
        sm = sb("sm", [P, 8])
        eps_t = sb("eps_t", [P, 1])
        o_rs = arena(2 * T * 4)
        rstd = at("rstd", [P, T], F32, o_rs)
        lnv = at("lnv", [P, T], F32, o_rs + T * 4)
        pb = at("pb", [P, 2, TP], F32, o_rs)
        o_hid = arena(MT * T * 4)
        hid = at("hid", [P, MT, T], F32, o_hid)
        pa = at("pa", [P, 2, TP], F32, o_hid)
        g8 = sb("g8", [P, MT, NS])
        t8 = sb("t8", [P, KT, NS])
        wsum = sb("wsum", [P, MT, NS])
        decay8 = sb("decay8", [P, HG, NS])
        logp = sb("logp", [P, HG, T])
        o_sq = arena(2 * MT * T * 4)
        sq = at("sq", [P, 2, MT, T], F32, o_sq)
        hs = at("hs", [P, 4, TP], F32, o_sq)
        o_mw = arena(8192)
        pool_w = at("pool_w", [P, 4, 2, 256], F32, o_mw)
        conv_w = at("conv_w", [P, 8, TAPS], F32, o_mw)
        acc1 = at("acc1", [P, TP], F32, o_mw + 1024)
        cprod = at("cprod", [P, NS, CONV_PAST], F32, o_mw + 2048)
        csum = at("csum", [P, NS], F32, o_mw + 3072)
        mean = at("mean", [P, T], F32, o_mw + 3200)
        cw_rows = at("cw_rows", [TAPS, 1024], F32, o_mw + 4352 - 256)
        o_gw = arena(2048)
        gate_up = at("gate_up", [16, 512], F32, o_gw)
        o_h = arena(2 * KT * T * 4)
        h_hi = at("h_hi", [P, KT, T], F32R, o_h)
        h_lo = at("h_lo", [P, KT, T], F32R, o_h + KT * T * 4)
        dec = at("dec", [P, 2, HG, TP], F32, o_h)
        gz = at("gz", [P, HG, T], F32, o_h)
        gl = at("gl", [P, HG, T], F32, o_h + 8448)
        fac = at("fac", [P, 2, HG, TP], F32, o_h + 8192)
        st = at("st", [P, 2, 1024], F32, o_h + 8192)
        scores = at("scores", [P, NCH, HG, CH], F32, o_h + 16384)
        kmask = at("kmask", [NS, 2, HG * DK], F32, o_h + 16384)
        s1 = at("s1", [P, 1024], F32, o_h + 20480)
        k8 = at("k8", [NS, HG * DK], F32, o_h + 20480)
        kdT = at("kdT", [P, NCH, HG * DK], F32, o_h + 24576)
        v8 = at("v8", [NS, 1024], F32, o_h + 24576)
        s2 = at("s2", [P, 1024], F32, o_h + 28672)
        o_z = arena(48 * T * 4)
        z = at("z", [P, 48, T], F32, o_z)
        zf = z[:, :, :].rearrange("p a t -> p (a t)")
        f_hi = at("f_hi", [P, KT, T], F32R, o_z)
        f_lo = at("f_lo", [P, KT, T], F32R, o_z + KT * T * 4)
        x_rows = at("x_rows", [P, NCH, D], F32, o_z)
        xs_rows = at("xs_rows", [NS, D], F32, o_z + 16384)
        c_rows = at("c_rows", [NC, D], F32, o_z + 24576)
        va_rows = at("va_rows", [80, P], F32, o_z + 32768)
        vb_rows = at("vb_rows", [VB_ROWS, P], F32, o_z + 33280)
        ba_rows = at("ba_rows", [96, 2, P], F32, o_z + 33792)
        cs_rows = at("cs_rows", [NC, D], F32, o_z + 34816)
        y_rows = at("y_rows", [P, NCH, D], F32, o_z)
        ys_rows = at("ys_rows", [NS, D], F32, o_z + 16384)
        vT_at = {0: o_z + 40 * T * 4, 1: o_z + 32 * T * 4}
        vT = {layer: at(f"vT{layer}", [P, NCH, 1024], F32, vT_at[layer]) for layer in range(2)}
        a_w = at("a_w", [P, KT, 16], F32, o_z + 46 * T * 4)
        pastc = at("pastc", [120, 2, 1024], F32, o_h + 8192)
        pastu = at("pastu", [120, 1024], F32, o_h + 28672)
        AW = KT * 16 + P - 16
        a_hi = at("a_hi", [P, AW], F32R, o_sq)
        a_lo = at("a_lo", [P, AW], F32R, o_sq + AW * 4)
        a_lr = at("a_lr", [16, T], F32, o_sq + 2 * AW * 4)
        tail = sb("tail", [CONV_TAIL, 1024])

        ps = stack.enter_context(nc.psum_tensor("ps", [P, 4, 512], F32))
        pm = stack.enter_context(nc.psum_tensor("pm", [P, 4, 512], F32))

        raw_in = [[sem(f"raw_in{p}{h}") for h in range(2)] for p in range(2)]
        hi_ready = sem("hi_ready")
        lo_ready = sem("lo_ready")
        split_used = sem("split_used")
        ada_used = sem("ada_used")
        evacuated = sem("evacuated")
        rows_in = sem("rows_in")
        const_in = sem("const_in")
        c_silu = sem("c_silu")
        tr_ready = sem("tr_ready")
        tr_taken = sem("tr_taken")
        filled = sem("filled")
        sq_ready = sem("sq_ready")
        ss_done = sem("ss_done")
        x_ready = sem("x_ready")
        gate8_done = sem("gate8_done")
        rstd_ready = sem("rstd_ready")
        t8_ready = sem("t8_ready")
        h8_hi = sem("h8_hi")
        hs_ready = sem("hs_ready")
        hh_ready = sem("hh_ready")
        h_ready = sem("h_ready")
        hid_relu = sem("hid_relu")
        hid_sq = sem("hid_sq")
        hid_hi = sem("hid_hi")
        hid_ready = sem("hid_ready")
        mix_hi = sem("mix_hi")
        mix_ready = sem("mix_ready")
        mix_f32 = sem("mix_f32")
        dve_step = sem("dve_step")
        act_step = sem("act_step")
        pool_step = sem("pool_step")
        aw_in = sem("aw_in")
        aw_hi = sem("aw_hi")
        aw_lo = sem("aw_lo")
        alr_psum = sem("alr_psum")
        alr_ready = sem("alr_ready")
        gate_psum = sem("gate_psum")
        gz_ready = sem("gz_ready")
        gl_ready = sem("gl_ready")
        logp_ready = sem("logp_ready")
        q_scaled = sem("q_scaled")
        past_in = sem("past_in")
        past_psum = sem("past_psum")
        past_taken = sem("past_taken")
        tail_psum = sem("tail_psum")
        tail_ready = sem("tail_ready")
        pool_d = sem("pool_d")
        pool_psum = sem("pool_psum")
        pool_taken = sem("pool_taken")
        k_ready = sem("k_ready")
        sig_ready = sem("sig_ready")
        ln_in = sem("ln_in")
        ln_out = sem("ln_out")
        vtr_psum = sem("vtr_psum")
        vtr_ready = sem("vtr_ready")
        dec8_ready = sem("dec8_ready")
        kmask_ready = sem("kmask_ready")
        kv_psum = sem("kv_psum")
        st_in = [sem(f"st_in{i}") for i in range(2)]
        st_ready = sem("st_ready")
        st_out = [sem(f"st_out{i}") for i in range(2)]
        o8_psum = sem("o8_psum")
        o8_taken = sem("o8_taken")
        sc_psum = sem("sc_psum")
        sc_taken = sem("sc_taken")
        prefix_ready = sem("prefix_ready")
        dif_ready = sem("dif_ready")
        exp_ready = sem("exp_ready")
        fac_ready = sem("fac_ready")
        kd_psum = sem("kd_psum")
        kd_ready = sem("kd_ready")
        s1_psum = sem("s1_psum")
        s1_ready = sem("s1_ready")
        kv1_psum = sem("kv1_psum")
        s2_ready = sem("s2_ready")
        o_psum = sem("o_psum")
        o_ready = sem("o_ready")
        osq_ready = sem("osq_ready")
        oss_psum = sem("oss_psum")
        ors_ready = sem("ors_ready")
        silu_ready = sem("silu_ready")
        cw_psum = sem("cw_psum")
        gb_sig = sem("gb_sig")
        cv_in = sem("cv_in")
        conv_step = sem("conv_step")
        ln_psum = sem("ln_psum")
        ln_mean = sem("ln_mean")
        ln_cent = sem("ln_cent")
        ln_sq = sem("ln_sq")
        ln_rstd = sem("ln_rstd")
        ln_done = sem("ln_done")
        cv_ready = sem("cv_ready")
        cv_done = sem("cv_done")
        conv_zero = sem("conv_zero")
        lb_exp = sem("lb_exp")
        y_ready = sem("y_ready")
        y_psum = sem("y_psum")
        y_taken = sem("y_taken")
        small_out = sem("small_out")
        y_out = sem("y_out")

        HEADS = [dict(layer=0, nv=8, dv=256, q=0, k=4, v=8), dict(layer=1, nv=4, dv=128, q=0, k=8, v=16),
                 dict(layer=1, nv=4, dv=128, q=4, k=12, v=20)]
        SETS = 1 + LEVELS
        BANKS_Z = 2 * KT

        def halves(t, w):
            v = t.rearrange("p h (n s w) -> p h n s w", s=2, w=w)
            return v[:, :, :, 0, :], v[:, :, :, 1, :]

        def heads_of(t, nv):
            return t.rearrange("p a t -> p (a t)")

        def bank2(p):
            return ps[:, MT * p:MT * p + MT, 0:T]

        block = stack.enter_context(nc.Block())

        @block.sync
        def _(sp):
            def group(g, i, p, view, cols, k0, prev):
                for h in range(2):
                    if prev is not None:
                        kind, at_ = prev
                        if kind == "gemm":
                            sp.wait_ge(lo_ready, NU * at_ + 2 * h + 2)
                        else:
                            sp.wait_ge(ada_used, 2 * at_ + h + 1)
                    sp.dma_start(raw[:, p, 2 * h:2 * h + 2, :].rearrange("p u (k n) -> p (u k) n", n=GC),
                                 view[:, bass.ds(k0 + 8 * h, 8), cols]).then_inc(raw_in[p][h], 16)

            def phase(kind, count, index, view, col, prev, k0=0):
                for p in range(2):
                    group(None, p, p, view, bass.ds(col(p), GC), k0, prev(p))
                if count > 2:
                    with sp.Fori(0, count // 2 - 1) as j:
                        for p in range(2):
                            i = 2 * j + (2 + p)
                            group(None, i, p, view, bass.ds(col(i), GC), k0, (kind, index + 2 * j + p))

            def kview(w):
                return w.rearrange("(k p) n -> p k n", p=P)

            def after(name):
                kind, count, g0, n0, a0 = PLAN[name]
                if g0 == 0:
                    return lambda p: None
                before = [v for v in PLAN.values() if v[2] + v[1] == g0][0][0]
                return lambda p: (before, (n0 if before == "gemm" else a0) - 2 + p)

            def static_phase(name, view, col, k0=0):
                kind, count, g0, n0, a0 = PLAN[name]
                phase(kind, count, n0 if kind == "gemm" else a0, view, col, after(name), k0)

            sp.dma_start(c_rows[0:1, :], io["c_prompt"]).then_inc(rows_in, 16)
            sp.dma_start(c_rows[1:NC, :], io["c_sample"]).then_inc(rows_in, 16)
            sp.dma_start(x_rows[:, :, :], io["x_prompt"][0].rearrange("(c p) d -> p c d", p=P)).then_inc(rows_in, 16)
            sp.dma_start(xs_rows[:, :], io["x_sample"].rearrange("b t d -> (b t) d")).then_inc(rows_in, 16)
            ada = [kview(io["w_ada"][l]) for l in range(2)]
            up = [kview(io["mlp_w_up"][l]) for l in range(2)]
            down = [kview(io["mlp_w_down"][l]) for l in range(2)]
            static_phase("ada0a", ada[0], lambda i: i * GC)
            kind, count, g0, n0, a0 = PLAN["in0"]
            w = kview(io["ev_w_in"][0])
            phase("gemm", 12, n0, w, lambda i: i * GC, after("in0"))
            phase("gemm", 4, n0 + 12, w, lambda i: (12 + i) * GC + 16, lambda p: ("gemm", n0 + 10 + p))
            static_phase("ada0b", ada[0], lambda i: (16 + i) * GC)
            static_phase("out0", kview(io["ev_w_out"][0]), lambda i: i * GC)

            def mlp(l, f, n, a):
                def ada_pair(b):
                    phase("ada", 2, a + 2 * b, ada[1], lambda i: (4 * f + 2 * b + i) * GC,
                          lambda p: ("gemm", n + 8 * b - 2 + p))
                if l == 0:
                    ada_pair(0)
                before_up = (lambda p: ("ada", a + p)) if l == 0 else (lambda p: ("gemm", n - 2 + p))
                phase("gemm", 8, n, up[l], lambda i: f * D + i * GC, before_up)
                if l == 0:
                    ada_pair(1)
                before_down = (lambda p: ("ada", a + 2 + p)) if l == 0 else (lambda p: ("gemm", n + 6 + p))
                phase("gemm", 8, n + 8, down[l], lambda i: i * GC, before_down, k0=f * KT)

            def mlp_layer(l):
                _, _, _, n0, a0 = PLAN[f"up{l}_0"]
                a0 = PLAN["ada1u0"][4]
                with sp.Fori(0, FF_CHUNKS) as f:
                    mlp(l, f, n0 + 16 * f, a0 + 4 * f)

            mlp_layer(0)
            w = kview(io["od_w_in"][0])
            static_phase("glu", w, lambda i: (16 + i) * GC)
            static_phase("in1", w, lambda i: i * GC)
            static_phase("ada1b", ada[1], lambda i: (16 + i) * GC)
            static_phase("out1", kview(io["od_w_out"][0]), lambda i: i * GC)
            mlp_layer(1)
            for r in range(3):
                sp.wait_ge(y_taken, 4 * (r + 1))
                if r < 2:
                    sp.dma_start(out["y_prompt"][0, r * P:(r + 1) * P, :], y_rows[:, r, :]).then_inc(y_out, 16)
                else:
                    sp.dma_start(out["y_sample"].rearrange("b t d -> (b t) d"), ys_rows[:, :]).then_inc(y_out, 16)
            sp.wait_ge(y_out, 48)
            sp.wait_ge(small_out, 16 * SMALL_OUTS)
            for i in range(2):
                sp.wait_ge(st_out[i], 16 * 4 * len(HEADS))

        @block.gpsimd
        def _(pool):
            steps = Count()

            def step(ins):
                ins.then_inc(pool_step, 1)
                pool.wait_ge(pool_step, steps.next())

            pool.dma_start(out["new_pool_sample"][0, :, 0:POOL_PAST - 1, :],
                           io["state_pool"][0, :, 1:POOL_PAST, :]).then_inc(small_out, 16)
            pool.dma_start(out["new_conv_sample"][0, :, 0:CONV_PAST - 1, :],
                           io["state_conv"][0, :, 1:CONV_PAST, :]).then_inc(small_out, 16)
            pool.dma_start(gate_up[:, :], io["ev_w_gate_up"][0]).then_inc(aw_in, 16)
            pool.dma_start(pool_w[:, :, :, :], io["ev_pool_w"][0].rearrange("g (c p) e -> p g c e", p=P)).then_inc(aw_in, 16)
            pool.wait_ge(tr_ready, START_BANKS)
            pool.dma_start(a_w[:, :, :], io["ev_w_in"][0][:, 3072:3088].rearrange("(k p) n -> p k n", p=P)).then_inc(aw_in, 16)

            def states(q):
                h = HEADS[q]
                n = HG * h["dv"]
                if h["layer"] == 0:
                    src, dst, hsl = io["state_gla"][0], out["new_gla_sample"][0], slice(0, HG)
                else:
                    src, dst, hsl = io["state_hgrn"][0], out["new_hgrn_sample"][0], slice(h["q"], h["q"] + HG)

                def load(b):
                    pool.dma_start(st[:, b % 2, 0:n].rearrange("p (h v) -> p h v", h=HG),
                                   src[b, hsl].rearrange("h k v -> k h v")).then_inc(st_in[b % 2], 16)

                pool.wait_ge(vtr_psum, 4 * q + 1)
                load(0)
                load(1)
                for b in range(NS):
                    pool.wait_ge(st_ready, NS * q + b + 1)
                    pool.dma_start(dst[b, hsl].rearrange("h k v -> k h v"),
                                   st[:, b % 2, 0:n].rearrange("p (h v) -> p h v", h=HG)).then_inc(st_out[b % 2], 16)
                    if b + 2 < NS:
                        pool.wait_ge(o8_psum, NS * q + b + 1)
                        pool.wait_ge(st_out[b % 2], 16 * (4 * q + b // 2 + 1))
                        load(b + 2)

            def prompt_state(q):
                h = HEADS[q]
                name, hsl = ("new_gla_prompt", slice(0, HG)) if h["layer"] == 0 else ("new_hgrn_prompt", slice(h["q"], h["q"] + HG))
                pool.wait_ge(s2_ready, q + 1)
                pool.dma_start(out[name][0, 0, hsl].rearrange("h k v -> k h v"),
                               s2[:, 0:HG * h["dv"]].rearrange("p (h v) -> p h v", h=HG)).then_inc(small_out, 16)

            pool.wait_ge(evacuated, PLAN["in0"][2] + 16)
            pool.wait_ge(alr_psum, 1)
            pool.dma_start(pastu[:, :], io["state_pool"][0].rearrange("b r c -> (b r) c")).then_inc(past_in, 16)
            states_first = None
            u = z[:, 24:32, 0:TP]
            for g, w in enumerate(WINDOWS):
                src, width, bufs = u[:, 2 * g:2 * g + 2, :], 1, [pa, pb]
                while width < w:
                    dst = bufs[0]
                    bufs.reverse()
                    nc.gpsimd.tensor_copy(dst[:, :, 0:width], src[:, :, 0:width])
                    step(nc.gpsimd.tensor_tensor(dst[:, :, width:TP], src[:, :, width:TP], src[:, :, 0:TP - width], ALU.add))
                    src, width = dst, 2 * width
                d = z[:, 32 + 2 * g:34 + 2 * g, 0:TP]
                inv = inv_count[:, g:g + 1, :].broadcast_to([P, 2, 16])
                nc.gpsimd.tensor_tensor(d[:, :, 0:16], src[:, :, 0:16], inv, ALU.mult)
                step(nc.gpsimd.tensor_scalar(d[:, :, 16:TP], src[:, :, 16:TP], 1.0 / w, None, ALU.mult))
                nc.gpsimd.tensor_tensor(d, d, u[:, 2 * g:2 * g + 2, :], ALU.subtract).then_inc(pool_d, 1)
            states(0)
            pool.wait_ge(tail_ready, 1)
            pool.dma_start(out["new_pool_prompt"][0, 0], tail[0:POOL_PAST, :]).then_inc(small_out, 16)
            pool.dma_start(out["new_pool_sample"][0, :, POOL_PAST - 1, :], tail[POOL_PAST:POOL_TAIL, :]).then_inc(small_out, 16)
            prompt_state(0)
            pool.wait_ge(pool_psum, 4)
            pool.dma_start(cw_rows[:, :], io["od_conv_w"][0]).then_inc(aw_in, 16)
            pool.wait_ge(split_used, NU * (PLAN["in1"][3] + 16))
            pool.dma_start(pastc[:, :, :], io["state_conv"][0].rearrange("(a b) r c -> (b r) a c", b=4)).then_inc(past_in, 16)
            pool.wait_ge(tail_ready, 2)
            pool.dma_start(out["new_conv_prompt"][0, 0], tail[0:CONV_PAST, :]).then_inc(small_out, 16)
            pool.dma_start(out["new_conv_sample"][0, :, CONV_PAST - 1, :], tail[CONV_PAST:CONV_TAIL, :]).then_inc(small_out, 16)
            for q in (1, 2):
                states(q)
                prompt_state(q)

        @block.tensor
        def _(pe):
            def gemm(count, n, g, xh, xl, ready, norm=None):
                def sums(i):
                    pe.wait_ge(sq_ready, norm + i + 1)
                    for m in range(MT):
                        last = nc.tensor.matmul(pm[:, 0, 0:T], ones[:, :], sq[:, i_parity[0], m, :], start=False,
                                                stop=False, skip_group_check=True)
                    last.then_inc(ss_done, 1)

                i_parity = [0]

                def body(i, p):
                    pe.wait_ge(evacuated, g + i - 1)
                    for u in range(NU):
                        ready(u)
                        pe.wait_ge(lo_ready, NU * (n + i) + (u + 1))
                        for m in range(MT):
                            acc = ps[:, MT * p + m, 0:T]
                            for kk in range(UK):
                                k = UK * u + kk
                                cols = slice(kk * GC + m * P, kk * GC + (m + 1) * P)
                                nc.tensor.matmul(acc, w_hi[:, u, cols], xh[:, k, :], start=(k == 0), stop=False)
                                nc.tensor.matmul(acc, w_hi[:, u, cols], xl[:, k, :], start=False, stop=False)
                                last = nc.tensor.matmul(acc, w_lo[:, u, cols], xh[:, k, :], start=False, stop=(k == KT - 1))
                        last.then_inc(split_used, 1)

                if norm is None:
                    with pe.Fori(0, count // 2) as j:
                        for p in range(2):
                            body(2 * j + p, p)
                    return
                for p in range(2):
                    body(p, p)
                nc.tensor.matmul(pm[:, 0, 0:T], ones[:, :], zeros[:, :], start=True, stop=False, skip_group_check=True)
                i_parity[0] = 0
                sums(0)
                with pe.Fori(0, count // 2 - 1) as j:
                    for p in range(2):
                        i = 2 * j + (2 + p)
                        body(i, p)
                        i_parity[0] = 1 - p
                        sums(i - 1)
                i_parity[0] = 1
                sums(count - 1)

            def ada_pair(a, g):
                for p in range(2):
                    if not (isinstance(g, int) and g + p < 2):
                        pe.wait_ge(evacuated, g + p - 1)
                    for h in range(2):
                        pe.wait_ge(raw_in[p][h], 8 * g + 16)
                        for m in range(MT):
                            for k8_ in range(8):
                                k = 8 * h + k8_
                                cols = slice((k % UK) * GC + m * P, (k % UK) * GC + (m + 1) * P)
                                last = nc.tensor.matmul(ps[:, MT * p + m, 0:NC], raw[:, p, k // UK, cols],
                                                        cT[:, k, :], start=(k == 0), stop=(k == KT - 1))
                        last.then_inc(ada_used, 1)

            def ada_static(name, j):
                kind, count, g0, n0, a0 = PLAN[name]
                ada_pair(a0 + 2 * j, g0 + 2 * j)

            def turn(dst, src, rows):
                return nc.tensor.transpose(dst, src, ident[0:rows, 0:rows])

            pe.wait_ge(const_in, 16 * CONSTS)
            pe.wait_ge(filled, 1)
            turn(pm[:, 0, 0:80], va_rows[:, :], 80)
            turn(pm[:, 0, 80:80 + VB_ROWS], vb_rows[:, :], VB_ROWS)
            turn(pm[:, 0, 128:224], ba_rows[:, 0, :], 96)
            turn(pm[:, 0, 224:320], ba_rows[:, 1, :], 96).then_inc(tr_ready, 1)
            pe.wait_ge(c_silu, 1)
            for k in range(KT):
                last = turn(pm[:, 1, k * NC:(k + 1) * NC], cs_rows[:, k * P:(k + 1) * P], NC)
            last.then_inc(tr_ready, 1)
            pe.wait_ge(rows_in, 64)
            for k in range(KT):
                b = (2 + k) % 4
                if k >= 2:
                    pe.wait_ge(tr_taken, k - 1)
                for c in range(NCH):
                    turn(pm[:, b, c * P:(c + 1) * P], x_rows[:, c, k * P:(k + 1) * P], P)
                turn(pm[:, b, TP:T], xs_rows[:, k * P:(k + 1) * P], NS).then_inc(tr_ready, 1)
            pe.wait_ge(tr_taken, START_BANKS)
            for i in range(KT // 2):
                pe.wait_ge(sq_ready, i + 1)
                for m in range(MT):
                    last = nc.tensor.matmul(pm[:, 0, 0:T], ones[:, :], sq[:, i % 2, m, :], start=(i + m == 0),
                                            stop=(i + m == KT // 2), skip_group_check=True)
                last.then_inc(ss_done, 1)
            kind, count, g0, n0, a0 = PLAN["ada0a"]
            ada_static("ada0a", 0)
            with pe.Fori(0, count // 2 - 1) as j:
                ada_pair(2 * j + 2, 2 * j + 2)

            def h_wait(n):
                return lambda u: pe.wait_ge(h_ready, KT * n + UK * (u + 1))

            gemm(16, PLAN["in0"][3], PLAN["in0"][2], h_hi, h_lo, h_wait(0))
            pe.wait_ge(aw_lo, 1)
            pe.wait_ge(rstd_ready, 1)
            for k in range(KT):
                cols = slice(16 * k, 16 * k + P)
                nc.tensor.matmul(pm[:, 0, 0:T], a_hi[:, cols], h_hi[:, k, :], start=(k == 0), stop=False)
                nc.tensor.matmul(pm[:, 0, 0:T], a_hi[:, cols], h_lo[:, k, :], start=False, stop=False)
                last = nc.tensor.matmul(pm[:, 0, 0:T], a_lo[:, cols], h_hi[:, k, :], start=False, stop=(k == KT - 1))
            last.then_inc(alr_psum, 1)
            pe.wait_ge(alr_ready, 1)
            for h in range(HG):
                last = nc.tensor.matmul(pm[:, h, 0:T], gate_up[:, h * DK:(h + 1) * DK], a_lr[:, :], start=True, stop=True)
            last.then_inc(gate_psum, 1)
            pe.wait_ge(evacuated, PLAN["in0"][2] + 16)
            pe.wait_ge(gz_ready, 1)
            for j in range(8):
                last = turn(pm[0:POOL_TAIL, 2 + j // 4, (j % 4) * P:(j % 4 + 1) * P],
                            z[:, 24 + j, T - POOL_TAIL:T], P)
            last.then_inc(tail_psum, 1)
            pe.wait_ge(past_in, 16)
            for j in range(8):
                last = turn(pm[:, j // 4, (j % 4) * 120:(j % 4 + 1) * 120], pastu[:, j * P:(j + 1) * P], 120)
            last.then_inc(past_psum, 1)
            pe.wait_ge(tail_ready, 1)
            pe.wait_ge(past_taken, 1)

            def recurrence(q, ada_name, ada_first, sample_slots, level_slots):
                hd = HEADS[q]
                nv, dv, zq, zk, zv = hd["nv"], hd["dv"], hd["q"], hd["k"], hd["v"]
                vt = vT[hd["layer"]]
                fill = [ada_first]

                def filler(slots, s):
                    if s in slots:
                        ada_static(ada_name, fill[0])
                        fill[0] += 1

                for c in range(NCH):
                    for j in range(nv):
                        b = c * (nv // 4) + j // 4
                        last = turn(pm[:, b, (j % 4) * P:(j % 4 + 1) * P], z[:, zv + j, c * CH:(c + 1) * CH], P)
                    last.then_inc(vtr_psum, 1)
                pe.wait_ge(vtr_ready, 4 * q + 2)
                for j in range(nv):
                    last = turn(pm[0:NS, j // 4, (j % 4) * P:(j % 4 + 1) * P], z[:, zv + j, TP:T], P)
                last.then_inc(vtr_psum, 1)
                if q:
                    pe.wait_ge(k_ready, q)
                for h in range(HG):
                    last = turn(pm[0:NS, 2, h * P:(h + 1) * P], z[:, zk + h, TP:T], P)
                last.then_inc(vtr_psum, 1)
                pe.wait_ge(vtr_ready, 4 * q + 4)
                pe.wait_ge(q_scaled, 1)
                for b in range(NS):
                    pe.wait_ge(kmask_ready, NS * q + b + 1)
                    if NS * q + b:
                        pe.wait_ge(st_ready, NS * q + b)
                    for h in range(HG):
                        o = h * dv
                        last = nc.tensor.matmul(pm[:, o // 512, o % 512:o % 512 + dv], kmask[:, b % 2, h * DK:(h + 1) * DK],
                                                v8[:, o:o + dv], start=True, stop=True)
                    last.then_inc(kv_psum, 1)
                    filler(sample_slots, b)
                    pe.wait_ge(st_ready, NS * q + b + 1)
                    for j in range(nv):
                        last = nc.tensor.matmul(pm[:, 3, j * NS + b:j * NS + b + 1], st[:, b % 2, j * P:(j + 1) * P],
                                                z[:, zq + j * P // dv, TP + b:TP + b + 1], start=True, stop=True)
                    last.then_inc(o8_psum, 1)
                for i in range(SETS):
                    if i == 0:
                        lhs = [[z[:, zk + h, c * CH:(c + 1) * CH] for h in range(HG)] for c in range(NCH)]
                        rhs = [[z[:, zq + h, c * CH:(c + 1) * CH] for h in range(HG)] for c in range(NCH)]
                    else:
                        pe.wait_ge(fac_ready, (LEVELS + 2) * q + i)
                        lhs = rhs = [[fac[:, (i - 1) % 2, h, c * CH:(c + 1) * CH] for h in range(HG)] for c in range(NCH)]
                        if i == 1:
                            pe.wait_ge(o8_taken, q + 1)
                        else:
                            pe.wait_ge(sc_taken, SETS * q + i - 1)
                    for c in range(NCH):
                        for h in range(HG):
                            last = nc.tensor.matmul(pm[:, 2 * (i % 2) + c, h * CH:(h + 1) * CH], lhs[c][h], rhs[c][h],
                                                    start=True, stop=True)
                    last.then_inc(sc_psum, 1)
                    filler(level_slots, i)
                pe.wait_ge(fac_ready, (LEVELS + 2) * q + LEVELS + 1)
                pe.wait_ge(sc_taken, SETS * q + SETS - 1)
                for c in range(NCH):
                    for h in range(HG):
                        last = turn(pm[:, c, h * P:(h + 1) * P], fac[:, 1, h, c * CH:(c + 1) * CH], P)
                last.then_inc(kd_psum, 1)
                pe.wait_ge(kd_ready, q + 1)
                pe.wait_ge(sc_taken, SETS * (q + 1))
                for h in range(HG):
                    o = h * dv
                    last = nc.tensor.matmul(pm[:, 2 + o // 512, o % 512:o % 512 + dv], kdT[:, 0, h * DK:(h + 1) * DK],
                                            vt[:, 0, o:o + dv], start=True, stop=True)
                last.then_inc(s1_psum, 1)
                for h in range(HG):
                    o = h * dv
                    last = nc.tensor.matmul(pm[:, o // 512, o % 512:o % 512 + dv], kdT[:, 1, h * DK:(h + 1) * DK],
                                            vt[:, 1, o:o + dv], start=True, stop=True)
                last.then_inc(kv1_psum, 1)
                pe.wait_ge(s1_ready, q + 1)
                pe.wait_ge(fac_ready, (LEVELS + 2) * (q + 1))
                for jj in range(nv // 2):
                    b0 = 2 if jj % 2 == 0 else 0
                    if jj == 1:
                        pe.wait_ge(s2_ready, q + 1)
                    if jj >= 2:
                        pe.wait_ge(o_ready, OPAIRS[q] + jj - 1)
                    for m in range(2):
                        j = 2 * jj + m
                        h = j * P // dv
                        nc.tensor.matmul(pm[:, b0 + m, 0:CH], vt[:, 0, j * P:(j + 1) * P], scores[:, 0, h, :], start=True, stop=True)
                        nc.tensor.matmul(pm[:, b0 + m, CH:TP], vt[:, 1, j * P:(j + 1) * P], scores[:, 1, h, :], start=True, stop=False)
                        last = nc.tensor.matmul(pm[:, b0 + m, CH:TP], s1[:, j * P:(j + 1) * P], fac[:, 0, h, 0:CH], start=False, stop=True)
                    last.then_inc(o_psum, 1)

            recurrence(0, "ada0b", 0, range(8), range(8))
            pe.wait_ge(past_taken, 1)
            pe.wait_ge(o_ready, OPAIRS[1])
            for g in range(4):
                pe.wait_ge(pool_d, g + 1)
                if g >= 2:
                    pe.wait_ge(pool_taken, g - 1)
                for e in range(2):
                    for c in range(2):
                        last = nc.tensor.matmul(pm[:, 2 * (g % 2) + e, 0:T], pool_w[:, g, c, e * P:(e + 1) * P],
                                                z[:, 32 + 2 * g + c, :], start=(c == 0), stop=(c == 1))
                last.then_inc(pool_psum, 1)
            pe.wait_ge(pool_taken, 4)
            pe.wait_ge(osq_ready, 1)
            for h in range(HG):
                for m in range(2):
                    last = nc.tensor.matmul(pm[:, h, 0:T], ones[:, :], z[:, 2 * h + m, :], start=(m == 0), stop=(m == 1))
            last.then_inc(oss_psum, 1)

            def mix_wait(n):
                return lambda u: pe.wait_ge(mix_ready, 4 * n + (3 if u == 0 else 4))

            gemm(8, PLAN["out0"][3], PLAN["out0"][2], h_hi, h_lo, mix_wait(0), norm=8)

            def mlp(l, f, n, g, a, hw, hc, norm=None):
                s = 20 if l == 0 else 16
                if l == 0:
                    ada_pair(a, g)
                up_g = g + 2 if l == 0 else g
                gemm(8, n, up_g, h_hi, h_lo, hw)
                if l == 0:
                    ada_pair(a + 2, g + 10)
                down_g = g + 12 if l == 0 else g + 8
                gemm(8, n + 8, down_g, f_hi, f_lo, lambda u: pe.wait_ge(hid_ready, 8 * hc + 2 * (u + 1)), norm=norm)

            def mlp_layer(l, hw, norm):
                first = PLAN["ada1u0" if l == 0 else "up1_0"]
                g0, n0, a0 = first[2], first[3], first[4]
                s = 20 if l == 0 else 16
                with pe.Fori(0, FF_CHUNKS - 1) as f:
                    mlp(l, f, n0 + 16 * f, g0 + s * f, a0 + 4 * f, hw, FF_CHUNKS * l + f)
                f = FF_CHUNKS - 1
                mlp(l, f, n0 + 16 * f, g0 + s * f, a0 + 4 * f, hw, FF_CHUNKS * l + f, norm=norm)

            mlp_layer(0, h_wait(1), 16)
            pe.wait_ge(rstd_ready, 3)
            pe.wait_ge(aw_in, 64)
            for j in range(8):
                last = turn(pm[:, 0, j * TAPS:(j + 1) * TAPS], cw_rows[:, j * P:(j + 1) * P], TAPS)
            last.then_inc(cw_psum, 1)
            gemm(8, PLAN["glu"][3], PLAN["glu"][2], h_hi, h_lo, h_wait(2))
            gemm(16, PLAN["in1"][3], PLAN["in1"][2], h_hi, h_lo, h_wait(2))
            pe.wait_ge(conv_step, 1)
            for j in range(8):
                last = turn(pm[0:CONV_TAIL, 2 + j // 4, (j % 4) * P:(j % 4 + 1) * P],
                            z[:, 32 + j, T - CONV_TAIL:T], P)
            last.then_inc(tail_psum, 1)
            pe.wait_ge(past_in, 32)
            for j in range(8):
                if j >= 2:
                    pe.wait_ge(past_taken, j)
                for a in range(2):
                    last = turn(pm[:, j % 2, a * 120:(a + 1) * 120], pastc[:, a, j * P:(j + 1) * P], 120)
                last.then_inc(past_psum, 1)
            pe.wait_ge(cv_done, 8)
            for j in range(8):
                last = nc.tensor.matmul(pm[:, 0, 0:T], ones[:, :], z[:, 40 + j, :], start=(j == 0), stop=(j == 7))
            last.then_inc(ln_psum, 1)
            pe.wait_ge(ln_sq, 1)
            for j in range(8):
                last = nc.tensor.matmul(pm[:, 1, 0:T], ones[:, :], z[:, 32 + j, :], start=(j == 0), stop=(j == 7))
            last.then_inc(ln_psum, 1)
            pe.wait_ge(ln_rstd, 1)
            pe.wait_ge(tail_ready, 2)
            recurrence(1, "ada1b", 0, range(0, 8, 2), range(0, 8, 2))
            pe.wait_ge(o_ready, OPAIRS[2])
            recurrence(2, "ada1b", 8, range(0, 8, 2), range(0, 8, 2))
            pe.wait_ge(o_ready, OPAIRS[3])
            pe.wait_ge(osq_ready, 2)
            for r in range(2):
                if r:
                    pe.wait_ge(ors_ready, 2)
                for h in range(4):
                    last = nc.tensor.matmul(pm[:, h, 0:T], ones[:, :], z[:, 4 * r + h, :], start=True, stop=True)
                last.then_inc(oss_psum, 1)
            gemm(8, PLAN["out1"][3], PLAN["out1"][2], h_hi, h_lo, mix_wait(1), norm=24)
            mlp_layer(1, h_wait(3), 32)
            for r in range(3):
                for b in range(4):
                    i = 4 * r + b
                    if r == 0:
                        pe.wait_ge(y_ready, 4 * b + 4)
                    if i >= 4:
                        pe.wait_ge(y_taken, i - 3)
                    for m in range(4):
                        k = 4 * b + m
                        if r < 2:
                            last = turn(pm[:, b, m * P:(m + 1) * P], x[:, k, r * P:(r + 1) * P], P)
                        else:
                            last = turn(pm[0:NS, b, m * P:(m + 1) * P], x[:, k, TP:T], P)
                    last.then_inc(y_psum, 1)

        @block.scalar
        def _(act):
            steps = Count()

            def step(ins):
                ins.then_inc(act_step, 1)
                act.wait_ge(act_step, steps.next())

            def hi(n, u, p, g):
                if u % 2 == 0:
                    act.wait_ge(raw_in[p][u // 2], 8 * (g - p) + 16)
                if not isinstance(n, int) or NU * n + u >= NU:
                    act.wait_ge(split_used, NU * n + u - (NU - 1))
                nc.scalar.activation(w_hi[:, u, :], raw[:, p, u, :], ACT.Copy).then_inc(hi_ready, 1)

            def hi_phase(count, n, g, after=None, last_next=None):
                def body(i, p, nxt):
                    hi(n + i, 2, p, g + i)
                    hi(n + i, 3, p, g + i)
                    if nxt is not None:
                        hi(nxt[0], 0, 1 - p, nxt[1])
                        hi(nxt[0], 1, 1 - p, nxt[1])
                    if after:
                        after(i, p)

                peel = 1 if isinstance(n, int) and n == 0 else 0
                for i in range(2 * peel):
                    body(i, i % 2, (n + i + 1, g + i + 1))
                with act.Fori(0, count // 2 - 1 - peel) as j:
                    for p in range(2):
                        i = 2 * j + (2 * peel + p)
                        body(i, p, (n + i + 1, g + i + 1))
                i = count - 2
                body(i, 0, (n + i + 1, g + i + 1))
                body(i + 1, 1, last_next)

            def square(norm, x0):
                def f(i, p):
                    act.wait_ge(x_ready, x0 + i + 1)
                    act.wait_ge(ss_done, norm + i - 1)
                    k = 2 * i
                    nc.scalar.activation(sq[:, p, :, :], x[:, bass.ds(k, 2), :], ACT.Square).then_inc(sq_ready, 1)
                return f

            def rms(r, sums, tail_only=False):
                act.wait_ge(ss_done, sums)
                step(nc.scalar.activation(lnv[:, :], pm[:, 0, 0:T], ACT.Ln, bias=eps_t[:, :], scale=1.0 / D))
                nc.scalar.activation(rstd[:, :], lnv[:, :], ACT.Exp, scale=-0.5).then_inc(rstd_ready, 1)

            def modulate(r, l, sh):
                act.wait_ge(t8_ready, r + 1)
                nc.scalar.activation(h_hi[:, :, TP:T], t8[:, :, :], ACT.Copy).then_inc(h8_hi, 1)
                for k in range(KT):
                    act.wait_ge(hs_ready, KT * r + k + 1)
                    nc.scalar.activation(h_hi[:, k, 0:TP], hs[:, k % 4, :], ACT.Identity,
                                         bias=mod[:, l, sh + k, 0:1]).then_inc(hh_ready, 1)

            act.dma_start(ident[:, :], io["ident"]).then_inc(const_in, 16)
            for name, row in VA.items():
                src = io[name]
                n = 16 if name == "norm_final" else 32
                src = src.rearrange("(k p) -> k p", p=P) if name == "norm_final" else src.rearrange("l (k p) -> (l k) p", p=P)
                act.dma_start(va_rows[row:row + n, :], src).then_inc(const_in, 16)
            for name, row in VB.items():
                src = io[name].rearrange("l (k p) -> (l k) p", p=P)
                act.dma_start(vb_rows[row:row + src.shape[0], :], src).then_inc(const_in, 16)
            act.dma_start(ba_rows[:, :, :], io["b_ada"].rearrange("l (m p) -> m l p", p=P)).then_inc(const_in, 16)
            act.dma_start(masks[:, :, :], io["masks"].rearrange("p (l t) -> p l t", l=LEVELS)).then_inc(const_in, 16)
            act.dma_start(inv_count[:, :, :], io["inv_count"].rearrange("p (g t) -> p g t", t=16)).then_inc(const_in, 16)

            act.wait_ge(rows_in, 64)
            nc.scalar.activation(cs_rows[:, :], c_rows[:, :], ACT.Silu).then_inc(c_silu, 1)
            act.preload_act_table_set("natural_log_exp_and_others")
            for i in range(KT // 2):
                act.wait_ge(tr_taken, 2 + 2 * i + 2)
                if i >= 2:
                    act.wait_ge(ss_done, i - 1)
                nc.scalar.activation(sq[:, i % 2, :, :], x[:, 2 * i:2 * i + 2, :], ACT.Square).then_inc(sq_ready, 1)
            rms(0, 8)
            act.wait_ge(filled, 2)
            nc.scalar.activation(sm[:, :], lb[:, :], ACT.Exp).then_inc(lb_exp, 1)
            _, _, g0, n0, _ = PLAN["in0"]
            hi(n0, 0, 0, g0)
            hi(n0, 1, 0, g0)
            modulate(0, 0, SH1)
            hi_phase(16, n0, g0)
            act.wait_ge(aw_in, 48)
            act.wait_ge(filled, 3)
            nc.scalar.activation(a_hi[:, 0:KT * 16], a_w[:, :, :].rearrange("p k n -> p (k n)"), ACT.Copy).then_inc(aw_hi, 1)
            act.wait_ge(gz_ready, 2)
            step(nc.scalar.activation(gl[:, :, :], gl[:, :, :], ACT.Exp))
            nc.scalar.activation(gl[:, :, :], gl[:, :, :], ACT.Ln, bias=1.0).then_inc(gl_ready, 1)
            act.wait_ge(evacuated, g0 + 16)
            nc.scalar.activation(z[:, 0:4, :], z[:, 0:4, :], ACT.Copy, scale=float(DK) ** -0.5).then_inc(q_scaled, 1)
            act.wait_ge(tail_psum, 1)
            nc.scalar.activation(tail[0:POOL_TAIL, :].rearrange("p (a n) -> p a n", a=2), pm[0:POOL_TAIL, 2:4, :],
                                 ACT.Copy).then_inc(tail_ready, 1)

            def recurrence(q):
                hd = HEADS[q]
                nv, dv, zq, zk, zv = hd["nv"], hd["dv"], hd["q"], hd["k"], hd["v"]
                vt = vT[hd["layer"]]
                nb = nv // 4
                act.wait_ge(logp_ready, q + 1)
                nc.scalar.activation(decay8[:, :, :], logp[:, :, TP:T], ACT.Exp).then_inc(dec8_ready, 1)
                for c in range(NCH):
                    act.wait_ge(vtr_psum, 4 * q + c + 1)
                    nc.scalar.activation(vt[:, c, 0:nv * P].rearrange("p (a n) -> p a n", n=512),
                                         pm[:, c * nb:(c + 1) * nb, :], ACT.Copy).then_inc(vtr_ready, 1)
                act.wait_ge(vtr_psum, 4 * q + 3)
                nc.scalar.activation(v8[:, 0:nv * P].rearrange("p (a n) -> p a n", n=512), pm[0:NS, 0:nb, :],
                                     ACT.Copy).then_inc(vtr_ready, 1)
                act.wait_ge(vtr_psum, 4 * q + 4)
                nc.scalar.activation(k8[:, :], pm[0:NS, 2, :], ACT.Copy).then_inc(vtr_ready, 1)
                act.wait_ge(vtr_ready, 4 * q + 4)
                for b in range(NS):
                    if b >= 2:
                        act.wait_ge(kv_psum, NS * q + b - 1)
                    nc.scalar.activation(kmask[:, b % 2, :], k8[:, :], ACT.Copy,
                                         scale=ident[0:NS, b:b + 1]).then_inc(kmask_ready, 1)
                for lv in range(LEVELS):
                    w = 1 << lv
                    act.wait_ge(dif_ready, (LEVELS + 1) * q + lv + 1)
                    dl, dr = halves(dec[:, lv % 2, :, :], w)
                    _, pr = halves(logp[:, :, 0:TP], w)
                    nc.scalar.activation(dr, pr, ACT.Exp)
                    nc.scalar.activation(dl, dl, ACT.Exp).then_inc(exp_ready, 1)
                act.wait_ge(dif_ready, (LEVELS + 1) * (q + 1))
                nc.scalar.activation(dec[:, 1, :, :], dec[:, 1, :, :], ACT.Exp).then_inc(exp_ready, 1)
                act.wait_ge(fac_ready, (LEVELS + 2) * q + LEVELS)
                nc.scalar.activation(dec[:, 0, :, 0:CH], logp[:, :, CH:TP], ACT.Exp).then_inc(exp_ready, 1)
                act.wait_ge(kd_psum, q + 1)
                nc.scalar.activation(kdT[:, :, :], pm[:, 0:2, :], ACT.Copy).then_inc(kd_ready, 1)
                act.wait_ge(s1_psum, q + 1)
                nc.scalar.activation(s1[:, 0:nv * P].rearrange("p (a n) -> p a n", n=512), pm[:, 2:2 + nb, :],
                                     ACT.Copy).then_inc(s1_ready, 1)
                for jj in range(nv // 2):
                    b0 = 2 if jj % 2 == 0 else 0
                    act.wait_ge(o_psum, OPAIRS[q] + jj + 1)
                    nc.scalar.activation(z[:, zv + 2 * jj:zv + 2 * jj + 2, 0:TP], pm[:, b0:b0 + 2, 0:TP],
                                         ACT.Copy).then_inc(o_ready, 1)

            def mix_high(n, batches):
                for i, (dst, src) in enumerate(batches):
                    if i >= 2:
                        act.wait_ge(mix_f32, n + i - 1)
                    nc.scalar.activation(h_hi[:, dst:dst + 4, :], z[:, src:src + 4, :], ACT.Copy).then_inc(mix_hi, 1)

            recurrence(0)
            for g in range(4):
                act.wait_ge(pool_psum, g + 1)
                for e in range(2):
                    j = 2 * g + e
                    last = nc.scalar.activation(z[:, 40 + j, :], pm[:, 2 * (g % 2) + e, 0:T], ACT.Copy,
                                                scale=vb[:, VB["ev_pool_scale"] + j:VB["ev_pool_scale"] + j + 1])
                last.then_inc(pool_taken, 1)
            act.wait_ge(o_ready, OPAIRS[1])
            act.wait_ge(o8_taken, 1)
            nc.scalar.activation(z[:, 0:8, :], z[:, 8:16, :], ACT.Square).then_inc(osq_ready, 1)
            act.wait_ge(oss_psum, 1)
            act.wait_ge(o_ready, OPAIRS[1])
            step(nc.scalar.activation(logp[:, :, :], pm[:, :, 0:T], ACT.Ln, bias=eps_t[:, :], scale=1.0 / 256))
            nc.scalar.activation(logp[:, :, :], logp[:, :, :], ACT.Exp, scale=-0.5).then_inc(ors_ready, 1)
            nc.scalar.activation(z[:, 16:24, :], z[:, 16:24, :], ACT.Silu).then_inc(silu_ready, 1)
            act.preload_act_table_set("natural_log_exp_and_others")
            act.wait_ge(pool_taken, 4)
            act.wait_ge(s2_ready, 1)
            act.wait_ge(small_out, 16 * 5)
            mix_high(0, [(8, 40), (12, 44), (0, 8), (4, 12)])
            _, _, g1, n1, _ = PLAN["out0"]
            hi(n1, 0, 0, g1)
            hi(n1, 1, 0, g1)
            hi_phase(8, n1, g1, after=square(8, 0), last_next=None)
            rms(1, 16)
            modulate(1, 0, SH2)

            def mlp_layer(l, norm, x0):
                first = PLAN["ada1u0" if l == 0 else "up1_0"]
                g0, n0 = first[2], first[3]
                s = 20 if l == 0 else 16
                gu = 2 if l == 0 else 0
                gd = 12 if l == 0 else 8
                hi(n0, 0, 0, g0 + gu)
                hi(n0, 1, 0, g0 + gu)
                with act.Fori(0, FF_CHUNKS - 1) as f:
                    n, g = n0 + 16 * f, g0 + s * f
                    hi_phase(8, n, g + gu, last_next=(n + 8, g + gd))
                    hi_phase(8, n + 8, g + gd, last_next=(n + 16, g + s + gu))
                f = FF_CHUNKS - 1
                n, g = n0 + 16 * f, g0 + s * f
                hi_phase(8, n, g + gu, last_next=(n + 8, g + gd))
                hi_phase(8, n + 8, g + gd, after=square(norm, x0), last_next=None)

            mlp_layer(0, 16, 32)
            rms(2, 24)
            _, _, g2, n2, _ = PLAN["glu"]
            hi(n2, 0, 0, g2)
            hi(n2, 1, 0, g2)
            modulate(2, 1, SH1)
            hi_phase(8, n2, g2, last_next=(n2 + 8, g2 + 8))
            act.wait_ge(evacuated, g2 + 8)
            nc.scalar.activation(z[:, 40:48, :], z[:, 40:48, :], ACT.Sigmoid).then_inc(gb_sig, 1)
            act.preload_act_table_set("natural_log_exp_and_others")
            _, _, g3, n3, _ = PLAN["in1"]
            hi_phase(16, n3, g3)
            act.wait_ge(tail_psum, 2)
            nc.scalar.activation(tail[0:CONV_TAIL, :].rearrange("p (a n) -> p a n", a=2), pm[0:CONV_TAIL, 2:4, :],
                                 ACT.Copy).then_inc(tail_ready, 1)
            act.wait_ge(ln_psum, 1)
            nc.scalar.activation(mean[:, :], pm[:, 0, 0:T], ACT.Copy, scale=1.0 / 1024).then_inc(ln_mean, 1)
            act.wait_ge(ln_cent, 1)
            act.wait_ge(tail_psum, 2)
            nc.scalar.activation(z[:, 32:40, :], z[:, 40:48, :], ACT.Square).then_inc(ln_sq, 1)
            act.wait_ge(ln_psum, 2)
            step(nc.scalar.activation(lnv[:, :], pm[:, 1, 0:T], ACT.Ln, bias=eps_t[:, :], scale=1.0 / 1024))
            nc.scalar.activation(rstd[:, :], lnv[:, :], ACT.Exp, scale=-0.5).then_inc(ln_rstd, 1)
            act.wait_ge(ln_done, 1)
            nc.scalar.activation(z[:, 40:48, :], z[:, 40:48, :], ACT.Silu).then_inc(cv_ready, 1)
            act.wait_ge(evacuated, g3 + 16)
            nc.scalar.activation(z[:, 24:32, :], z[:, 24:32, :], ACT.Silu).then_inc(silu_ready, 1)
            for q in (1, 2):
                zk = HEADS[q]["k"]
                if q == 2:
                    act.wait_ge(dec8_ready, 2)
                    act.wait_ge(exp_ready, (LEVELS + 2) * 2)
                    act.wait_ge(s2_ready, 2)
                nc.scalar.activation(logp[:, :, :], z[:, zk:zk + 4, :], ACT.Sigmoid)
                nc.scalar.activation(z[:, zk:zk + 4, :], z[:, zk:zk + 4, :], ACT.Sigmoid, scale=-1.0).then_inc(sig_ready, 1)
                act.preload_act_table_set("natural_log_exp_and_others")
                act.wait_ge(ln_in, q)
                nc.scalar.activation(gz[:, :, :], gz[:, :, :], ACT.Ln)
                nc.scalar.activation(logp[:, :, :], logp[:, :, :], ACT.Ln).then_inc(ln_out, 1)
                recurrence(q)
            act.wait_ge(o_ready, OPAIRS[3])
            act.wait_ge(o8_taken, 3)
            nc.scalar.activation(z[:, 0:8, :], z[:, 16:24, :], ACT.Square).then_inc(osq_ready, 1)
            for r in range(2):
                act.wait_ge(oss_psum, 2 + r)
                rs = z[:, 8 + 4 * r:12 + 4 * r, :]
                step(nc.scalar.activation(rs, pm[:, :, 0:T], ACT.Ln, bias=eps_t[:, :], scale=1.0 / 128))
                nc.scalar.activation(rs, rs, ACT.Exp, scale=-0.5).then_inc(ors_ready, 1)
            act.wait_ge(cv_ready, 1)
            act.wait_ge(s2_ready, 3)
            act.wait_ge(small_out, 16 * SMALL_OUTS)
            mix_high(2, [(8, 40), (12, 44), (0, 16), (4, 20)])
            _, _, g4, n4, _ = PLAN["out1"]
            hi(n4, 0, 0, g4)
            hi(n4, 1, 0, g4)
            hi_phase(8, n4, g4, after=square(24, 40), last_next=None)
            rms(3, 32)
            modulate(3, 1, SH2)
            mlp_layer(1, 32, 72)
            rms(4, 40)
            for r in range(3):
                for b in range(4):
                    act.wait_ge(y_psum, 4 * r + b + 1)
                    rows, dst = (P, y_rows[:, r, b * 512:(b + 1) * 512]) if r < 2 else (NS, ys_rows[:, b * 512:(b + 1) * 512])
                    nc.scalar.activation(dst, pm[0:rows, b, :], ACT.Copy).then_inc(y_taken, 1)

        @block.vector
        def _(dve):
            steps = Count()

            def step(ins):
                ins.then_inc(dve_step, 1)
                dve.wait_ge(dve_step, steps.next())

            def lo(n, u, p):
                dve.wait_ge(hi_ready, NU * n + (u + 1))
                nc.vector.tensor_tensor(w_lo[:, u, :], raw[:, p, u, :], w_hi[:, u, :].bitcast(F32),
                                        ALU.subtract).then_inc(lo_ready, 1)

            def lo_phase(count, n, evac, last_next=None, middle=None, loop_work=None):
                def body(i, p, nxt, wrk=None):
                    lo(n + i, 2, p)
                    if wrk:
                        wrk(0)
                    lo(n + i, 3, p)
                    if wrk:
                        wrk(1)
                    if nxt is not None:
                        lo(nxt, 0, 1 - p)
                        if wrk:
                            wrk(2)
                        lo(nxt, 1, 1 - p)
                        if wrk:
                            wrk(3)
                    evac(i, p)

                with dve.Fori(0, count // 2 - 1) as j:
                    for p in range(2):
                        i = 2 * j + p
                        body(i, p, n + i + 1, (lambda s, p=p: loop_work(j, 4 * p + s)) if loop_work else None)
                i = count - 2
                j = count // 2 - 1
                body(i, 0, n + i + 1, (lambda s: loop_work(j, s)) if loop_work else None)
                wrk = (lambda s: loop_work(j, 4 + s)) if loop_work else None
                if last_next is not None and middle is None:
                    body(i + 1, 1, last_next, wrk)
                else:
                    body(i + 1, 1, None, wrk)
                    if wrk:
                        wrk(2)
                        wrk(3)
                    if middle:
                        middle()
                    if last_next is not None:
                        lo(last_next, 0, 0)
                        lo(last_next, 1, 0)

            def ada_evac(l, a, g, m, p):
                dve.wait_ge(ada_used, 2 * a + 2)
                nc.vector.tensor_tensor(mod[:, l, bass.ds(m, 2), :], ps[:, MT * p:MT * p + MT, 0:NC],
                                        bada[:, l, bass.ds(m, 2)].unsqueeze(2).broadcast_to([P, 2, NC]),
                                        ALU.add).then_inc(evacuated, 1)

            def ada_static(name, j):
                kind, count, g0, n0, a0 = PLAN[name]
                l, m0 = (1 if name.startswith("ada1") else 0), (32 if name.endswith("b") else 0)
                for p in range(2):
                    i = 2 * j + p
                    ada_evac(l, a0 + i, g0 + i, m0 + 2 * i, p)

            def z_evac(n, z0):
                def f(i, p):
                    dve.wait_ge(split_used, NU * (n + i) + NU)
                    off = (z0 + 2 * i) * T
                    nc.vector.tensor_copy(zf[:, bass.ds(off, MT * T)].rearrange("p (a t) -> p a t", a=MT),
                                          bank2(p)).then_inc(evacuated, 1)
                return f

            def up_evac(n, g, h):
                def f(i, p):
                    dve.wait_ge(split_used, NU * (n + i) + NU)
                    nc.vector.tensor_scalar(hid[:, :, :], bank2(p), 0.0, None, ALU.max).then_inc(evacuated, 1)
                    dve.wait_ge(evacuated, g + i + 1)
                    nc.vector.tensor_tensor(hid[:, :, :], hid[:, :, :], hid[:, :, :], ALU.mult).then_inc(hid_sq, 1)
                    dve.wait_ge(hid_sq, h + i + 1)
                    k = 2 * i
                    nc.vector.tensor_copy(f_hi[:, bass.ds(k, 2), :], hid[:, :, :]).then_inc(hid_hi, 1)
                    dve.wait_ge(hid_hi, h + i + 1)
                    nc.vector.tensor_tensor(f_lo[:, bass.ds(k, 2), :], hid[:, :, :],
                                            f_hi[:, bass.ds(k, 2), :].bitcast(F32), ALU.subtract).then_inc(hid_ready, 1)
                return f

            def res_evac(n, r, l, gate):
                def f(i, p):
                    dve.wait_ge(split_used, NU * (n + i) + NU)
                    k = 2 * i
                    nc.vector.tensor_tensor(g8[:, :, :], bank2(p)[:, :, TP:T], mod[:, l, bass.ds(gate + k, 2), 1:NC],
                                            ALU.mult).then_inc(gate8_done, 1)
                    for m in range(MT):
                        xa = x[:, bass.ds(k + m, 1), 0:TP].rearrange("p a t -> p (a t)")
                        ga = mod[:, l, bass.ds(gate + k + m, 1), 0:1].rearrange("p a t -> p (a t)")
                        last = nc.vector.scalar_tensor_tensor(xa, ps[:, MT * p + m, 0:TP], ga, xa, ALU.mult, ALU.add)
                    last.then_inc(evacuated, 1)
                    dve.wait_ge(gate8_done, r + i + 1)
                    x8 = x[:, bass.ds(k, 2), TP:T]
                    nc.vector.tensor_tensor(x8, x8, g8[:, :, :], ALU.add).then_inc(x_ready, 1)
                return f

            def gains(l, norm0, sc):
                step(nc.vector.scalar_tensor_tensor(
                    amod[:, :, :], mod[:, l, sc:sc + KT, :], 1.0,
                    va[:, norm0:norm0 + KT].unsqueeze(2).broadcast_to([P, KT, NC]), ALU.add, ALU.mult))

            def modulate(r, l, sh):
                dve.wait_ge(rstd_ready, r + 1)
                step(nc.vector.tensor_tensor(t8[:, :, :], x[:, :, TP:T], amod[:, :, 1:NC], ALU.mult))
                step(nc.vector.tensor_tensor(t8[:, :, :], t8[:, :, :],
                                             rstd[:, TP:T].unsqueeze(1).broadcast_to([P, KT, NS]), ALU.mult))
                nc.vector.tensor_tensor(t8[:, :, :], t8[:, :, :], mod[:, l, sh:sh + KT, 1:NC], ALU.add).then_inc(t8_ready, 1)

                def scale(k):
                    nc.vector.scalar_tensor_tensor(hs[:, k % 4, :], x[:, k, 0:TP], amod[:, k, 0:1], rstd[:, 0:TP],
                                                   ALU.mult, ALU.mult).then_inc(hs_ready, 1)

                def low(k):
                    dve.wait_ge(hh_ready, KT * r + k + 1)
                    nc.vector.scalar_tensor_tensor(h_lo[:, k, 0:TP], hs[:, k % 4, :], mod[:, l, sh + k, 0:1],
                                                   h_hi[:, k, 0:TP].bitcast(F32), ALU.add, ALU.subtract).then_inc(h_ready, 1)

                for k in range(3):
                    scale(k)
                dve.wait_ge(h8_hi, r + 1)
                nc.vector.tensor_tensor(h_lo[:, :, TP:T], t8[:, :, :], h_hi[:, :, TP:T].bitcast(F32), ALU.subtract)
                for k in range(KT):
                    low(k)
                    if k + 3 < KT:
                        if k:
                            dve.wait_ge(h_ready, KT * r + k)
                        scale(k + 3)

            nc.vector.memset(ones[:, :], 1.0)
            nc.vector.memset(zeros[:, :], 0.0)
            nc.vector.memset(eps_t[:, :], EPS).then_inc(filled, 1)
            dve.wait_ge(tr_ready, 1)
            nc.vector.tensor_copy(va[:, :], pm[:, 0, 0:80])
            nc.vector.tensor_copy(vb[:, :], pm[:, 0, 80:80 + VB_ROWS])
            nc.vector.tensor_copy(bada[:, :, :], pm[:, 0, 128:320].rearrange("p (l m) -> p l m", l=2)).then_inc(tr_taken, 1)
            dve.wait_ge(tr_ready, 2)
            nc.vector.tensor_copy(cT[:, :, :], pm[:, 1, 0:KT * NC].rearrange("p (k n) -> p k n", n=NC)).then_inc(tr_taken, 1)
            for k in range(KT):
                dve.wait_ge(tr_ready, 3 + k)
                nc.vector.tensor_copy(x[:, k, :], pm[:, (2 + k) % 4, 0:T]).then_inc(tr_taken, 1)
            dve.wait_ge(tr_taken, START_BANKS)
            raw_lb = vb[:, VB["od_lb_raw"]:VB["od_lb_raw"] + 8]
            nc.vector.tensor_tensor(lb[:, :], raw_lb, raw_lb, ALU.subtract).then_inc(filled, 1)
            dve.wait_ge(lb_exp, 1)
            step(nc.vector.reciprocal(oml[:, :], sm[:, :]))
            step(nc.vector.tensor_tensor(sm[:, :], sm[:, :], oml[:, :], ALU.mult))
            step(nc.vector.tensor_tensor(lb[:, :], sm[:, :], sm[:, :], ALU.subtract))
            step(nc.vector.tensor_scalar(oml[:, :], lb[:, :], -1.0, 1.0, ALU.mult, ALU.add))
            dve.wait_ge(ss_done, 8)
            _, count, g0, n0, a0 = PLAN["ada0a"]
            with dve.Fori(0, count // 2) as j:
                for p in range(2):
                    ada_evac(0, 2 * j + p, 2 * j + p, 4 * j + 2 * p, p)
            dve.wait_ge(evacuated, g0 + count)
            gains(0, VA["norm_mix"], SC1)
            n0 = PLAN["in0"][3]
            lo(n0, 0, 0)
            lo(n0, 1, 0)
            modulate(0, 0, SH1)
            lo_phase(16, n0, z_evac(n0, 0))
            nc.vector.memset(a_hi[:, KT * 16:AW].bitcast(F32), 0.0)
            nc.vector.memset(a_lo[:, KT * 16:AW].bitcast(F32), 0.0).then_inc(filled, 1)
            dve.wait_ge(aw_hi, 1)
            nc.vector.tensor_tensor(a_lo[:, 0:KT * 16], a_w[:, :, :].rearrange("p k n -> p (k n)"),
                                    a_hi[:, 0:KT * 16].bitcast(F32), ALU.subtract).then_inc(aw_lo, 1)
            dve.wait_ge(alr_psum, 1)
            nc.vector.tensor_copy(a_lr[:, :], pm[0:16, 0, 0:T]).then_inc(alr_ready, 1)
            dve.wait_ge(gate_psum, 1)
            b0 = VB["ev_b_gate"]
            for h in range(HG):
                last = nc.vector.tensor_scalar(gz[:, h, :], pm[:, h, 0:T], vb[:, b0 + h:b0 + h + 1], None, ALU.add)
            last.then_inc(gz_ready, 1)
            dve.wait_ge(gz_ready, 1)
            gzf = gz[:, :, :].rearrange("p h t -> p (h t)")
            glf = gl[:, :, :].rearrange("p h t -> p (h t)")
            lpf = logp[:, :, :].rearrange("p h t -> p (h t)")
            nc.vector.scalar_tensor_tensor(glf, gzf, -1.0, gzf, ALU.mult, ALU.min).then_inc(gz_ready, 1)
            dve.wait_ge(gl_ready, 1)
            step(nc.vector.scalar_tensor_tensor(lpf, gzf, 0.0, glf, ALU.min, ALU.subtract))
            nc.vector.tensor_scalar(lpf, lpf, 1.0 / 16.0, None, ALU.mult).then_inc(logp_ready, 1)
            dve.wait_ge(past_psum, 1)
            dve.wait_ge(evacuated, PLAN["in0"][2] + 16)
            for g, w in enumerate(WINDOWS):
                b = g // 2
                c0 = (g % 2) * 240
                past = pm[:, b, c0:c0 + 240].rearrange("p (j b r) -> p j b r", j=2, r=POOL_PAST)
                u8 = z[:, 24 + 2 * g:26 + 2 * g, TP:T]
                d8 = z[:, 32 + 2 * g:34 + 2 * g, TP:T]
                step(nc.vector.tensor_reduce(wsum[:, :, :], past[:, :, :, POOL_PAST - w + 1:POOL_PAST], AX.X, ALU.add))
                step(nc.vector.tensor_tensor(wsum[:, :, :], wsum[:, :, :], u8, ALU.add))
                last = nc.vector.scalar_tensor_tensor(d8, wsum[:, :, :], 1.0 / w, u8, ALU.mult, ALU.subtract)
                if g < 3:
                    step(last)
            last.then_inc(past_taken, 1)

            def recurrence(q, ada_name, ada_first, sample_slots, level_slots):
                hd = HEADS[q]
                nv, dv, zq, zk, zv = hd["nv"], hd["dv"], hd["q"], hd["k"], hd["v"]
                fill = [ada_first]

                def filler(slots, s):
                    if s in slots:
                        ada_static(ada_name, fill[0])
                        fill[0] += 1

                dve.wait_ge(dec8_ready, q + 1)
                for b in range(NS):
                    dve.wait_ge(kv_psum, NS * q + b + 1)
                    dve.wait_ge(st_in[b % 2], 16 * (4 * q + b // 2 + 1))
                    for h in range(HG):
                        o = h * dv
                        s_ = st[:, b % 2, o:o + dv]
                        last = nc.vector.scalar_tensor_tensor(s_, s_, decay8[:, h, b:b + 1],
                                                              pm[:, o // 512, o % 512:o % 512 + dv], ALU.mult, ALU.add)
                    last.then_inc(st_ready, 1)
                    filler(sample_slots, b)
                dve.wait_ge(o8_psum, NS * (q + 1))
                nc.vector.tensor_copy(z[:, zv:zv + nv, TP:T], pm[:, 3, 0:nv * NS].rearrange("p (j b) -> p j b", b=NS)).then_inc(o8_taken, 1)
                for i in range(2):
                    dve.wait_ge(st_out[i], 16 * 4 * (q + 1))

                def differ(lv):
                    w = 1 << lv
                    left, _ = halves(logp[:, :, 0:TP], w)
                    dl, _ = halves(dec[:, lv % 2, :, :], w)
                    mid = left[:, :, :, w - 1:w].broadcast_to([P, HG, TP // (2 * w), w])
                    nc.vector.tensor_tensor(dl, mid, left, ALU.subtract).then_inc(dif_ready, 1)

                def take(i):
                    dve.wait_ge(sc_psum, SETS * q + i + 1)
                    if i:
                        dve.wait_ge(sc_taken, SETS * q + i)
                    for c in range(NCH):
                        prod = pm[:, 2 * (i % 2) + c, :].rearrange("p (h t) -> p h t", h=HG)
                        if i == 0:
                            last = nc.vector.tensor_tensor(scores[:, c, :, :], prod,
                                                           ident[:, :].unsqueeze(1).broadcast_to([P, HG, CH]), ALU.mult)
                        else:
                            last = nc.vector.copy_predicated(scores[:, c, :, :],
                                                             masks[:, i - 1, :].unsqueeze(1).broadcast_to([P, HG, CH]), prod)
                    last.then_inc(sc_taken, 1)

                differ(0)
                take(0)
                filler(level_slots, 0)
                for lv in range(LEVELS):
                    w = 1 << lv
                    dve.wait_ge(exp_ready, (LEVELS + 2) * q + lv + 1)
                    dl, dr = halves(dec[:, lv % 2, :, :], w)
                    fl, fr = halves(fac[:, lv % 2, :, :], w)
                    ql, qr = halves(z[:, zq:zq + HG, 0:TP], w)
                    kl, kr = halves(z[:, zk:zk + HG, 0:TP], w)
                    left, right = halves(logp[:, :, 0:TP], w)
                    nc.vector.tensor_tensor(fl, kl, dl, ALU.mult)
                    nc.vector.tensor_tensor(fr, qr, dr, ALU.mult).then_inc(fac_ready, 1)
                    mid = left[:, :, :, w - 1:w].broadcast_to([P, HG, TP // (2 * w), w])
                    nc.vector.tensor_tensor(right, right, mid, ALU.add).then_inc(prefix_ready, 1)
                    dve.wait_ge(prefix_ready, LEVELS * q + lv + 1)
                    if lv + 1 < LEVELS:
                        differ(lv + 1)
                    else:
                        lp = logp[:, :, 0:TP].rearrange("p h (c t) -> p h c t", c=NCH)
                        end = lp[:, :, :, CH - 1:CH].broadcast_to([P, HG, NCH, CH])
                        nc.vector.tensor_tensor(dec[:, 1, :, :].rearrange("p h (c t) -> p h c t", c=NCH), end, lp,
                                                ALU.subtract).then_inc(dif_ready, 1)
                    if lv:
                        take(lv)
                        filler(level_slots, lv)
                dve.wait_ge(exp_ready, (LEVELS + 2) * q + LEVELS + 1)
                nc.vector.tensor_tensor(fac[:, 1, :, :], z[:, zk:zk + HG, 0:TP], dec[:, 1, :, :], ALU.mult).then_inc(fac_ready, 1)
                take(LEVELS)
                filler(level_slots, LEVELS)
                dve.wait_ge(exp_ready, (LEVELS + 2) * (q + 1))
                nc.vector.tensor_tensor(fac[:, 0, :, 0:CH], z[:, zq:zq + HG, CH:TP], dec[:, 0, :, 0:CH], ALU.mult).then_inc(fac_ready, 1)
                dve.wait_ge(kv1_psum, q + 1)
                dve.wait_ge(s1_ready, q + 1)
                if q == 2:
                    dve.wait_ge(small_out, 16 * (SMALL_OUTS - 1))
                for h in range(HG):
                    o = h * dv
                    last = nc.vector.scalar_tensor_tensor(s2[:, o:o + dv], s1[:, o:o + dv], dec[:, 0, h, CH - 1:CH],
                                                          pm[:, o // 512, o % 512:o % 512 + dv], ALU.mult, ALU.add)
                last.then_inc(s2_ready, 1)

            def mix_low(n, batches):
                for i, (dst, src) in enumerate(batches):
                    dve.wait_ge(mix_hi, n + i + 1)
                    nc.vector.tensor_tensor(h_lo[:, dst:dst + 4, :], z[:, src:src + 4, :],
                                            h_hi[:, dst:dst + 4, :].bitcast(F32), ALU.subtract).then_inc(mix_ready, 1)

            recurrence(0, "ada0b", 0, range(8), range(8))
            dve.wait_ge(ors_ready, 1)
            gn = VB["ev_gla_norm"]
            for m in range(2):
                o_ = z[:, 8 + m:16:2, :]
                last = nc.vector.scalar_tensor_tensor(o_, o_, vb[:, gn + m:gn + m + 1], logp[:, :, :], ALU.mult, ALU.mult)
            step(last)
            dve.wait_ge(silu_ready, 1)
            for i in range(2):
                a = 8 + 4 * i
                nc.vector.tensor_tensor(z[:, a:a + 4, :], z[:, a:a + 4, :], z[:, a + 8:a + 12, :], ALU.mult).then_inc(mix_f32, 1)
            mix_low(0, [(8, 40), (12, 44), (0, 8), (4, 12)])
            n1 = PLAN["out0"][3]
            lo(n1, 0, 0)
            lo(n1, 1, 0)
            lo_phase(8, n1, res_evac(n1, 0, 0, G1))
            gains(0, VA["norm_mlp"], SC2)
            modulate(1, 0, SH2)

            def mlp_layer(l, r0):
                first = PLAN["ada1u0" if l == 0 else "up1_0"]
                g0, n0, a0 = first[2], first[3], first[4]
                s = 20 if l == 0 else 16
                gu = 2 if l == 0 else 0
                gd = 12 if l == 0 else 8

                def ada(f, b):
                    for p in range(2):
                        ada_evac(1, a0 + 4 * f + (2 * b + p), None, 8 * f + (4 * b + 2 * p), p)

                def chunk(f, last_chunk):
                    n, g = n0 + 16 * f, g0 + s * f
                    h = 8 * (FF_CHUNKS * l + f)
                    lo_phase(8, n, up_evac(n, g + gu, h), last_next=n + 8,
                             middle=(lambda: ada(f, 1)) if l == 0 else None)
                    lo_phase(8, n + 8, res_evac(n + 8, r0 + 8 * f, l, G2),
                             last_next=None if last_chunk else n + 16,
                             middle=(lambda: ada(f + 1, 0)) if l == 0 and not last_chunk else None)

                if l == 0:
                    ada(0, 0)
                lo(n0, 0, 0)
                lo(n0, 1, 0)
                with dve.Fori(0, FF_CHUNKS - 1) as f:
                    chunk(f, False)
                chunk(FF_CHUNKS - 1, True)

            mlp_layer(0, 8)
            gains(1, VA["norm_mix"] + KT, SC1)
            n2, g2 = PLAN["glu"][3], PLAN["glu"][2]
            lo(n2, 0, 0)
            lo(n2, 1, 0)
            modulate(2, 1, SH1)
            dve.wait_ge(cw_psum, 1)
            nc.vector.tensor_copy(conv_w[:, :, :], pm[:, 0, 0:8 * TAPS].rearrange("p (j r) -> p j r", r=TAPS)).then_inc(conv_step, 1)
            n3, g3 = PLAN["in1"][3], PLAN["in1"][2]
            lo_phase(8, n2, z_evac(n2, 32), last_next=n3)
            dve.wait_ge(gb_sig, 1)
            dve.wait_ge(conv_step, 1)
            nc.vector.tensor_tensor(z[:, 32:40, :], z[:, 32:40, :], z[:, 40:48, :], ALU.mult).then_inc(cv_in, 1)
            dve.wait_ge(cv_in, 1)

            PER_BLOCK = TAPS + 1

            def conv(j, s):
                src = zf[:, bass.ds((32 + j) * T, TP)]
                acc = [zf[:, bass.ds((40 + j) * T, TP)], acc1[:, :]]
                base = 1 + PER_BLOCK * j
                for shift in range(4 * s, min(4 * s + 4, TAPS)):
                    tap = TAPS - 1 - shift
                    wt = conv_w[:, bass.ds(j, 1), tap:tap + 1].rearrange("p a t -> p (a t)")
                    a = acc[shift % 2]
                    if shift == 0:
                        bias = vb[:, bass.ds(VB["od_conv_b"] + j, 1)]
                        ins = nc.vector.tensor_scalar(a, src, wt, bias, ALU.mult, ALU.add)
                    elif shift == 1:
                        step_zero = None
                        dve.wait_ge(conv_step, base)
                        nc.vector.tensor_scalar(a, src, 0.0, None, ALU.mult).then_inc(conv_zero, 1)
                        dve.wait_ge(conv_zero, j + 1)
                        ins = nc.vector.scalar_tensor_tensor(a[:, 1:TP], src[:, 0:TP - 1], wt, a[:, 1:TP], ALU.mult, ALU.add)
                    else:
                        dve.wait_ge(conv_step, base + (shift - 1))
                        ins = nc.vector.scalar_tensor_tensor(a[:, shift:TP], src[:, 0:TP - shift], wt, a[:, shift:TP],
                                                             ALU.mult, ALU.add)
                    ins.then_inc(conv_step, 1)
                if s == 7:
                    dve.wait_ge(conv_step, base + TAPS)
                    nc.vector.tensor_tensor(acc[0], acc[0], acc[1], ALU.add).then_inc(conv_step, 1)

            lo_phase(16, n3, z_evac(n3, 0), loop_work=conv)
            for j in range(8):
                dve.wait_ge(past_psum, 2 + j)
                wj = conv_w[:, j, 0:CONV_PAST].unsqueeze(1).broadcast_to([P, NS, CONV_PAST])
                past = pm[:, j % 2, 0:NS * CONV_PAST].rearrange("p (b r) -> p b r", r=CONV_PAST)
                nc.vector.tensor_tensor(cprod[:, :, :], past, wj, ALU.mult).then_inc(past_taken, 1)
                dve.wait_ge(past_taken, 2 + j)
                step(nc.vector.tensor_reduce(csum[:, :], cprod[:, :, :], AX.X, ALU.add))
                o_ = z[:, 40 + j, TP:T]
                step(nc.vector.scalar_tensor_tensor(o_, z[:, 32 + j, TP:T], conv_w[:, j, TAPS - 1:TAPS], csum[:, :], ALU.mult, ALU.add))
                cb = VB["od_conv_b"] + j
                nc.vector.tensor_scalar(o_, o_, vb[:, cb:cb + 1], None, ALU.add).then_inc(cv_done, 1)
            dve.wait_ge(ln_mean, 1)
            dve.wait_ge(conv_step, 1 + 8 * PER_BLOCK)
            cvz = z[:, 40:48, :]
            nc.vector.tensor_tensor(cvz, cvz, mean[:, :].unsqueeze(1).broadcast_to([P, 8, T]), ALU.subtract).then_inc(ln_cent, 1)
            dve.wait_ge(ln_rstd, 1)
            step(nc.vector.tensor_tensor(cvz, cvz, rstd[:, :].unsqueeze(1).broadcast_to([P, 8, T]), ALU.mult))
            for j in range(8):
                g_, b_ = VB["od_ln_g"] + j, VB["od_ln_b"] + j
                last = nc.vector.tensor_scalar(z[:, 40 + j, :], z[:, 40 + j, :], vb[:, g_:g_ + 1], vb[:, b_:b_ + 1], ALU.mult, ALU.add)
            last.then_inc(ln_done, 1)
            for q in (1, 2):
                zk = HEADS[q]["k"]
                dve.wait_ge(sig_ready, q)
                for h in range(HG):
                    c = HEADS[q]["q"] + h
                    nc.vector.tensor_scalar(z[:, zk + h, :], z[:, zk + h, :], oml[:, c:c + 1], None, ALU.mult)
                    last = nc.vector.tensor_scalar(logp[:, h, :], logp[:, h, :], oml[:, c:c + 1], lb[:, c:c + 1], ALU.mult, ALU.add)
                last.then_inc(k_ready, 1)
                dve.wait_ge(k_ready, q)
                nc.vector.tensor_scalar(gzf, lpf, MIN_GATE, 1.0 / TWO60, ALU.max, ALU.max)
                step(nc.vector.tensor_scalar(lpf, lpf, MIN_GATE, TWO60, ALU.max, ALU.mult))
                nc.vector.tensor_scalar(lpf, lpf, 1.0, None, ALU.min).then_inc(ln_in, 1)
                dve.wait_ge(ln_out, q)
                nc.vector.tensor_tensor(lpf, lpf, gzf, ALU.add).then_inc(logp_ready, 1)
                dve.wait_ge(logp_ready, q + 1)
                recurrence(q, "ada1b", 8 * (q - 1), range(0, 8, 2), range(0, 8, 2))
            dve.wait_ge(ors_ready, 3)
            hn = VB["od_hgrn_norm"]
            step(nc.vector.scalar_tensor_tensor(z[:, 16:24, :], z[:, 16:24, :], vb[:, hn:hn + 1], z[:, 8:16, :], ALU.mult, ALU.mult))
            dve.wait_ge(silu_ready, 2)
            for i in range(2):
                a = 16 + 4 * i
                nc.vector.tensor_tensor(z[:, a:a + 4, :], z[:, a:a + 4, :], z[:, a + 8:a + 12, :], ALU.mult).then_inc(mix_f32, 1)
            mix_low(4, [(8, 40), (12, 44), (0, 16), (4, 20)])
            n4 = PLAN["out1"][3]
            lo(n4, 0, 0)
            lo(n4, 1, 0)
            lo_phase(8, n4, res_evac(n4, 40, 1, G1))
            gains(1, VA["norm_mlp"] + KT, SC2)
            modulate(3, 1, SH2)
            mlp_layer(1, 48)
            dve.wait_ge(rstd_ready, 5)
            for k in range(KT):
                c = VA["norm_final"] + k
                nc.vector.scalar_tensor_tensor(x[:, k, :], x[:, k, :], va[:, c:c + 1], rstd[:, :], ALU.mult, ALU.mult).then_inc(y_ready, 1)


INPUTS = ["x_prompt", "x_sample", "c_prompt", "c_sample", "state_gla", "state_pool", "state_hgrn", "state_conv",
          "w_ada", "b_ada", "norm_mix", "norm_mlp", "norm_final", "ev_w_in", "ev_w_gate_up", "ev_b_gate",
          "ev_gla_norm", "ev_pool_w", "ev_pool_scale", "ev_w_out", "od_w_in", "od_lb_raw", "od_hgrn_norm",
          "od_conv_w", "od_conv_b", "od_ln_g", "od_ln_b", "od_w_out", "mlp_w_up", "mlp_w_down"]
OUTPUTS = [("y_prompt", (1, 256, 2048)), ("y_sample", (8, 1, 2048)),
           ("new_gla_prompt", (1, 1, 4, 128, 256)), ("new_pool_prompt", (1, 1, 15, 1024)),
           ("new_hgrn_prompt", (1, 1, 8, 128, 128)), ("new_conv_prompt", (1, 1, 30, 1024)),
           ("new_gla_sample", (1, 8, 4, 128, 256)), ("new_pool_sample", (1, 8, 15, 1024)),
           ("new_hgrn_sample", (1, 8, 8, 128, 128)), ("new_conv_sample", (1, 8, 30, 1024))]


def kernel(**inputs):
    import concourse.bacc as bacc
    from concourse.bass_utils import run_bass_kernel_spmd

    nc = bacc.Bacc("TRN2", target_bir_lowering=False, num_devices=1)
    arrays, io, out = {}, {}, {}
    for name, a in list((n, inputs[n]) for n in INPUTS) + list(constants().items()):
        a = np.ascontiguousarray(a)
        arrays[f"in_{name}"] = a
        io[name] = nc.dram_tensor(f"in_{name}", a.shape, mybir.dt.from_np(a.dtype), kind="ExternalInput").ap()
    for name, shape in OUTPUTS:
        out[name] = nc.dram_tensor(f"out_{name}", shape, F32, kind="ExternalOutput").ap()
    build(nc, io, out)
    r = run_bass_kernel_spmd(nc, [arrays], core_ids=[0])
    return tuple(r.results[0][f"out_{name}"] for name, _ in OUTPUTS)
```

```python
from contextlib import ExitStack

import numpy as np

import concourse.bass as bass
from concourse import mybir

F32 = mybir.dt.float32
F32R = mybir.dt.float32r
I32 = mybir.dt.int32
U8 = mybir.dt.uint8
ALU = mybir.AluOpType
ACT = mybir.ActivationFunctionType
AX = mybir.AxisListType

P = 128
D = 2048
KT = D // P
TP = 256
NS = 8
T = TP + NS
NC = NS + 1
GC = 256
MT = GC // P
UK = 4
NU = KT // UK
UW = UK * GC
CH = 128
NCH = TP // CH
LEVELS = 7
HG = 4
DK = 128
WINDOWS = (2, 4, 8, 16)
POOL_PAST = 15
TAPS = 31
CONV_PAST = 30
EPS = 1e-6
MIN_GATE = 1e-30
TWO60 = float(2 ** 60)
FF_CHUNKS = 4
POOL_TAIL = POOL_PAST + NS
CONV_TAIL = CONV_PAST + NS

VA = {"norm_mix": 0, "norm_mlp": 32, "norm_final": 64}
VB = {"ev_b_gate": 0, "ev_gla_norm": 4, "ev_pool_scale": 6, "od_lb_raw": 14, "od_hgrn_norm": 22,
      "od_conv_b": 23, "od_ln_g": 31, "od_ln_b": 39}
VB_ROWS = 47
SH1, SC1, G1, SH2, SC2, G2 = range(0, 96, 16)


def make_plan():
    order = [("ada0a", "ada", 16), ("in0", "gemm", 16), ("ada0b", "ada", 32), ("out0", "gemm", 8)]
    for f in range(FF_CHUNKS):
        order += [(f"ada1u{f}", "ada", 2), (f"up0_{f}", "gemm", 8),
                  (f"ada1d{f}", "ada", 2), (f"down0_{f}", "gemm", 8)]
    order += [("glu", "gemm", 8), ("in1", "gemm", 16), ("ada1b", "ada", 32), ("out1", "gemm", 8)]
    for f in range(FF_CHUNKS):
        order += [(f"up1_{f}", "gemm", 8), (f"down1_{f}", "gemm", 8)]
    plan, g, a = {}, 0, 0
    for name, kind, count in order:
        plan[name] = (kind, count, g, a)
        g += count
        a += count if kind == "ada" else 0
    return plan


PLAN = make_plan()


def constants():
    s, t = np.arange(CH)[:, None], np.arange(CH)[None, :]
    masks = np.zeros((CH, LEVELS, CH), np.int32)
    for lv in range(LEVELS):
        h = 1 << lv
        masks[:, lv, :] = (s // (2 * h) == t // (2 * h)) & (s % (2 * h) < h) & (t % (2 * h) >= h)
    inv = np.zeros((P, len(WINDOWS), 16), np.float32)
    for g, w in enumerate(WINDOWS):
        inv[:, g, :] = 1.0 / np.minimum(np.arange(16) + 1, w).astype(np.float32)
    return {"ident": np.eye(P, dtype=np.float32), "masks": masks.reshape(CH, LEVELS * CH),
            "inv_count": inv.reshape(P, -1)}


START_BANKS = 2 + KT
CONSTS = 1 + len(VA) + len(VB) + 3
SMALL_OUTS = 9
CHUNK_GROUPS = (20, 16)
OPAIRS = [0, 4, 6, 8]


class Count:
    def __init__(self):
        self.n = 0

    def next(self):
        self.n += 1
        return self.n


def build(nc, io, out):
    stack = ExitStack()
    with stack:
        used = [(nc.sbuf_base + 31) // 32 * 32]

        def at(name, shape, dt, offset):
            return nc.alloc_sbuf_tensor_at(name, shape, dt, offset=offset)

        def sb(name, shape, dt=F32):
            size = int(np.prod(shape[1:])) * (1 if dt == U8 else 4)
            offset = used[0]
            used[0] += (size + 31) // 32 * 32
            assert used[0] <= nc.sbuf_top, (name, used[0], nc.sbuf_top)
            return at(name, shape, dt, offset)

        def arena(size):
            offset = used[0]
            used[0] += (size + 31) // 32 * 32
            assert used[0] <= nc.sbuf_top
            return offset

        def sem(name):
            return stack.enter_context(nc.semaphore(name))

        x = sb("x", [P, KT, T])
        raw = sb("raw", [P, 2, NU, UW])
        w_hi = sb("w_hi", [P, NU, UW], F32R)
        w_lo = sb("w_lo", [P, NU, UW], F32R)
        mod = sb("mod", [P, 2, 96, NC])
        amod = sb("amod", [P, KT, NC])
        CW = 2 * NC
        c_hl = sb("c_hl", [P, KT * CW + P - CW], F32R)
        sel = sb("sel", [CW, NC])
        mod_rows = sb("mod_rows", [CW, 2, GC])
        bada = sb("bada", [P, 2, 96])
        va = sb("va", [P, 80])
        vb = sb("vb", [P, VB_ROWS])
        ident = sb("ident", [P, P])
        ones = sb("ones", [P, P])
        zero = sb("zero", [P, 1])
        masks = sb("masks", [P, LEVELS, CH], U8)
        inv_count = sb("inv_count", [P, len(WINDOWS), 16])
        lb = sb("lb", [P, 8])
        oml = sb("oml", [P, 8])
        sm = sb("sm", [P, 8])
        eps_t = sb("eps_t", [P, 1])
        o_rs = arena(2 * T * 4)
        rstd = at("rstd", [P, T], F32, o_rs)
        lnv = at("lnv", [P, T], F32, o_rs + T * 4)
        pb = at("pb", [P, 2, TP], F32, o_rs)
        o_hid = arena(MT * T * 4)
        hid = at("hid", [P, MT, T], F32, o_hid)
        pa = at("pa", [P, 2, TP], F32, o_hid)
        g8 = sb("g8", [P, MT, NS])
        t8 = sb("t8", [P, KT, NS])
        wsum = sb("wsum", [P, MT, NS])
        decay8 = sb("decay8", [P, HG, NS])
        logp = sb("logp", [P, HG, T])
        o_sq = arena(2 * MT * T * 4)
        sq = at("sq", [P, 2, MT, T], F32, o_sq)
        hs = at("hs", [P, 4, TP], F32, o_sq)
        o_mw = arena(8192)
        pool_w = at("pool_w", [P, 4, 2, 256], F32, o_mw)
        conv_w = at("conv_w", [P, 8, TAPS], F32, o_mw)
        acc1 = at("acc1", [P, TP], F32, o_mw + 1024)
        cprod = at("cprod", [P, NS, CONV_PAST], F32, o_mw + 2048)
        csum = at("csum", [P, NS], F32, o_mw + 3072)
        mean = at("mean", [P, T], F32, o_mw + 3200)
        cw_rows = at("cw_rows", [TAPS, 1024], F32, o_mw + 4352 - 256)
        o_gw = arena(2048)
        gate_up = at("gate_up", [16, 512], F32, o_gw)
        o_h = arena(2 * KT * T * 4)
        h_hi = at("h_hi", [P, KT, T], F32R, o_h)
        h_lo = at("h_lo", [P, KT, T], F32R, o_h + KT * T * 4)
        dec = at("dec", [P, 2, HG, TP], F32, o_h)
        gz = at("gz", [P, HG, T], F32, o_h)
        gl = at("gl", [P, HG, T], F32, o_h + 8448)
        fac = at("fac", [P, 2, HG, TP], F32, o_h + 8192)
        st = at("st", [P, 2, 1024], F32, o_h + 8192)
        scores = at("scores", [P, NCH, HG, CH], F32, o_h + 16384)
        kmask = at("kmask", [NS, 2, HG * DK], F32, o_h + 16384)
        s1 = at("s1", [P, 1024], F32, o_h + 20480)
        k8 = at("k8", [NS, HG * DK], F32, o_h + 20480)
        kdT = at("kdT", [P, NCH, HG * DK], F32, o_h + 24576)
        v8 = at("v8", [NS, 1024], F32, o_h + 24576)
        s2 = at("s2", [P, 1024], F32, o_h + 28672)
        o_z = arena(48 * T * 4)
        z = at("z", [P, 48, T], F32, o_z)
        zf = z[:, :, :].rearrange("p a t -> p (a t)")
        f_hi = at("f_hi", [P, KT, T], F32R, o_z)
        f_lo = at("f_lo", [P, KT, T], F32R, o_z + KT * T * 4)
        x_rows = at("x_rows", [P, NCH, D], F32, o_z)
        xs_rows = at("xs_rows", [NS, D], F32, o_z + 16384)
        c_rows = at("c_rows", [NC, D], F32, o_z + 24576)
        va_rows = at("va_rows", [80, P], F32, o_z + 32768)
        vb_rows = at("vb_rows", [VB_ROWS, P], F32, o_z + 33280)
        ba_rows = at("ba_rows", [96, 2, P], F32, o_z + 33792)
        cs_rows = at("cs_rows", [NC, D], F32, o_z + 34816)
        mask_rows = at("mask_rows", [P, LEVELS, CH], I32, o_z + 43008)
        y_rows = at("y_rows", [P, NCH, D], F32, o_z)
        ys_rows = at("ys_rows", [NS, D], F32, o_z + 16384)
        vT_at = {0: o_z + 40 * T * 4, 1: o_z + 32 * T * 4}
        vT = {layer: at(f"vT{layer}", [P, NCH, 1024], F32, vT_at[layer]) for layer in range(2)}
        a_w = at("a_w", [P, KT, 16], F32, o_z + 46 * T * 4)
        pastc = at("pastc", [120, 2, 1024], F32, o_h + 8192)
        pastu = at("pastu", [120, 1024], F32, o_h + 28672)
        AW = KT * 16 + P - 16
        a_hi = at("a_hi", [P, AW], F32R, o_sq)
        a_lo = at("a_lo", [P, AW], F32R, o_sq + AW * 4)
        a_lr = at("a_lr", [16, T], F32, o_sq + 2 * AW * 4)
        tail = sb("tail", [CONV_TAIL, 1024])

        ps = stack.enter_context(nc.psum_tensor("ps", [P, 4, 512], F32))
        pm = stack.enter_context(nc.psum_tensor("pm", [P, 4, 512], F32))

        raw_in = [[sem(f"raw_in{p}{h}") for h in range(2)] for p in range(2)]
        hi_ready = sem("hi_ready")
        lo_ready = sem("lo_ready")
        split_used = sem("split_used")
        evacuated = sem("evacuated")
        turned = sem("turned")
        mod_ready = sem("mod_ready")
        rows_in = sem("rows_in")
        const_in = sem("const_in")
        c_silu = sem("c_silu")
        c_high = sem("c_high")
        tr_ready = sem("tr_ready")
        tr_taken = sem("tr_taken")
        filled = sem("filled")
        sq_ready = sem("sq_ready")
        ss_done = sem("ss_done")
        x_ready = sem("x_ready")
        gate8_done = sem("gate8_done")
        rstd_ready = sem("rstd_ready")
        t8_ready = sem("t8_ready")
        h8_hi = sem("h8_hi")
        hs_ready = sem("hs_ready")
        hh_ready = sem("hh_ready")
        h_ready = sem("h_ready")
        hid_relu = sem("hid_relu")
        hid_sq = sem("hid_sq")
        hid_hi = sem("hid_hi")
        hid_ready = sem("hid_ready")
        mix_hi = sem("mix_hi")
        mix_ready = sem("mix_ready")
        mix_f32 = sem("mix_f32")
        dve_step = sem("dve_step")
        act_step = sem("act_step")
        pool_step = sem("pool_step")
        aw_in = sem("aw_in")
        aw_hi = sem("aw_hi")
        aw_lo = sem("aw_lo")
        alr_psum = sem("alr_psum")
        alr_ready = sem("alr_ready")
        gate_psum = sem("gate_psum")
        gz_ready = sem("gz_ready")
        gl_ready = sem("gl_ready")
        logp_ready = sem("logp_ready")
        q_scaled = sem("q_scaled")
        past_in = sem("past_in")
        past_psum = sem("past_psum")
        past_taken = sem("past_taken")
        tail_psum = sem("tail_psum")
        tail_ready = sem("tail_ready")
        pool_d = sem("pool_d")
        pool_psum = sem("pool_psum")
        pool_taken = sem("pool_taken")
        k_ready = sem("k_ready")
        sig_ready = sem("sig_ready")
        ln_in = sem("ln_in")
        ln_out = sem("ln_out")
        vtr_psum = sem("vtr_psum")
        vtr_ready = sem("vtr_ready")
        dec8_ready = sem("dec8_ready")
        kmask_ready = sem("kmask_ready")
        kv_psum = sem("kv_psum")
        st_in = [sem(f"st_in{i}") for i in range(2)]
        st_ready = sem("st_ready")
        st_out = [sem(f"st_out{i}") for i in range(2)]
        o8_psum = sem("o8_psum")
        o8_taken = sem("o8_taken")
        sc_psum = sem("sc_psum")
        sc_taken = sem("sc_taken")
        prefix_ready = sem("prefix_ready")
        dif_ready = sem("dif_ready")
        exp_ready = sem("exp_ready")
        fac_ready = sem("fac_ready")
        kd_psum = sem("kd_psum")
        kd_ready = sem("kd_ready")
        s1_psum = sem("s1_psum")
        s1_ready = sem("s1_ready")
        kv1_psum = sem("kv1_psum")
        s2_ready = sem("s2_ready")
        o_psum = sem("o_psum")
        o_ready = sem("o_ready")
        osq_ready = sem("osq_ready")
        oss_psum = sem("oss_psum")
        ors_ready = sem("ors_ready")
        silu_ready = sem("silu_ready")
        cw_psum = sem("cw_psum")
        gb_sig = sem("gb_sig")
        cv_in = sem("cv_in")
        conv_step = sem("conv_step")
        ln_psum = sem("ln_psum")
        ln_mean = sem("ln_mean")
        ln_cent = sem("ln_cent")
        ln_sq = sem("ln_sq")
        ln_rstd = sem("ln_rstd")
        ln_done = sem("ln_done")
        cv_ready = sem("cv_ready")
        cv_done = sem("cv_done")
        conv_zero = sem("conv_zero")
        lb_exp = sem("lb_exp")
        y_ready = sem("y_ready")
        y_psum = sem("y_psum")
        y_taken = sem("y_taken")
        small_out = sem("small_out")
        y_out = sem("y_out")

        HEADS = [dict(layer=0, nv=8, dv=256, q=0, k=4, v=8), dict(layer=1, nv=4, dv=128, q=0, k=8, v=16),
                 dict(layer=1, nv=4, dv=128, q=4, k=12, v=20)]
        SETS = 1 + LEVELS
        BANKS_Z = 2 * KT

        def halves(t, w):
            v = t.rearrange("p h (n s w) -> p h n s w", s=2, w=w)
            return v[:, :, :, 0, :], v[:, :, :, 1, :]

        def heads_of(t, nv):
            return t.rearrange("p a t -> p (a t)")

        def bank2(p):
            return ps[:, MT * p:MT * p + MT, 0:T]

        block = stack.enter_context(nc.Block())

        @block.sync
        def _(sp):
            def group(g, p, view, col, k0):
                for h in range(2):
                    if not isinstance(g, int) or g >= 2:
                        sp.wait_ge(lo_ready, NU * (g - 2) + (2 * h + 2))
                    sp.dma_start(raw[:, p, 2 * h:2 * h + 2, :].rearrange("p u (k n) -> p (u k) n", n=GC),
                                 view[:, bass.ds(k0 + 8 * h, 8), bass.ds(col, GC)]).then_inc(raw_in[p][h], 16)

            def phase(count, g, view, col, k0=0):
                peel = 1 if count == 2 or (isinstance(g, int) and g == 0) else 0
                for i in range(2 * peel):
                    group(g + i, i, view, col(i), k0)
                if count // 2 > peel:
                    with sp.Fori(0, count // 2 - peel) as j:
                        for p in range(2):
                            i = 2 * j + (2 * peel + p)
                            group(g + i, p, view, col(i), k0)

            def kview(w):
                return w.rearrange("(k p) n -> p k n", p=P)

            def static_phase(name, view, col, k0=0):
                phase(PLAN[name][1], PLAN[name][2], view, col, k0)

            sp.dma_start(c_rows[0:1, :], io["c_prompt"]).then_inc(rows_in, 16)
            sp.dma_start(c_rows[1:NC, :], io["c_sample"]).then_inc(rows_in, 16)
            sp.dma_start(x_rows[:, :, :], io["x_prompt"][0].rearrange("(c p) d -> p c d", p=P)).then_inc(rows_in, 16)
            sp.dma_start(xs_rows[:, :], io["x_sample"].rearrange("b t d -> (b t) d")).then_inc(rows_in, 16)
            ada = [kview(io["w_ada"][l]) for l in range(2)]
            up = [kview(io["mlp_w_up"][l]) for l in range(2)]
            down = [kview(io["mlp_w_down"][l]) for l in range(2)]
            static_phase("ada0a", ada[0], lambda i: i * GC)
            g0 = PLAN["in0"][2]
            w = kview(io["ev_w_in"][0])
            phase(12, g0, w, lambda i: i * GC)
            phase(4, g0 + 12, w, lambda i: (12 + i) * GC + 16)
            static_phase("ada0b", ada[0], lambda i: (16 + i) * GC)
            static_phase("out0", kview(io["ev_w_out"][0]), lambda i: i * GC)

            def mlp_layer(l):
                g0 = PLAN["ada1u0" if l == 0 else "up1_0"][2]
                with sp.Fori(0, FF_CHUNKS) as f:
                    g = g0 + CHUNK_GROUPS[l] * f
                    for b in range(2):
                        if l == 0:
                            phase(2, g, ada[1], lambda i: (4 * f + 2 * b + i) * GC)
                            g = g + 2
                        if b == 0:
                            phase(8, g, up[l], lambda i: f * D + i * GC)
                        else:
                            phase(8, g, down[l], lambda i: i * GC, k0=f * KT)
                        g = g + 8

            mlp_layer(0)
            w = kview(io["od_w_in"][0])
            static_phase("glu", w, lambda i: (16 + i) * GC)
            static_phase("in1", w, lambda i: i * GC)
            static_phase("ada1b", ada[1], lambda i: (16 + i) * GC)
            static_phase("out1", kview(io["od_w_out"][0]), lambda i: i * GC)
            mlp_layer(1)
            for r in range(3):
                sp.wait_ge(y_taken, 4 * (r + 1))
                if r < 2:
                    sp.dma_start(out["y_prompt"][0, r * P:(r + 1) * P, :], y_rows[:, r, :]).then_inc(y_out, 16)
                else:
                    sp.dma_start(out["y_sample"].rearrange("b t d -> (b t) d"), ys_rows[:, :]).then_inc(y_out, 16)
            sp.wait_ge(y_out, 48)
            sp.wait_ge(small_out, 16 * SMALL_OUTS)
            for i in range(2):
                sp.wait_ge(st_out[i], 16 * 4 * len(HEADS))

        @block.gpsimd
        def _(pool):
            steps = Count()

            def step(ins):
                ins.then_inc(pool_step, 1)
                pool.wait_ge(pool_step, steps.next())

            pool.dma_start(out["new_pool_sample"][0, :, 0:POOL_PAST - 1, :],
                           io["state_pool"][0, :, 1:POOL_PAST, :]).then_inc(small_out, 16)
            pool.dma_start(out["new_conv_sample"][0, :, 0:CONV_PAST - 1, :],
                           io["state_conv"][0, :, 1:CONV_PAST, :]).then_inc(small_out, 16)
            pool.dma_start(gate_up[:, :], io["ev_w_gate_up"][0]).then_inc(aw_in, 16)
            pool.dma_start(pool_w[:, :, :, :], io["ev_pool_w"][0].rearrange("g (c p) e -> p g c e", p=P)).then_inc(aw_in, 16)
            pool.wait_ge(tr_ready, START_BANKS)
            pool.dma_start(a_w[:, :, :], io["ev_w_in"][0][:, 3072:3088].rearrange("(k p) n -> p k n", p=P)).then_inc(aw_in, 16)

            def states(q):
                h = HEADS[q]
                n = HG * h["dv"]
                if h["layer"] == 0:
                    src, dst, hsl = io["state_gla"][0], out["new_gla_sample"][0], slice(0, HG)
                else:
                    src, dst, hsl = io["state_hgrn"][0], out["new_hgrn_sample"][0], slice(h["q"], h["q"] + HG)

                def load(b):
                    pool.dma_start(st[:, b % 2, 0:n].rearrange("p (h v) -> p h v", h=HG),
                                   src[b, hsl].rearrange("h k v -> k h v")).then_inc(st_in[b % 2], 16)

                pool.wait_ge(vtr_psum, 4 * q + 1)
                load(0)
                load(1)
                for b in range(NS):
                    pool.wait_ge(st_ready, NS * q + b + 1)
                    pool.dma_start(dst[b, hsl].rearrange("h k v -> k h v"),
                                   st[:, b % 2, 0:n].rearrange("p (h v) -> p h v", h=HG)).then_inc(st_out[b % 2], 16)
                    if b + 2 < NS:
                        pool.wait_ge(o8_psum, NS * q + b + 1)
                        pool.wait_ge(st_out[b % 2], 16 * (4 * q + b // 2 + 1))
                        load(b + 2)

            def prompt_state(q):
                h = HEADS[q]
                name, hsl = ("new_gla_prompt", slice(0, HG)) if h["layer"] == 0 else ("new_hgrn_prompt", slice(h["q"], h["q"] + HG))
                pool.wait_ge(s2_ready, q + 1)
                pool.dma_start(out[name][0, 0, hsl].rearrange("h k v -> k h v"),
                               s2[:, 0:HG * h["dv"]].rearrange("p (h v) -> p h v", h=HG)).then_inc(small_out, 16)

            pool.wait_ge(evacuated, PLAN["in0"][2] + 16)
            pool.wait_ge(alr_psum, 1)
            pool.dma_start(pastu[:, :], io["state_pool"][0].rearrange("b r c -> (b r) c")).then_inc(past_in, 16)
            states_first = None
            u = z[:, 24:32, 0:TP]
            for g, w in enumerate(WINDOWS):
                src, width, bufs = u[:, 2 * g:2 * g + 2, :], 1, [pa, pb]
                while width < w:
                    dst = bufs[0]
                    bufs.reverse()
                    nc.gpsimd.tensor_copy(dst[:, :, 0:width], src[:, :, 0:width])
                    step(nc.gpsimd.tensor_tensor(dst[:, :, width:TP], src[:, :, width:TP], src[:, :, 0:TP - width], ALU.add))
                    src, width = dst, 2 * width
                d = z[:, 32 + 2 * g:34 + 2 * g, 0:TP]
                inv = inv_count[:, g:g + 1, :].broadcast_to([P, 2, 16])
                nc.gpsimd.tensor_tensor(d[:, :, 0:16], src[:, :, 0:16], inv, ALU.mult)
                step(nc.gpsimd.tensor_scalar(d[:, :, 16:TP], src[:, :, 16:TP], 1.0 / w, None, ALU.mult))
                nc.gpsimd.tensor_tensor(d, d, u[:, 2 * g:2 * g + 2, :], ALU.subtract).then_inc(pool_d, 1)
            states(0)
            pool.wait_ge(tail_ready, 1)
            pool.dma_start(out["new_pool_prompt"][0, 0], tail[0:POOL_PAST, :]).then_inc(small_out, 16)
            pool.dma_start(out["new_pool_sample"][0, :, POOL_PAST - 1, :], tail[POOL_PAST:POOL_TAIL, :]).then_inc(small_out, 16)
            prompt_state(0)
            pool.wait_ge(pool_psum, 4)
            pool.dma_start(cw_rows[:, :], io["od_conv_w"][0]).then_inc(aw_in, 16)
            pool.wait_ge(split_used, NU * (PLAN["in1"][2] + 16))
            pool.dma_start(pastc[:, :, :], io["state_conv"][0].rearrange("(a b) r c -> (b r) a c", b=4)).then_inc(past_in, 16)
            pool.wait_ge(tail_ready, 2)
            pool.dma_start(out["new_conv_prompt"][0, 0], tail[0:CONV_PAST, :]).then_inc(small_out, 16)
            pool.dma_start(out["new_conv_sample"][0, :, CONV_PAST - 1, :], tail[CONV_PAST:CONV_TAIL, :]).then_inc(small_out, 16)
            for q in (1, 2):
                states(q)
                prompt_state(q)

        @block.tensor
        def _(pe):
            def gemm(count, g, xh, xl, ready, norm=None):
                def sums(i):
                    pe.wait_ge(sq_ready, norm + i + 1)
                    for m in range(MT):
                        last = nc.tensor.matmul(pm[:, 0, 0:T], ones[:, :], sq[:, i_parity[0], m, :], start=False,
                                                stop=False, skip_group_check=True)
                    last.then_inc(ss_done, 1)

                i_parity = [0]

                def body(i, p):
                    pe.wait_ge(evacuated, g + i - 1)
                    for u in range(NU):
                        ready(u)
                        pe.wait_ge(lo_ready, NU * (g + i) + (u + 1))
                        for m in range(MT):
                            acc = ps[:, MT * p + m, 0:T]
                            for kk in range(UK):
                                k = UK * u + kk
                                cols = slice(kk * GC + m * P, kk * GC + (m + 1) * P)
                                nc.tensor.matmul(acc, w_hi[:, u, cols], xh[:, k, :], start=(k == 0), stop=False)
                                nc.tensor.matmul(acc, w_hi[:, u, cols], xl[:, k, :], start=False, stop=False)
                                last = nc.tensor.matmul(acc, w_lo[:, u, cols], xh[:, k, :], start=False, stop=(k == KT - 1))
                        last.then_inc(split_used, 1)

                if norm is None:
                    with pe.Fori(0, count // 2) as j:
                        for p in range(2):
                            body(2 * j + p, p)
                    return
                for p in range(2):
                    body(p, p)
                nc.tensor.matmul(pm[:, 0, 0:T], ones[:, :], zero[:, :].broadcast_to([P, T]), start=True, stop=False, skip_group_check=True)
                i_parity[0] = 0
                sums(0)
                with pe.Fori(0, count // 2 - 1) as j:
                    for p in range(2):
                        i = 2 * j + (2 + p)
                        body(i, p)
                        i_parity[0] = 1 - p
                        sums(i - 1)
                i_parity[0] = 1
                sums(count - 1)

            def ada_turn(a, p):
                pe.wait_ge(mod_ready, a - 1) if not isinstance(a, int) or a >= 2 else None
                for m in range(MT):
                    last = nc.tensor.matmul(ps[:, MT * p + 1, m * NC:(m + 1) * NC], mod_rows[:, p, m * P:(m + 1) * P],
                                            sel[:, :], start=True, stop=True)
                last.then_inc(turned, 1)

            def ada_group(a, g, p, turn_last=True):
                if not isinstance(g, int) or g >= 2:
                    pe.wait_ge(evacuated, g - 1)
                for u in range(NU):
                    pe.wait_ge(lo_ready, NU * g + (u + 1))
                    for kk in range(UK):
                        k = UK * u + kk
                        rows = c_hl[:, k * CW:k * CW + P]
                        for part, first in ((w_hi, True), (w_lo, False)):
                            last = nc.tensor.matmul(ps[:, MT * p, 0:GC], rows, part[:, u, kk * GC:(kk + 1) * GC],
                                                    start=(k == 0 and first), stop=(k == KT - 1 and not first))
                    last.then_inc(split_used, 1)
                    if u == 1 and turn_last:
                        pe.wait_ge(evacuated, g)
                        ada_turn(a - 1, 1 - p)

            def ada_end(a, g):
                pe.wait_ge(evacuated, g)
                ada_turn(a - 1, 1)

            def ada_pair(a, g):
                ada_group(a, g, 0, turn_last=False)
                ada_group(a + 1, g + 1, 1)
                ada_end(a + 2, g + 2)

            def turn(dst, src, rows):
                return nc.tensor.transpose(dst, src, ident[0:rows, 0:rows])

            pe.wait_ge(const_in, 16 * CONSTS)
            pe.wait_ge(filled, 1)
            turn(pm[:, 0, 0:80], va_rows[:, :], 80)
            turn(pm[:, 0, 80:80 + VB_ROWS], vb_rows[:, :], VB_ROWS)
            turn(pm[:, 0, 128:224], ba_rows[:, 0, :], 96)
            turn(pm[:, 0, 224:320], ba_rows[:, 1, :], 96).then_inc(tr_ready, 1)
            pe.wait_ge(c_silu, 1)
            for k in range(KT):
                last = turn(pm[:, 1, k * NC:(k + 1) * NC], cs_rows[:, k * P:(k + 1) * P], NC)
            last.then_inc(tr_ready, 1)
            pe.wait_ge(rows_in, 64)
            for k in range(KT):
                b = (2 + k) % 4
                if k >= 2:
                    pe.wait_ge(tr_taken, k - 1)
                for c in range(NCH):
                    turn(pm[:, b, c * P:(c + 1) * P], x_rows[:, c, k * P:(k + 1) * P], P)
                turn(pm[:, b, TP:T], xs_rows[:, k * P:(k + 1) * P], NS).then_inc(tr_ready, 1)
            pe.wait_ge(tr_taken, START_BANKS)
            for i in range(KT // 2):
                pe.wait_ge(sq_ready, i + 1)
                for m in range(MT):
                    last = nc.tensor.matmul(pm[:, 0, 0:T], ones[:, :], sq[:, i % 2, m, :], start=(i + m == 0),
                                            stop=(i + m == KT // 2), skip_group_check=True)
                last.then_inc(ss_done, 1)
            count = PLAN["ada0a"][1]
            ada_group(0, 0, 0, turn_last=False)
            for i in range(1, 4):
                ada_group(i, i, i % 2)
            with pe.Fori(0, count // 2 - 2) as j:
                for p in range(2):
                    ada_group(2 * j + (4 + p), 2 * j + (4 + p), p)
            ada_end(count, count)

            def h_wait(n):
                return lambda u: pe.wait_ge(h_ready, KT * n + UK * (u + 1))

            pe.wait_ge(mod_ready, PLAN["ada0b"][3])
            gemm(16, PLAN["in0"][2], h_hi, h_lo, h_wait(0))
            pe.wait_ge(aw_lo, 1)
            pe.wait_ge(rstd_ready, 1)
            for k in range(KT):
                cols = slice(16 * k, 16 * k + P)
                nc.tensor.matmul(pm[:, 0, 0:T], a_hi[:, cols], h_hi[:, k, :], start=(k == 0), stop=False)
                nc.tensor.matmul(pm[:, 0, 0:T], a_hi[:, cols], h_lo[:, k, :], start=False, stop=False)
                last = nc.tensor.matmul(pm[:, 0, 0:T], a_lo[:, cols], h_hi[:, k, :], start=False, stop=(k == KT - 1))
            last.then_inc(alr_psum, 1)
            pe.wait_ge(alr_ready, 1)
            for h in range(HG):
                last = nc.tensor.matmul(pm[:, h, 0:T], gate_up[:, h * DK:(h + 1) * DK], a_lr[:, :], start=True, stop=True)
            last.then_inc(gate_psum, 1)
            pe.wait_ge(evacuated, PLAN["in0"][2] + 16)
            pe.wait_ge(gz_ready, 1)
            for j in range(8):
                last = turn(pm[0:POOL_TAIL, 2 + j // 4, (j % 4) * P:(j % 4 + 1) * P],
                            z[:, 24 + j, T - POOL_TAIL:T], P)
            last.then_inc(tail_psum, 1)
            pe.wait_ge(past_in, 16)
            for j in range(8):
                last = turn(pm[:, j // 4, (j % 4) * 120:(j % 4 + 1) * 120], pastu[:, j * P:(j + 1) * P], 120)
            last.then_inc(past_psum, 1)
            pe.wait_ge(tail_ready, 1)
            pe.wait_ge(past_taken, 1)

            def recurrence(q, ada_name, ada_first, sample_slots, level_slots):
                hd = HEADS[q]
                nv, dv, zq, zk, zv = hd["nv"], hd["dv"], hd["q"], hd["k"], hd["v"]
                vt = vT[hd["layer"]]
                fill = [ada_first]

                def filler(slots, s):
                    if s in slots:
                        _, count, g0, a0 = PLAN[ada_name]
                        j = fill[0]
                        ada_group(a0 + 2 * j, g0 + 2 * j, 0, turn_last=j > 0)
                        ada_group(a0 + 2 * j + 1, g0 + 2 * j + 1, 1)
                        if 2 * j + 2 == count:
                            ada_end(a0 + count, g0 + count)
                        fill[0] += 1

                for c in range(NCH):
                    for j in range(nv):
                        b = c * (nv // 4) + j // 4
                        last = turn(pm[:, b, (j % 4) * P:(j % 4 + 1) * P], z[:, zv + j, c * CH:(c + 1) * CH], P)
                    last.then_inc(vtr_psum, 1)
                pe.wait_ge(vtr_ready, 4 * q + 2)
                for j in range(nv):
                    last = turn(pm[0:NS, j // 4, (j % 4) * P:(j % 4 + 1) * P], z[:, zv + j, TP:T], P)
                last.then_inc(vtr_psum, 1)
                if q:
                    pe.wait_ge(k_ready, q)
                for h in range(HG):
                    last = turn(pm[0:NS, 2, h * P:(h + 1) * P], z[:, zk + h, TP:T], P)
                last.then_inc(vtr_psum, 1)
                pe.wait_ge(vtr_ready, 4 * q + 4)
                pe.wait_ge(q_scaled, 1)
                for b in range(NS):
                    pe.wait_ge(kmask_ready, NS * q + b + 1)
                    if NS * q + b:
                        pe.wait_ge(st_ready, NS * q + b)
                    for h in range(HG):
                        o = h * dv
                        last = nc.tensor.matmul(pm[:, o // 512, o % 512:o % 512 + dv], kmask[:, b % 2, h * DK:(h + 1) * DK],
                                                v8[:, o:o + dv], start=True, stop=True)
                    last.then_inc(kv_psum, 1)
                    filler(sample_slots, b)
                    pe.wait_ge(st_ready, NS * q + b + 1)
                    for j in range(nv):
                        last = nc.tensor.matmul(pm[:, 3, j * NS + b:j * NS + b + 1], st[:, b % 2, j * P:(j + 1) * P],
                                                z[:, zq + j * P // dv, TP + b:TP + b + 1], start=True, stop=True)
                    last.then_inc(o8_psum, 1)
                for i in range(SETS):
                    if i == 0:
                        lhs = [[z[:, zk + h, c * CH:(c + 1) * CH] for h in range(HG)] for c in range(NCH)]
                        rhs = [[z[:, zq + h, c * CH:(c + 1) * CH] for h in range(HG)] for c in range(NCH)]
                    else:
                        pe.wait_ge(fac_ready, (LEVELS + 2) * q + i)
                        lhs = rhs = [[fac[:, (i - 1) % 2, h, c * CH:(c + 1) * CH] for h in range(HG)] for c in range(NCH)]
                        if i == 1:
                            pe.wait_ge(o8_taken, q + 1)
                        else:
                            pe.wait_ge(sc_taken, SETS * q + i - 1)
                    for c in range(NCH):
                        for h in range(HG):
                            last = nc.tensor.matmul(pm[:, 2 * (i % 2) + c, h * CH:(h + 1) * CH], lhs[c][h], rhs[c][h],
                                                    start=True, stop=True)
                    last.then_inc(sc_psum, 1)
                    filler(level_slots, i)
                pe.wait_ge(fac_ready, (LEVELS + 2) * q + LEVELS + 1)
                pe.wait_ge(sc_taken, SETS * q + SETS - 1)
                for c in range(NCH):
                    for h in range(HG):
                        last = turn(pm[:, c, h * P:(h + 1) * P], fac[:, 1, h, c * CH:(c + 1) * CH], P)
                last.then_inc(kd_psum, 1)
                pe.wait_ge(kd_ready, q + 1)
                pe.wait_ge(sc_taken, SETS * (q + 1))
                for h in range(HG):
                    o = h * dv
                    last = nc.tensor.matmul(pm[:, 2 + o // 512, o % 512:o % 512 + dv], kdT[:, 0, h * DK:(h + 1) * DK],
                                            vt[:, 0, o:o + dv], start=True, stop=True)
                last.then_inc(s1_psum, 1)
                for h in range(HG):
                    o = h * dv
                    last = nc.tensor.matmul(pm[:, o // 512, o % 512:o % 512 + dv], kdT[:, 1, h * DK:(h + 1) * DK],
                                            vt[:, 1, o:o + dv], start=True, stop=True)
                last.then_inc(kv1_psum, 1)
                pe.wait_ge(s1_ready, q + 1)
                pe.wait_ge(fac_ready, (LEVELS + 2) * (q + 1))
                for jj in range(nv // 2):
                    b0 = 2 if jj % 2 == 0 else 0
                    if jj == 1:
                        pe.wait_ge(s2_ready, q + 1)
                    if jj >= 2:
                        pe.wait_ge(o_ready, OPAIRS[q] + jj - 1)
                    for m in range(2):
                        j = 2 * jj + m
                        h = j * P // dv
                        nc.tensor.matmul(pm[:, b0 + m, 0:CH], vt[:, 0, j * P:(j + 1) * P], scores[:, 0, h, :], start=True, stop=True)
                        nc.tensor.matmul(pm[:, b0 + m, CH:TP], vt[:, 1, j * P:(j + 1) * P], scores[:, 1, h, :], start=True, stop=False)
                        last = nc.tensor.matmul(pm[:, b0 + m, CH:TP], s1[:, j * P:(j + 1) * P], fac[:, 0, h, 0:CH], start=False, stop=True)
                    last.then_inc(o_psum, 1)

            recurrence(0, "ada0b", 0, range(8), range(8))
            pe.wait_ge(past_taken, 1)
            pe.wait_ge(o_ready, OPAIRS[1])
            for g in range(4):
                pe.wait_ge(pool_d, g + 1)
                if g >= 2:
                    pe.wait_ge(pool_taken, g - 1)
                for e in range(2):
                    for c in range(2):
                        last = nc.tensor.matmul(pm[:, 2 * (g % 2) + e, 0:T], pool_w[:, g, c, e * P:(e + 1) * P],
                                                z[:, 32 + 2 * g + c, :], start=(c == 0), stop=(c == 1))
                last.then_inc(pool_psum, 1)
            pe.wait_ge(pool_taken, 4)
            pe.wait_ge(osq_ready, 1)
            for h in range(HG):
                for m in range(2):
                    last = nc.tensor.matmul(pm[:, h, 0:T], ones[:, :], z[:, 2 * h + m, :], start=(m == 0), stop=(m == 1))
            last.then_inc(oss_psum, 1)

            def mix_wait(n):
                return lambda u: pe.wait_ge(mix_ready, 4 * n + (3 if u == 0 else 4))

            pe.wait_ge(mod_ready, PLAN["ada1u0"][3])
            gemm(8, PLAN["out0"][2], h_hi, h_lo, mix_wait(0), norm=8)

            def mlp_layer(l, hw, norms):
                _, _, g0, a0 = PLAN["ada1u0" if l == 0 else "up1_0"]

                def chunk(f, norm):
                    g, a = g0 + CHUNK_GROUPS[l] * f, a0 + 4 * f
                    for b in range(2):
                        if l == 0:
                            ada_pair(a + 2 * b, g)
                            g = g + 2

                        def ready(u):
                            if l == 0 and u == 0:
                                pe.wait_ge(mod_ready, a + (2 * b + 2))
                            if b == 0:
                                hw(u)
                            else:
                                pe.wait_ge(hid_ready, 8 * (FF_CHUNKS * l + f) + 2 * (u + 1))

                        if b == 0:
                            gemm(8, g, h_hi, h_lo, ready)
                        else:
                            gemm(8, g, f_hi, f_lo, ready, norm=norm)
                        g = g + 8

                with pe.Fori(0, FF_CHUNKS - 1) as f:
                    chunk(f, None)
                chunk(FF_CHUNKS - 1, norms)

            mlp_layer(0, h_wait(1), 16)
            pe.wait_ge(rstd_ready, 3)
            pe.wait_ge(aw_in, 64)
            for j in range(8):
                last = turn(pm[:, 0, j * TAPS:(j + 1) * TAPS], cw_rows[:, j * P:(j + 1) * P], TAPS)
            last.then_inc(cw_psum, 1)
            gemm(8, PLAN["glu"][2], h_hi, h_lo, h_wait(2))
            gemm(16, PLAN["in1"][2], h_hi, h_lo, h_wait(2))
            pe.wait_ge(conv_step, 1)
            for j in range(8):
                last = turn(pm[0:CONV_TAIL, 2 + j // 4, (j % 4) * P:(j % 4 + 1) * P],
                            z[:, 32 + j, T - CONV_TAIL:T], P)
            last.then_inc(tail_psum, 1)
            pe.wait_ge(past_in, 32)
            for j in range(8):
                if j >= 2:
                    pe.wait_ge(past_taken, j)
                for a in range(2):
                    last = turn(pm[:, j % 2, a * 120:(a + 1) * 120], pastc[:, a, j * P:(j + 1) * P], 120)
                last.then_inc(past_psum, 1)
            pe.wait_ge(cv_done, 8)
            for j in range(8):
                last = nc.tensor.matmul(pm[:, 0, 0:T], ones[:, :], z[:, 40 + j, :], start=(j == 0), stop=(j == 7))
            last.then_inc(ln_psum, 1)
            pe.wait_ge(ln_sq, 1)
            for j in range(8):
                last = nc.tensor.matmul(pm[:, 1, 0:T], ones[:, :], z[:, 32 + j, :], start=(j == 0), stop=(j == 7))
            last.then_inc(ln_psum, 1)
            pe.wait_ge(ln_rstd, 1)
            pe.wait_ge(tail_ready, 2)
            recurrence(1, "ada1b", 0, range(0, 8, 2), range(0, 8, 2))
            pe.wait_ge(o_ready, OPAIRS[2])
            recurrence(2, "ada1b", 8, range(0, 8, 2), range(0, 8, 2))
            pe.wait_ge(o_ready, OPAIRS[3])
            pe.wait_ge(osq_ready, 2)
            for r in range(2):
                if r:
                    pe.wait_ge(ors_ready, 2)
                for h in range(4):
                    last = nc.tensor.matmul(pm[:, h, 0:T], ones[:, :], z[:, 4 * r + h, :], start=True, stop=True)
                last.then_inc(oss_psum, 1)
            pe.wait_ge(mod_ready, 96)
            gemm(8, PLAN["out1"][2], h_hi, h_lo, mix_wait(1), norm=24)
            mlp_layer(1, h_wait(3), 32)
            for r in range(3):
                for b in range(4):
                    i = 4 * r + b
                    if r == 0:
                        pe.wait_ge(y_ready, 4 * b + 4)
                    if i >= 4:
                        pe.wait_ge(y_taken, i - 3)
                    for m in range(4):
                        k = 4 * b + m
                        if r < 2:
                            last = turn(pm[:, b, m * P:(m + 1) * P], x[:, k, r * P:(r + 1) * P], P)
                        else:
                            last = turn(pm[0:NS, b, m * P:(m + 1) * P], x[:, k, TP:T], P)
                    last.then_inc(y_psum, 1)

        @block.scalar
        def _(act):
            steps = Count()

            def step(ins):
                ins.then_inc(act_step, 1)
                act.wait_ge(act_step, steps.next())

            def hi(g, u, p):
                if u % 2 == 0:
                    act.wait_ge(raw_in[p][u // 2], 8 * (g - p) + 16)
                if not isinstance(g, int) or g:
                    act.wait_ge(split_used, NU * g + u - (NU - 1))
                nc.scalar.activation(w_hi[:, u, :], raw[:, p, u, :], ACT.Copy).then_inc(hi_ready, 1)

            def hi_phase(count, g, after=None, last_next=None, middle=None):
                def body(i, p, nxt=True):
                    hi(g + i, 2, p)
                    hi(g + i, 3, p)
                    if nxt:
                        hi(g + i + 1, 0, 1 - p)
                        hi(g + i + 1, 1, 1 - p)
                    if after:
                        after(i, p)

                with act.Fori(0, count // 2 - 1) as j:
                    for p in range(2):
                        body(2 * j + p, p)
                body(count - 2, 0)
                body(count - 1, 1, nxt=False)
                if middle:
                    middle()
                if last_next is not None:
                    hi(last_next, 0, 0)
                    hi(last_next, 1, 0)

            def hi_ada(g, p):
                for u in range(NU):
                    hi(g, u, p)

            def square(norm, x0):
                def f(i, p):
                    act.wait_ge(x_ready, x0 + i + 1)
                    act.wait_ge(ss_done, norm + i - 1)
                    k = 2 * i
                    nc.scalar.activation(sq[:, p, :, :], x[:, bass.ds(k, 2), :], ACT.Square).then_inc(sq_ready, 1)
                return f

            def rms(r, sums, tail_only=False):
                act.wait_ge(ss_done, sums)
                step(nc.scalar.activation(lnv[:, :], pm[:, 0, 0:T], ACT.Ln, bias=eps_t[:, :], scale=1.0 / D))
                nc.scalar.activation(rstd[:, :], lnv[:, :], ACT.Exp, scale=-0.5).then_inc(rstd_ready, 1)

            def modulate(r, l, sh):
                act.wait_ge(t8_ready, r + 1)
                nc.scalar.activation(h_hi[:, :, TP:T], t8[:, :, :], ACT.Copy).then_inc(h8_hi, 1)
                for k in range(KT):
                    act.wait_ge(hs_ready, KT * r + k + 1)
                    nc.scalar.activation(h_hi[:, k, 0:TP], hs[:, k % 4, :], ACT.Identity,
                                         bias=mod[:, l, sh + k, 0:1]).then_inc(hh_ready, 1)

            act.dma_start(ident[:, :], io["ident"]).then_inc(const_in, 16)
            for name, row in VA.items():
                src = io[name]
                n = 16 if name == "norm_final" else 32
                src = src.rearrange("(k p) -> k p", p=P) if name == "norm_final" else src.rearrange("l (k p) -> (l k) p", p=P)
                act.dma_start(va_rows[row:row + n, :], src).then_inc(const_in, 16)
            for name, row in VB.items():
                src = io[name].rearrange("l (k p) -> (l k) p", p=P)
                act.dma_start(vb_rows[row:row + src.shape[0], :], src).then_inc(const_in, 16)
            act.dma_start(ba_rows[:, :, :], io["b_ada"].rearrange("l (m p) -> m l p", p=P)).then_inc(const_in, 16)
            act.dma_start(mask_rows[:, :, :], io["masks"].rearrange("p (l t) -> p l t", l=LEVELS)).then_inc(const_in, 16)
            act.dma_start(inv_count[:, :, :], io["inv_count"].rearrange("p (g t) -> p g t", t=16)).then_inc(const_in, 16)

            act.wait_ge(rows_in, 64)
            nc.scalar.activation(cs_rows[:, :], c_rows[:, :], ACT.Silu).then_inc(c_silu, 1)
            act.preload_act_table_set("natural_log_exp_and_others")
            act.wait_ge(tr_ready, 2)
            nc.scalar.activation(c_hl[:, 0:KT * CW].rearrange("p (k n) -> p k n", n=CW)[:, :, 0:NC],
                                 pm[:, 1, 0:KT * NC].rearrange("p (k n) -> p k n", n=NC), ACT.Copy).then_inc(c_high, 1)
            for i in range(KT // 2):
                act.wait_ge(tr_taken, 2 + 2 * i + 2)
                if i >= 2:
                    act.wait_ge(ss_done, i - 1)
                nc.scalar.activation(sq[:, i % 2, :, :], x[:, 2 * i:2 * i + 2, :], ACT.Square).then_inc(sq_ready, 1)
            rms(0, 8)
            act.wait_ge(filled, 2)
            nc.scalar.activation(sm[:, :], lb[:, :], ACT.Exp).then_inc(lb_exp, 1)
            for p in range(2):
                hi_ada(p, p)
            with act.Fori(0, PLAN["ada0a"][1] // 2 - 1) as j:
                for p in range(2):
                    hi_ada(2 * j + (2 + p), p)
            g0 = PLAN["in0"][2]
            hi(g0, 0, 0)
            hi(g0, 1, 0)
            modulate(0, 0, SH1)
            hi_phase(16, g0)
            act.wait_ge(aw_in, 48)
            act.wait_ge(filled, 3)
            nc.scalar.activation(a_hi[:, 0:KT * 16], a_w[:, :, :].rearrange("p k n -> p (k n)"), ACT.Copy).then_inc(aw_hi, 1)
            act.wait_ge(gz_ready, 2)
            step(nc.scalar.activation(gl[:, :, :], gl[:, :, :], ACT.Exp))
            nc.scalar.activation(gl[:, :, :], gl[:, :, :], ACT.Ln, bias=1.0).then_inc(gl_ready, 1)
            act.wait_ge(evacuated, g0 + 16)
            nc.scalar.activation(z[:, 0:4, :], z[:, 0:4, :], ACT.Copy, scale=float(DK) ** -0.5).then_inc(q_scaled, 1)
            act.wait_ge(tail_psum, 1)
            nc.scalar.activation(tail[0:POOL_TAIL, :].rearrange("p (a n) -> p a n", a=2), pm[0:POOL_TAIL, 2:4, :],
                                 ACT.Copy).then_inc(tail_ready, 1)

            def recurrence(q, ada_name, ada_first, sample_slots, level_slots):
                hd = HEADS[q]
                fill = [ada_first]

                def filler(slots, s):
                    if s in slots:
                        for p in range(2):
                            hi_ada(PLAN[ada_name][2] + 2 * fill[0] + p, p)
                        fill[0] += 1

                nv, dv, zq, zk, zv = hd["nv"], hd["dv"], hd["q"], hd["k"], hd["v"]
                vt = vT[hd["layer"]]
                nb = nv // 4
                act.wait_ge(logp_ready, q + 1)
                nc.scalar.activation(decay8[:, :, :], logp[:, :, TP:T], ACT.Exp).then_inc(dec8_ready, 1)
                for c in range(NCH):
                    act.wait_ge(vtr_psum, 4 * q + c + 1)
                    nc.scalar.activation(vt[:, c, 0:nv * P].rearrange("p (a n) -> p a n", n=512),
                                         pm[:, c * nb:(c + 1) * nb, :], ACT.Copy).then_inc(vtr_ready, 1)
                act.wait_ge(vtr_psum, 4 * q + 3)
                nc.scalar.activation(v8[:, 0:nv * P].rearrange("p (a n) -> p a n", n=512), pm[0:NS, 0:nb, :],
                                     ACT.Copy).then_inc(vtr_ready, 1)
                act.wait_ge(vtr_psum, 4 * q + 4)
                nc.scalar.activation(k8[:, :], pm[0:NS, 2, :], ACT.Copy).then_inc(vtr_ready, 1)
                act.wait_ge(vtr_ready, 4 * q + 4)
                for b in range(NS):
                    if b >= 2:
                        act.wait_ge(kv_psum, NS * q + b - 1)
                    nc.scalar.activation(kmask[:, b % 2, :], k8[:, :], ACT.Copy,
                                         scale=ident[0:NS, b:b + 1]).then_inc(kmask_ready, 1)
                    if b:
                        filler(sample_slots, b - 1)
                filler(sample_slots, NS - 1)
                for lv in range(LEVELS):
                    w = 1 << lv
                    act.wait_ge(dif_ready, (LEVELS + 1) * q + lv + 1)
                    dl, dr = halves(dec[:, lv % 2, :, :], w)
                    _, pr = halves(logp[:, :, 0:TP], w)
                    nc.scalar.activation(dr, pr, ACT.Exp)
                    nc.scalar.activation(dl, dl, ACT.Exp).then_inc(exp_ready, 1)
                    filler(level_slots, lv)
                act.wait_ge(dif_ready, (LEVELS + 1) * (q + 1))
                nc.scalar.activation(dec[:, 1, :, :], dec[:, 1, :, :], ACT.Exp).then_inc(exp_ready, 1)
                filler(level_slots, LEVELS)
                act.wait_ge(fac_ready, (LEVELS + 2) * q + LEVELS)
                nc.scalar.activation(dec[:, 0, :, 0:CH], logp[:, :, CH:TP], ACT.Exp).then_inc(exp_ready, 1)
                act.wait_ge(kd_psum, q + 1)
                nc.scalar.activation(kdT[:, :, :], pm[:, 0:2, :], ACT.Copy).then_inc(kd_ready, 1)
                act.wait_ge(s1_psum, q + 1)
                nc.scalar.activation(s1[:, 0:nv * P].rearrange("p (a n) -> p a n", n=512), pm[:, 2:2 + nb, :],
                                     ACT.Copy).then_inc(s1_ready, 1)
                for jj in range(nv // 2):
                    b0 = 2 if jj % 2 == 0 else 0
                    act.wait_ge(o_psum, OPAIRS[q] + jj + 1)
                    nc.scalar.activation(z[:, zv + 2 * jj:zv + 2 * jj + 2, 0:TP], pm[:, b0:b0 + 2, 0:TP],
                                         ACT.Copy).then_inc(o_ready, 1)

            def mix_high(n, batches):
                for i, (dst, src) in enumerate(batches):
                    if i >= 2:
                        act.wait_ge(mix_f32, n + i - 1)
                    nc.scalar.activation(h_hi[:, dst:dst + 4, :], z[:, src:src + 4, :], ACT.Copy).then_inc(mix_hi, 1)

            recurrence(0, "ada0b", 0, range(8), range(8))
            for g in range(4):
                act.wait_ge(pool_psum, g + 1)
                for e in range(2):
                    j = 2 * g + e
                    last = nc.scalar.activation(z[:, 40 + j, :], pm[:, 2 * (g % 2) + e, 0:T], ACT.Copy,
                                                scale=vb[:, VB["ev_pool_scale"] + j:VB["ev_pool_scale"] + j + 1])
                last.then_inc(pool_taken, 1)
            act.wait_ge(o_ready, OPAIRS[1])
            act.wait_ge(o8_taken, 1)
            nc.scalar.activation(z[:, 0:8, :], z[:, 8:16, :], ACT.Square).then_inc(osq_ready, 1)
            act.wait_ge(oss_psum, 1)
            act.wait_ge(o_ready, OPAIRS[1])
            step(nc.scalar.activation(logp[:, :, :], pm[:, :, 0:T], ACT.Ln, bias=eps_t[:, :], scale=1.0 / 256))
            nc.scalar.activation(logp[:, :, :], logp[:, :, :], ACT.Exp, scale=-0.5).then_inc(ors_ready, 1)
            nc.scalar.activation(z[:, 16:24, :], z[:, 16:24, :], ACT.Silu).then_inc(silu_ready, 1)
            act.preload_act_table_set("natural_log_exp_and_others")
            act.wait_ge(pool_taken, 4)
            act.wait_ge(s2_ready, 1)
            act.wait_ge(small_out, 16 * 5)
            mix_high(0, [(8, 40), (12, 44), (0, 8), (4, 12)])
            g1 = PLAN["out0"][2]
            hi(g1, 0, 0)
            hi(g1, 1, 0)
            hi_phase(8, g1, after=square(8, 0))
            rms(1, 16)
            modulate(1, 0, SH2)

            def mlp_layer(l, norm, x0):
                g0 = PLAN["ada1u0" if l == 0 else "up1_0"][2]
                lead = 2 if l == 0 else 0

                def ada(g):
                    return (lambda: (hi_ada(g, 0), hi_ada(g + 1, 1))) if l == 0 else None

                def chunk(f, after, next_up):
                    g = g0 + CHUNK_GROUPS[l] * f + lead
                    hi_phase(8, g, middle=ada(g + 8), last_next=g + 8 + lead)
                    g = g + 8 + lead
                    hi_phase(8, g, after=after, middle=ada(g + 8) if next_up else None,
                             last_next=g + 8 + lead if next_up else None)

                if l == 0:
                    ada(g0)()
                hi(g0 + lead, 0, 0)
                hi(g0 + lead, 1, 0)
                with act.Fori(0, FF_CHUNKS - 1) as f:
                    chunk(f, None, True)
                chunk(FF_CHUNKS - 1, square(norm, x0), False)

            mlp_layer(0, 16, 32)
            rms(2, 24)
            g2 = PLAN["glu"][2]
            hi(g2, 0, 0)
            hi(g2, 1, 0)
            modulate(2, 1, SH1)
            hi_phase(8, g2, last_next=g2 + 8)
            act.wait_ge(evacuated, g2 + 8)
            nc.scalar.activation(z[:, 40:48, :], z[:, 40:48, :], ACT.Sigmoid).then_inc(gb_sig, 1)
            act.preload_act_table_set("natural_log_exp_and_others")
            g3 = PLAN["in1"][2]
            hi_phase(16, g3)
            act.wait_ge(tail_psum, 2)
            nc.scalar.activation(tail[0:CONV_TAIL, :].rearrange("p (a n) -> p a n", a=2), pm[0:CONV_TAIL, 2:4, :],
                                 ACT.Copy).then_inc(tail_ready, 1)
            act.wait_ge(ln_psum, 1)
            nc.scalar.activation(mean[:, :], pm[:, 0, 0:T], ACT.Copy, scale=1.0 / 1024).then_inc(ln_mean, 1)
            act.wait_ge(ln_cent, 1)
            act.wait_ge(tail_psum, 2)
            nc.scalar.activation(z[:, 32:40, :], z[:, 40:48, :], ACT.Square).then_inc(ln_sq, 1)
            act.wait_ge(ln_psum, 2)
            step(nc.scalar.activation(lnv[:, :], pm[:, 1, 0:T], ACT.Ln, bias=eps_t[:, :], scale=1.0 / 1024))
            nc.scalar.activation(rstd[:, :], lnv[:, :], ACT.Exp, scale=-0.5).then_inc(ln_rstd, 1)
            act.wait_ge(ln_done, 1)
            nc.scalar.activation(z[:, 40:48, :], z[:, 40:48, :], ACT.Silu).then_inc(cv_ready, 1)
            act.wait_ge(evacuated, g3 + 16)
            nc.scalar.activation(z[:, 24:32, :], z[:, 24:32, :], ACT.Silu).then_inc(silu_ready, 1)
            for q in (1, 2):
                zk = HEADS[q]["k"]
                if q == 2:
                    act.wait_ge(dec8_ready, 2)
                    act.wait_ge(exp_ready, (LEVELS + 2) * 2)
                    act.wait_ge(s2_ready, 2)
                nc.scalar.activation(logp[:, :, :], z[:, zk:zk + 4, :], ACT.Sigmoid)
                nc.scalar.activation(z[:, zk:zk + 4, :], z[:, zk:zk + 4, :], ACT.Sigmoid, scale=-1.0).then_inc(sig_ready, 1)
                act.preload_act_table_set("natural_log_exp_and_others")
                act.wait_ge(ln_in, q)
                nc.scalar.activation(gz[:, :, :], gz[:, :, :], ACT.Ln)
                nc.scalar.activation(logp[:, :, :], logp[:, :, :], ACT.Ln).then_inc(ln_out, 1)
                recurrence(q, "ada1b", 8 * (q - 1), range(0, 8, 2), range(0, 8, 2))
            act.wait_ge(o_ready, OPAIRS[3])
            act.wait_ge(o8_taken, 3)
            nc.scalar.activation(z[:, 0:8, :], z[:, 16:24, :], ACT.Square).then_inc(osq_ready, 1)
            for r in range(2):
                act.wait_ge(oss_psum, 2 + r)
                rs = z[:, 8 + 4 * r:12 + 4 * r, :]
                step(nc.scalar.activation(rs, pm[:, :, 0:T], ACT.Ln, bias=eps_t[:, :], scale=1.0 / 128))
                nc.scalar.activation(rs, rs, ACT.Exp, scale=-0.5).then_inc(ors_ready, 1)
            act.wait_ge(cv_ready, 1)
            act.wait_ge(s2_ready, 3)
            act.wait_ge(small_out, 16 * SMALL_OUTS)
            mix_high(2, [(8, 40), (12, 44), (0, 16), (4, 20)])
            g4 = PLAN["out1"][2]
            hi(g4, 0, 0)
            hi(g4, 1, 0)
            hi_phase(8, g4, after=square(24, 40))
            rms(3, 32)
            modulate(3, 1, SH2)
            mlp_layer(1, 32, 72)
            rms(4, 40)
            for r in range(3):
                for b in range(4):
                    act.wait_ge(y_psum, 4 * r + b + 1)
                    rows, dst = (P, y_rows[:, r, b * 512:(b + 1) * 512]) if r < 2 else (NS, ys_rows[:, b * 512:(b + 1) * 512])
                    nc.scalar.activation(dst, pm[0:rows, b, :], ACT.Copy).then_inc(y_taken, 1)

        @block.vector
        def _(dve):
            steps = Count()

            def step(ins):
                ins.then_inc(dve_step, 1)
                dve.wait_ge(dve_step, steps.next())

            def lo(n, u, p):
                dve.wait_ge(hi_ready, NU * n + (u + 1))
                nc.vector.tensor_tensor(w_lo[:, u, :], raw[:, p, u, :], w_hi[:, u, :].bitcast(F32),
                                        ALU.subtract).then_inc(lo_ready, 1)

            def lo_phase(count, n, evac, last_next=None, middle=None, loop_work=None):
                def body(i, p, nxt, wrk=None):
                    lo(n + i, 2, p)
                    if wrk:
                        wrk(0)
                    lo(n + i, 3, p)
                    if wrk:
                        wrk(1)
                    if nxt is not None:
                        lo(nxt, 0, 1 - p)
                        if wrk:
                            wrk(2)
                        lo(nxt, 1, 1 - p)
                        if wrk:
                            wrk(3)
                    evac(i, p)

                with dve.Fori(0, count // 2 - 1) as j:
                    for p in range(2):
                        i = 2 * j + p
                        body(i, p, n + i + 1, (lambda s, p=p: loop_work(j, 4 * p + s)) if loop_work else None)
                i = count - 2
                j = count // 2 - 1
                body(i, 0, n + i + 1, (lambda s: loop_work(j, s)) if loop_work else None)
                wrk = (lambda s: loop_work(j, 4 + s)) if loop_work else None
                if last_next is not None and middle is None:
                    body(i + 1, 1, last_next, wrk)
                else:
                    body(i + 1, 1, None, wrk)
                    if wrk:
                        wrk(2)
                        wrk(3)
                    if middle:
                        middle()
                    if last_next is not None:
                        lo(last_next, 0, 0)
                        lo(last_next, 1, 0)

            def ada_rows(g, p):
                dve.wait_ge(split_used, NU * g + NU)
                nc.vector.tensor_copy(mod_rows[:, p, :], ps[0:CW, MT * p, 0:GC]).then_inc(evacuated, 1)

            def ada_add(a, p):
                dve.wait_ge(turned, a + 1)
                nc.vector.tensor_tensor(modf[:, bass.ds(2 * a, 2), :],
                                        ps[:, MT * p + 1, 0:MT * NC].rearrange("p (m n) -> p m n", n=NC),
                                        badaf[:, bass.ds(2 * a, 2)].unsqueeze(2).broadcast_to([P, 2, NC]),
                                        ALU.add).then_inc(mod_ready, 1)

            def ada_group(a, g, p, with_last=True):
                for u in range(2):
                    lo(g, u, p)
                if with_last:
                    ada_rows(g - 1, 1 - p)
                for u in range(2, NU):
                    lo(g, u, p)
                if with_last:
                    ada_add(a - 1, 1 - p)

            def ada_end(a, g):
                ada_rows(g - 1, 1)
                ada_add(a - 1, 1)

            modf = mod[:, :, :, :].rearrange("p l m n -> p (l m) n")
            badaf = bada[:, :, :].rearrange("p l m -> p (l m)")

            def z_evac(n, z0):
                def f(i, p):
                    dve.wait_ge(split_used, NU * (n + i) + NU)
                    off = (z0 + 2 * i) * T
                    nc.vector.tensor_copy(zf[:, bass.ds(off, MT * T)].rearrange("p (a t) -> p a t", a=MT),
                                          bank2(p)).then_inc(evacuated, 1)
                return f

            def up_evac(n, g, h):
                def f(i, p):
                    dve.wait_ge(split_used, NU * (n + i) + NU)
                    nc.vector.tensor_scalar(hid[:, :, :], bank2(p), 0.0, None, ALU.max).then_inc(evacuated, 1)
                    dve.wait_ge(evacuated, g + i + 1)
                    nc.vector.tensor_tensor(hid[:, :, :], hid[:, :, :], hid[:, :, :], ALU.mult).then_inc(hid_sq, 1)
                    dve.wait_ge(hid_sq, h + i + 1)
                    k = 2 * i
                    nc.vector.tensor_copy(f_hi[:, bass.ds(k, 2), :], hid[:, :, :]).then_inc(hid_hi, 1)
                    dve.wait_ge(hid_hi, h + i + 1)
                    nc.vector.tensor_tensor(f_lo[:, bass.ds(k, 2), :], hid[:, :, :],
                                            f_hi[:, bass.ds(k, 2), :].bitcast(F32), ALU.subtract).then_inc(hid_ready, 1)
                return f

            def res_evac(n, r, l, gate):
                def f(i, p):
                    dve.wait_ge(split_used, NU * (n + i) + NU)
                    k = 2 * i
                    nc.vector.tensor_tensor(g8[:, :, :], bank2(p)[:, :, TP:T], mod[:, l, bass.ds(gate + k, 2), 1:NC],
                                            ALU.mult).then_inc(gate8_done, 1)
                    for m in range(MT):
                        xa = x[:, bass.ds(k + m, 1), 0:TP].rearrange("p a t -> p (a t)")
                        ga = mod[:, l, bass.ds(gate + k + m, 1), 0:1].rearrange("p a t -> p (a t)")
                        last = nc.vector.scalar_tensor_tensor(xa, ps[:, MT * p + m, 0:TP], ga, xa, ALU.mult, ALU.add)
                    last.then_inc(evacuated, 1)
                    dve.wait_ge(gate8_done, r + i + 1)
                    x8 = x[:, bass.ds(k, 2), TP:T]
                    nc.vector.tensor_tensor(x8, x8, g8[:, :, :], ALU.add).then_inc(x_ready, 1)
                return f

            def gains(l, norm0, sc):
                step(nc.vector.scalar_tensor_tensor(
                    amod[:, :, :], mod[:, l, sc:sc + KT, :], 1.0,
                    va[:, norm0:norm0 + KT].unsqueeze(2).broadcast_to([P, KT, NC]), ALU.add, ALU.mult))

            def modulate(r, l, sh):
                dve.wait_ge(rstd_ready, r + 1)
                step(nc.vector.tensor_tensor(t8[:, :, :], x[:, :, TP:T], amod[:, :, 1:NC], ALU.mult))
                step(nc.vector.tensor_tensor(t8[:, :, :], t8[:, :, :],
                                             rstd[:, TP:T].unsqueeze(1).broadcast_to([P, KT, NS]), ALU.mult))
                nc.vector.tensor_tensor(t8[:, :, :], t8[:, :, :], mod[:, l, sh:sh + KT, 1:NC], ALU.add).then_inc(t8_ready, 1)

                def scale(k):
                    nc.vector.scalar_tensor_tensor(hs[:, k % 4, :], x[:, k, 0:TP], amod[:, k, 0:1], rstd[:, 0:TP],
                                                   ALU.mult, ALU.mult).then_inc(hs_ready, 1)

                def low(k):
                    dve.wait_ge(hh_ready, KT * r + k + 1)
                    nc.vector.scalar_tensor_tensor(h_lo[:, k, 0:TP], hs[:, k % 4, :], mod[:, l, sh + k, 0:1],
                                                   h_hi[:, k, 0:TP].bitcast(F32), ALU.add, ALU.subtract).then_inc(h_ready, 1)

                for k in range(3):
                    scale(k)
                dve.wait_ge(h8_hi, r + 1)
                nc.vector.tensor_tensor(h_lo[:, :, TP:T], t8[:, :, :], h_hi[:, :, TP:T].bitcast(F32), ALU.subtract)
                for k in range(KT):
                    low(k)
                    if k + 3 < KT:
                        if k:
                            dve.wait_ge(h_ready, KT * r + k)
                        scale(k + 3)

            nc.vector.memset(ones[:, :], 1.0)
            nc.vector.memset(zero[:, :], 0.0)
            nc.vector.memset(c_hl[:, KT * CW:].bitcast(F32), 0.0)
            nc.vector.memset(eps_t[:, :], EPS).then_inc(filled, 1)
            dve.wait_ge(tr_ready, 1)
            nc.vector.tensor_copy(va[:, :], pm[:, 0, 0:80])
            nc.vector.tensor_copy(vb[:, :], pm[:, 0, 80:80 + VB_ROWS])
            nc.vector.tensor_copy(bada[:, :, :], pm[:, 0, 128:320].rearrange("p (l m) -> p l m", l=2)).then_inc(tr_taken, 1)
            dve.wait_ge(c_high, 1)
            c_parts = c_hl[:, 0:KT * CW].rearrange("p (k n) -> p k n", n=CW)
            nc.vector.tensor_tensor(c_parts[:, :, NC:CW], pm[:, 1, 0:KT * NC].rearrange("p (k n) -> p k n", n=NC),
                                    c_parts[:, :, 0:NC].bitcast(F32), ALU.subtract).then_inc(tr_taken, 1)
            nc.vector.tensor_tensor(sel[:, :], ident[0:CW, 0:NC], ident[0:CW, NC:CW], ALU.add)
            nc.vector.tensor_copy(masks[:, :, :], mask_rows[:, :, :])
            for k in range(KT):
                dve.wait_ge(tr_ready, 3 + k)
                nc.vector.tensor_copy(x[:, k, :], pm[:, (2 + k) % 4, 0:T]).then_inc(tr_taken, 1)
            dve.wait_ge(tr_taken, START_BANKS)
            raw_lb = vb[:, VB["od_lb_raw"]:VB["od_lb_raw"] + 8]
            nc.vector.tensor_tensor(lb[:, :], raw_lb, raw_lb, ALU.subtract).then_inc(filled, 1)
            dve.wait_ge(lb_exp, 1)
            step(nc.vector.reciprocal(oml[:, :], sm[:, :]))
            step(nc.vector.tensor_tensor(sm[:, :], sm[:, :], oml[:, :], ALU.mult))
            step(nc.vector.tensor_tensor(lb[:, :], sm[:, :], sm[:, :], ALU.subtract))
            step(nc.vector.tensor_scalar(oml[:, :], lb[:, :], -1.0, 1.0, ALU.mult, ALU.add))
            dve.wait_ge(ss_done, 8)
            count = PLAN["ada0a"][1]
            ada_group(0, 0, 0, with_last=False)
            ada_group(1, 1, 1)
            with dve.Fori(0, count // 2 - 1) as j:
                for p in range(2):
                    ada_group(2 * j + (2 + p), 2 * j + (2 + p), p)
            ada_end(count, count)
            dve.wait_ge(mod_ready, count)
            gains(0, VA["norm_mix"], SC1)
            n0 = PLAN["in0"][2]
            lo(n0, 0, 0)
            lo(n0, 1, 0)
            modulate(0, 0, SH1)
            lo_phase(16, n0, z_evac(n0, 0))
            nc.vector.memset(a_hi[:, KT * 16:AW].bitcast(F32), 0.0)
            nc.vector.memset(a_lo[:, KT * 16:AW].bitcast(F32), 0.0).then_inc(filled, 1)
            dve.wait_ge(aw_hi, 1)
            nc.vector.tensor_tensor(a_lo[:, 0:KT * 16], a_w[:, :, :].rearrange("p k n -> p (k n)"),
                                    a_hi[:, 0:KT * 16].bitcast(F32), ALU.subtract).then_inc(aw_lo, 1)
            dve.wait_ge(alr_psum, 1)
            nc.vector.tensor_copy(a_lr[:, :], pm[0:16, 0, 0:T]).then_inc(alr_ready, 1)
            dve.wait_ge(gate_psum, 1)
            b0 = VB["ev_b_gate"]
            for h in range(HG):
                last = nc.vector.tensor_scalar(gz[:, h, :], pm[:, h, 0:T], vb[:, b0 + h:b0 + h + 1], None, ALU.add)
            last.then_inc(gz_ready, 1)
            dve.wait_ge(gz_ready, 1)
            gzf = gz[:, :, :].rearrange("p h t -> p (h t)")
            glf = gl[:, :, :].rearrange("p h t -> p (h t)")
            lpf = logp[:, :, :].rearrange("p h t -> p (h t)")
            nc.vector.scalar_tensor_tensor(glf, gzf, -1.0, gzf, ALU.mult, ALU.min).then_inc(gz_ready, 1)
            dve.wait_ge(gl_ready, 1)
            step(nc.vector.scalar_tensor_tensor(lpf, gzf, 0.0, glf, ALU.min, ALU.subtract))
            nc.vector.tensor_scalar(lpf, lpf, 1.0 / 16.0, None, ALU.mult).then_inc(logp_ready, 1)
            dve.wait_ge(past_psum, 1)
            dve.wait_ge(evacuated, PLAN["in0"][2] + 16)
            for g, w in enumerate(WINDOWS):
                b = g // 2
                c0 = (g % 2) * 240
                past = pm[:, b, c0:c0 + 240].rearrange("p (j b r) -> p j b r", j=2, r=POOL_PAST)
                u8 = z[:, 24 + 2 * g:26 + 2 * g, TP:T]
                d8 = z[:, 32 + 2 * g:34 + 2 * g, TP:T]
                step(nc.vector.tensor_reduce(wsum[:, :, :], past[:, :, :, POOL_PAST - w + 1:POOL_PAST], AX.X, ALU.add))
                step(nc.vector.tensor_tensor(wsum[:, :, :], wsum[:, :, :], u8, ALU.add))
                last = nc.vector.scalar_tensor_tensor(d8, wsum[:, :, :], 1.0 / w, u8, ALU.mult, ALU.subtract)
                if g < 3:
                    step(last)
            last.then_inc(past_taken, 1)

            def recurrence(q, ada_name, ada_first, sample_slots, level_slots):
                hd = HEADS[q]
                nv, dv, zq, zk, zv = hd["nv"], hd["dv"], hd["q"], hd["k"], hd["v"]
                fill = [ada_first]

                def filler(slots, s):
                    if s in slots:
                        _, count, g0, a0 = PLAN[ada_name]
                        j = fill[0]
                        ada_group(a0 + 2 * j, g0 + 2 * j, 0, with_last=j > 0)
                        ada_group(a0 + 2 * j + 1, g0 + 2 * j + 1, 1)
                        if 2 * j + 2 == count:
                            ada_end(a0 + count, g0 + count)
                        fill[0] += 1

                dve.wait_ge(dec8_ready, q + 1)
                for b in range(NS):
                    dve.wait_ge(kv_psum, NS * q + b + 1)
                    dve.wait_ge(st_in[b % 2], 16 * (4 * q + b // 2 + 1))
                    for h in range(HG):
                        o = h * dv
                        s_ = st[:, b % 2, o:o + dv]
                        last = nc.vector.scalar_tensor_tensor(s_, s_, decay8[:, h, b:b + 1],
                                                              pm[:, o // 512, o % 512:o % 512 + dv], ALU.mult, ALU.add)
                    last.then_inc(st_ready, 1)
                    filler(sample_slots, b)
                dve.wait_ge(o8_psum, NS * (q + 1))
                nc.vector.tensor_copy(z[:, zv:zv + nv, TP:T], pm[:, 3, 0:nv * NS].rearrange("p (j b) -> p j b", b=NS)).then_inc(o8_taken, 1)
                for i in range(2):
                    dve.wait_ge(st_out[i], 16 * 4 * (q + 1))

                def differ(lv):
                    w = 1 << lv
                    left, _ = halves(logp[:, :, 0:TP], w)
                    dl, _ = halves(dec[:, lv % 2, :, :], w)
                    mid = left[:, :, :, w - 1:w].broadcast_to([P, HG, TP // (2 * w), w])
                    nc.vector.tensor_tensor(dl, mid, left, ALU.subtract).then_inc(dif_ready, 1)

                def take(i):
                    dve.wait_ge(sc_psum, SETS * q + i + 1)
                    if i:
                        dve.wait_ge(sc_taken, SETS * q + i)
                    for c in range(NCH):
                        prod = pm[:, 2 * (i % 2) + c, :].rearrange("p (h t) -> p h t", h=HG)
                        if i == 0:
                            last = nc.vector.tensor_tensor(scores[:, c, :, :], prod,
                                                           ident[:, :].unsqueeze(1).broadcast_to([P, HG, CH]), ALU.mult)
                        else:
                            last = nc.vector.copy_predicated(scores[:, c, :, :],
                                                             masks[:, i - 1, :].unsqueeze(1).broadcast_to([P, HG, CH]), prod)
                    last.then_inc(sc_taken, 1)

                differ(0)
                take(0)
                filler(level_slots, 0)
                for lv in range(LEVELS):
                    w = 1 << lv
                    dve.wait_ge(exp_ready, (LEVELS + 2) * q + lv + 1)
                    dl, dr = halves(dec[:, lv % 2, :, :], w)
                    fl, fr = halves(fac[:, lv % 2, :, :], w)
                    ql, qr = halves(z[:, zq:zq + HG, 0:TP], w)
                    kl, kr = halves(z[:, zk:zk + HG, 0:TP], w)
                    left, right = halves(logp[:, :, 0:TP], w)
                    nc.vector.tensor_tensor(fl, kl, dl, ALU.mult)
                    nc.vector.tensor_tensor(fr, qr, dr, ALU.mult).then_inc(fac_ready, 1)
                    mid = left[:, :, :, w - 1:w].broadcast_to([P, HG, TP // (2 * w), w])
                    nc.vector.tensor_tensor(right, right, mid, ALU.add).then_inc(prefix_ready, 1)
                    dve.wait_ge(prefix_ready, LEVELS * q + lv + 1)
                    if lv + 1 < LEVELS:
                        differ(lv + 1)
                    else:
                        lp = logp[:, :, 0:TP].rearrange("p h (c t) -> p h c t", c=NCH)
                        end = lp[:, :, :, CH - 1:CH].broadcast_to([P, HG, NCH, CH])
                        nc.vector.tensor_tensor(dec[:, 1, :, :].rearrange("p h (c t) -> p h c t", c=NCH), end, lp,
                                                ALU.subtract).then_inc(dif_ready, 1)
                    if lv:
                        take(lv)
                        filler(level_slots, lv)
                dve.wait_ge(exp_ready, (LEVELS + 2) * q + LEVELS + 1)
                nc.vector.tensor_tensor(fac[:, 1, :, :], z[:, zk:zk + HG, 0:TP], dec[:, 1, :, :], ALU.mult).then_inc(fac_ready, 1)
                take(LEVELS)
                filler(level_slots, LEVELS)
                dve.wait_ge(exp_ready, (LEVELS + 2) * (q + 1))
                nc.vector.tensor_tensor(fac[:, 0, :, 0:CH], z[:, zq:zq + HG, CH:TP], dec[:, 0, :, 0:CH], ALU.mult).then_inc(fac_ready, 1)
                dve.wait_ge(kv1_psum, q + 1)
                dve.wait_ge(s1_ready, q + 1)
                if q == 2:
                    dve.wait_ge(small_out, 16 * (SMALL_OUTS - 1))
                for h in range(HG):
                    o = h * dv
                    last = nc.vector.scalar_tensor_tensor(s2[:, o:o + dv], s1[:, o:o + dv], dec[:, 0, h, CH - 1:CH],
                                                          pm[:, o // 512, o % 512:o % 512 + dv], ALU.mult, ALU.add)
                last.then_inc(s2_ready, 1)

            def mix_low(n, batches):
                for i, (dst, src) in enumerate(batches):
                    dve.wait_ge(mix_hi, n + i + 1)
                    nc.vector.tensor_tensor(h_lo[:, dst:dst + 4, :], z[:, src:src + 4, :],
                                            h_hi[:, dst:dst + 4, :].bitcast(F32), ALU.subtract).then_inc(mix_ready, 1)

            recurrence(0, "ada0b", 0, range(8), range(8))
            dve.wait_ge(ors_ready, 1)
            gn = VB["ev_gla_norm"]
            for m in range(2):
                o_ = z[:, 8 + m:16:2, :]
                last = nc.vector.scalar_tensor_tensor(o_, o_, vb[:, gn + m:gn + m + 1], logp[:, :, :], ALU.mult, ALU.mult)
            step(last)
            dve.wait_ge(silu_ready, 1)
            for i in range(2):
                a = 8 + 4 * i
                nc.vector.tensor_tensor(z[:, a:a + 4, :], z[:, a:a + 4, :], z[:, a + 8:a + 12, :], ALU.mult).then_inc(mix_f32, 1)
            mix_low(0, [(8, 40), (12, 44), (0, 8), (4, 12)])
            n1 = PLAN["out0"][2]
            lo(n1, 0, 0)
            lo(n1, 1, 0)
            dve.wait_ge(mod_ready, PLAN["ada1u0"][3])
            lo_phase(8, n1, res_evac(n1, 0, 0, G1))
            gains(0, VA["norm_mlp"], SC2)
            modulate(1, 0, SH2)

            def mlp_layer(l, r0):
                _, _, g0, a0 = PLAN["ada1u0" if l == 0 else "up1_0"]
                lead = 2 if l == 0 else 0

                def ada(a, g):
                    def f():
                        ada_group(a, g, 0, with_last=False)
                        ada_group(a + 1, g + 1, 1)
                        ada_end(a + 2, g + 2)
                    return f if l == 0 else None

                def chunk(f, last_chunk):
                    g, a = g0 + CHUNK_GROUPS[l] * f + lead, a0 + 4 * f
                    lo_phase(8, g, up_evac(g, g, 8 * (FF_CHUNKS * l + f)), last_next=g + 8 + lead,
                             middle=ada(a + 2, g + 8))
                    g = g + 8 + lead
                    lo_phase(8, g, res_evac(g, r0 + 8 * f, l, G2),
                             last_next=None if last_chunk else g + 8 + lead,
                             middle=None if last_chunk else ada(a + 4, g + 8))

                if l == 0:
                    ada(a0, g0)()
                lo(g0 + lead, 0, 0)
                lo(g0 + lead, 1, 0)
                with dve.Fori(0, FF_CHUNKS - 1) as f:
                    chunk(f, False)
                chunk(FF_CHUNKS - 1, True)

            mlp_layer(0, 8)
            gains(1, VA["norm_mix"] + KT, SC1)
            n2 = PLAN["glu"][2]
            lo(n2, 0, 0)
            lo(n2, 1, 0)
            modulate(2, 1, SH1)
            dve.wait_ge(cw_psum, 1)
            nc.vector.tensor_copy(conv_w[:, :, :], pm[:, 0, 0:8 * TAPS].rearrange("p (j r) -> p j r", r=TAPS)).then_inc(conv_step, 1)
            n3 = PLAN["in1"][2]
            lo_phase(8, n2, z_evac(n2, 32), last_next=n3)
            dve.wait_ge(gb_sig, 1)
            dve.wait_ge(conv_step, 1)
            nc.vector.tensor_tensor(z[:, 32:40, :], z[:, 32:40, :], z[:, 40:48, :], ALU.mult).then_inc(cv_in, 1)
            dve.wait_ge(cv_in, 1)

            PER_BLOCK = TAPS + 1

            def conv(j, s):
                src = zf[:, bass.ds((32 + j) * T, TP)]
                acc = [zf[:, bass.ds((40 + j) * T, TP)], acc1[:, :]]
                base = 1 + PER_BLOCK * j
                for shift in range(4 * s, min(4 * s + 4, TAPS)):
                    tap = TAPS - 1 - shift
                    wt = conv_w[:, bass.ds(j, 1), tap:tap + 1].rearrange("p a t -> p (a t)")
                    a = acc[shift % 2]
                    if shift == 0:
                        bias = vb[:, bass.ds(VB["od_conv_b"] + j, 1)]
                        ins = nc.vector.tensor_scalar(a, src, wt, bias, ALU.mult, ALU.add)
                    elif shift == 1:
                        dve.wait_ge(conv_step, base)
                        nc.vector.tensor_scalar(a, src, 0.0, None, ALU.mult).then_inc(conv_zero, 1)
                        dve.wait_ge(conv_zero, j + 1)
                        ins = nc.vector.scalar_tensor_tensor(a[:, 1:TP], src[:, 0:TP - 1], wt, a[:, 1:TP], ALU.mult, ALU.add)
                    else:
                        dve.wait_ge(conv_step, base + (shift - 1))
                        ins = nc.vector.scalar_tensor_tensor(a[:, shift:TP], src[:, 0:TP - shift], wt, a[:, shift:TP],
                                                             ALU.mult, ALU.add)
                    ins.then_inc(conv_step, 1)
                if s == 7:
                    dve.wait_ge(conv_step, base + TAPS)
                    nc.vector.tensor_tensor(acc[0], acc[0], acc[1], ALU.add).then_inc(conv_step, 1)

            lo_phase(16, n3, z_evac(n3, 0), loop_work=conv)
            for j in range(8):
                dve.wait_ge(past_psum, 2 + j)
                wj = conv_w[:, j, 0:CONV_PAST].unsqueeze(1).broadcast_to([P, NS, CONV_PAST])
                past = pm[:, j % 2, 0:NS * CONV_PAST].rearrange("p (b r) -> p b r", r=CONV_PAST)
                nc.vector.tensor_tensor(cprod[:, :, :], past, wj, ALU.mult).then_inc(past_taken, 1)
                dve.wait_ge(past_taken, 2 + j)
                step(nc.vector.tensor_reduce(csum[:, :], cprod[:, :, :], AX.X, ALU.add))
                o_ = z[:, 40 + j, TP:T]
                step(nc.vector.scalar_tensor_tensor(o_, z[:, 32 + j, TP:T], conv_w[:, j, TAPS - 1:TAPS], csum[:, :], ALU.mult, ALU.add))
                cb = VB["od_conv_b"] + j
                nc.vector.tensor_scalar(o_, o_, vb[:, cb:cb + 1], None, ALU.add).then_inc(cv_done, 1)
            dve.wait_ge(ln_mean, 1)
            dve.wait_ge(conv_step, 1 + 8 * PER_BLOCK)
            cvz = z[:, 40:48, :]
            nc.vector.tensor_tensor(cvz, cvz, mean[:, :].unsqueeze(1).broadcast_to([P, 8, T]), ALU.subtract).then_inc(ln_cent, 1)
            dve.wait_ge(ln_rstd, 1)
            step(nc.vector.tensor_tensor(cvz, cvz, rstd[:, :].unsqueeze(1).broadcast_to([P, 8, T]), ALU.mult))
            for j in range(8):
                g_, b_ = VB["od_ln_g"] + j, VB["od_ln_b"] + j
                last = nc.vector.tensor_scalar(z[:, 40 + j, :], z[:, 40 + j, :], vb[:, g_:g_ + 1], vb[:, b_:b_ + 1], ALU.mult, ALU.add)
            last.then_inc(ln_done, 1)
            for q in (1, 2):
                zk = HEADS[q]["k"]
                dve.wait_ge(sig_ready, q)
                for h in range(HG):
                    c = HEADS[q]["q"] + h
                    nc.vector.tensor_scalar(z[:, zk + h, :], z[:, zk + h, :], oml[:, c:c + 1], None, ALU.mult)
                    last = nc.vector.tensor_scalar(logp[:, h, :], logp[:, h, :], oml[:, c:c + 1], lb[:, c:c + 1], ALU.mult, ALU.add)
                last.then_inc(k_ready, 1)
                dve.wait_ge(k_ready, q)
                nc.vector.tensor_scalar(gzf, lpf, MIN_GATE, 1.0 / TWO60, ALU.max, ALU.max)
                step(nc.vector.tensor_scalar(lpf, lpf, MIN_GATE, TWO60, ALU.max, ALU.mult))
                nc.vector.tensor_scalar(lpf, lpf, 1.0, None, ALU.min).then_inc(ln_in, 1)
                dve.wait_ge(ln_out, q)
                nc.vector.tensor_tensor(lpf, lpf, gzf, ALU.add).then_inc(logp_ready, 1)
                dve.wait_ge(logp_ready, q + 1)
                recurrence(q, "ada1b", 8 * (q - 1), range(0, 8, 2), range(0, 8, 2))
            dve.wait_ge(ors_ready, 3)
            hn = VB["od_hgrn_norm"]
            step(nc.vector.scalar_tensor_tensor(z[:, 16:24, :], z[:, 16:24, :], vb[:, hn:hn + 1], z[:, 8:16, :], ALU.mult, ALU.mult))
            dve.wait_ge(silu_ready, 2)
            for i in range(2):
                a = 16 + 4 * i
                nc.vector.tensor_tensor(z[:, a:a + 4, :], z[:, a:a + 4, :], z[:, a + 8:a + 12, :], ALU.mult).then_inc(mix_f32, 1)
            mix_low(4, [(8, 40), (12, 44), (0, 16), (4, 20)])
            n4 = PLAN["out1"][2]
            lo(n4, 0, 0)
            lo(n4, 1, 0)
            dve.wait_ge(mod_ready, 96)
            lo_phase(8, n4, res_evac(n4, 40, 1, G1))
            gains(1, VA["norm_mlp"] + KT, SC2)
            modulate(3, 1, SH2)
            mlp_layer(1, 48)
            dve.wait_ge(rstd_ready, 5)
            for k in range(KT):
                c = VA["norm_final"] + k
                nc.vector.scalar_tensor_tensor(x[:, k, :], x[:, k, :], va[:, c:c + 1], rstd[:, :], ALU.mult, ALU.mult).then_inc(y_ready, 1)


INPUTS = ["x_prompt", "x_sample", "c_prompt", "c_sample", "state_gla", "state_pool", "state_hgrn", "state_conv",
          "w_ada", "b_ada", "norm_mix", "norm_mlp", "norm_final", "ev_w_in", "ev_w_gate_up", "ev_b_gate",
          "ev_gla_norm", "ev_pool_w", "ev_pool_scale", "ev_w_out", "od_w_in", "od_lb_raw", "od_hgrn_norm",
          "od_conv_w", "od_conv_b", "od_ln_g", "od_ln_b", "od_w_out", "mlp_w_up", "mlp_w_down"]
OUTPUTS = [("y_prompt", (1, 256, 2048)), ("y_sample", (8, 1, 2048)),
           ("new_gla_prompt", (1, 1, 4, 128, 256)), ("new_pool_prompt", (1, 1, 15, 1024)),
           ("new_hgrn_prompt", (1, 1, 8, 128, 128)), ("new_conv_prompt", (1, 1, 30, 1024)),
           ("new_gla_sample", (1, 8, 4, 128, 256)), ("new_pool_sample", (1, 8, 15, 1024)),
           ("new_hgrn_sample", (1, 8, 8, 128, 128)), ("new_conv_sample", (1, 8, 30, 1024))]


def kernel(**inputs):
    import concourse.bacc as bacc
    from concourse.bass_utils import run_bass_kernel_spmd

    nc = bacc.Bacc("TRN2", target_bir_lowering=False, num_devices=1)
    arrays, io, out = {}, {}, {}
    for name, a in list((n, inputs[n]) for n in INPUTS) + list(constants().items()):
        a = np.ascontiguousarray(a)
        arrays[f"in_{name}"] = a
        io[name] = nc.dram_tensor(f"in_{name}", a.shape, mybir.dt.from_np(a.dtype), kind="ExternalInput").ap()
    for name, shape in OUTPUTS:
        out[name] = nc.dram_tensor(f"out_{name}", shape, F32, kind="ExternalOutput").ap()
    build(nc, io, out)
    r = run_bass_kernel_spmd(nc, [arrays], core_ids=[0])
    return tuple(r.results[0][f"out_{name}"] for name, _ in OUTPUTS)
```

```python
from contextlib import ExitStack

import numpy as np

import concourse.bass as bass
from concourse import mybir

F32 = mybir.dt.float32
F32R = mybir.dt.float32r
I32 = mybir.dt.int32
U8 = mybir.dt.uint8
ALU = mybir.AluOpType
ACT = mybir.ActivationFunctionType
AX = mybir.AxisListType

P = 128
D = 2048
KT = D // P
TP = 256
NS = 8
T = TP + NS
NC = NS + 1
GC = 256
MT = GC // P
UK = 4
NU = KT // UK
UW = UK * GC
CH = 128
NCH = TP // CH
LEVELS = 7
HG = 4
DK = 128
WINDOWS = (2, 4, 8, 16)
POOL_PAST = 15
TAPS = 31
CONV_PAST = 30
EPS = 1e-6
MIN_GATE = 1e-30
TWO60 = float(2 ** 60)
FF_CHUNKS = 4
POOL_TAIL = POOL_PAST + NS
CONV_TAIL = CONV_PAST + NS

VA = {"norm_mix": 0, "norm_mlp": 32, "norm_final": 64}
VB = {"ev_b_gate": 0, "ev_gla_norm": 4, "ev_pool_scale": 6, "od_lb_raw": 14, "od_hgrn_norm": 22,
      "od_conv_b": 23, "od_ln_g": 31, "od_ln_b": 39}
VB_ROWS = 47
SH1, SC1, G1, SH2, SC2, G2 = range(0, 96, 16)


def make_plan():
    order = [("ada0a", "ada", 16), ("in0", "gemm", 16), ("ada0b", "ada", 32), ("out0", "gemm", 8)]
    for f in range(FF_CHUNKS):
        order += [(f"up0_{f}", "mixed", 10), (f"down0_{f}", "mixed", 10)]
    order += [("glu", "gemm", 8), ("in1", "gemm", 16), ("ada1b", "ada", 32), ("out1", "gemm", 8)]
    for f in range(FF_CHUNKS):
        order += [(f"up1_{f}", "gemm", 8), (f"down1_{f}", "gemm", 8)]
    plan, g, a = {}, 0, 0
    for name, kind, count in order:
        plan[name] = (kind, count, g, a)
        g += count
        a += {"ada": count, "gemm": 0, "mixed": 2}[kind]
    return plan


PLAN = make_plan()


FILLS = {"ada0b": {"gate": 1, "past": 3, "vt0": 2, **{f"kv0_{b}": 1 + (b % 4 == 3) for b in range(NS)},
                   **{f"lv0_{i}": 1 + i % 2 for i in range(LEVELS + 1)}, "kd0": 1, "o0_1": 1, "pool": 2},
         "ada1b": {"ln1": 1, "ln2": 1, "gates2": 2, **{f"kv{q}_{b}": 1 for q in (1, 2) for b in range(NS)},
                   **{f"lv{q}_{i}": 1 for q in (1, 2) for i in range(1, LEVELS)}}}
assert all(sum(points.values()) == PLAN[name][1] for name, points in FILLS.items())


def fills(count, point):
    for name, points in FILLS.items():
        for _ in range(points.get(point, 0)):
            yield name, (count.next() - 1) % PLAN[name][1]


def constants():
    s, t = np.arange(CH)[:, None], np.arange(CH)[None, :]
    masks = np.zeros((CH, LEVELS, CH), np.int32)
    for lv in range(LEVELS):
        h = 1 << lv
        masks[:, lv, :] = (s // (2 * h) == t // (2 * h)) & (s % (2 * h) < h) & (t % (2 * h) >= h)
    inv = np.zeros((P, len(WINDOWS), 16), np.float32)
    for g, w in enumerate(WINDOWS):
        inv[:, g, :] = 1.0 / np.minimum(np.arange(16) + 1, w).astype(np.float32)
    return {"ident": np.eye(P, dtype=np.float32), "masks": masks.reshape(CH, LEVELS * CH),
            "inv_count": inv.reshape(P, -1)}


START_BANKS = 2 + KT
CONSTS = len(VA) + len(VB) + 1
SMALL_OUTS = 9
CHUNK_GROUPS = (20, 16)
OPAIRS = [0, 4, 6, 8]


class Count:
    def __init__(self):
        self.n = 0

    def next(self):
        self.n += 1
        return self.n


def build(nc, io, out):
    stack = ExitStack()
    with stack:
        used = [(nc.sbuf_base + 31) // 32 * 32]

        def at(name, shape, dt, offset):
            return nc.alloc_sbuf_tensor_at(name, shape, dt, offset=offset)

        def sb(name, shape, dt=F32):
            size = int(np.prod(shape[1:])) * (1 if dt == U8 else 4)
            offset = used[0]
            used[0] += (size + 31) // 32 * 32
            assert used[0] <= nc.sbuf_top, (name, used[0], nc.sbuf_top)
            return at(name, shape, dt, offset)

        def arena(size):
            offset = used[0]
            used[0] += (size + 31) // 32 * 32
            assert used[0] <= nc.sbuf_top
            return offset

        def sem(name):
            return stack.enter_context(nc.semaphore(name))

        x = sb("x", [P, KT, T])
        raw = sb("raw", [P, 2, NU, UW])
        w_hi = sb("w_hi", [P, NU, UW], F32R)
        w_lo = sb("w_lo", [P, NU, UW], F32R)
        mod = sb("mod", [P, 2, 96, NC])
        amod = sb("amod", [P, KT, NC])
        CW = 2 * NC
        c_hl = sb("c_hl", [P, KT * CW + P - CW], F32R)
        sel = sb("sel", [CW, NC])
        mod_rows = sb("mod_rows", [CW, 2, GC])
        bada = sb("bada", [P, 2, 96])
        va = sb("va", [P, 80])
        vb = sb("vb", [P, VB_ROWS])
        ident = sb("ident", [P, P])
        ones = sb("ones", [P, P])
        zero = sb("zero", [P, 1])
        masks = sb("masks", [P, LEVELS, CH], U8)
        inv_count = sb("inv_count", [P, len(WINDOWS), 16])
        lb = sb("lb", [P, 8])
        oml = sb("oml", [P, 8])
        sm = sb("sm", [P, 8])
        eps_t = sb("eps_t", [P, 1])
        o_rs = arena(2 * T * 4)
        rstd = at("rstd", [P, T], F32, o_rs)
        lnv = at("lnv", [P, T], F32, o_rs + T * 4)
        pb = at("pb", [P, 2, TP], F32, o_rs)
        o_hid = arena(MT * T * 4)
        hid = at("hid", [P, MT, T], F32, o_hid)
        pa = at("pa", [P, 2, TP], F32, o_hid)
        g8 = sb("g8", [P, MT, NS])
        t8 = sb("t8", [P, KT, NS])
        wsum = sb("wsum", [P, MT, NS])
        decay8 = sb("decay8", [P, HG, NS])
        logp = sb("logp", [P, HG, T])
        o_sq = arena(2 * MT * T * 4)
        sq = at("sq", [P, 2, MT, T], F32, o_sq)
        hs = at("hs", [P, 4, TP], F32, o_sq)
        o_mw = arena(8192)
        pool_w = at("pool_w", [P, 4, 2, 256], F32, o_mw)
        conv_w = at("conv_w", [P, 8, TAPS], F32, o_mw)
        acc1 = at("acc1", [P, TP], F32, o_mw + 1024)
        cprod = at("cprod", [P, NS, CONV_PAST], F32, o_mw + 2048)
        mean = at("mean", [P, T], F32, o_mw + 3200)
        cw_rows = at("cw_rows", [TAPS, 1024], F32, o_mw + 4352 - 256)
        o_gw = arena(2048)
        gate_up = at("gate_up", [16, 512], F32, o_gw)
        o_h = arena(2 * KT * T * 4)
        h_hi = at("h_hi", [P, KT, T], F32R, o_h)
        h_lo = at("h_lo", [P, KT, T], F32R, o_h + KT * T * 4)
        dec = at("dec", [P, 2, HG, TP], F32, o_h)
        gz = at("gz", [P, HG, T], F32, o_h)
        gl = at("gl", [P, HG, T], F32, o_sq)
        fac = at("fac", [P, 2, HG, TP], F32, o_h + 8192)
        st = at("st", [P, 2, 1024], F32, o_h + 8192)
        scores = at("scores", [P, NCH, HG, CH], F32, o_h + 16384)
        kmask = at("kmask", [NS, 2, HG * DK], F32, o_h + 16384)
        s1 = at("s1", [P, 1024], F32, o_h + 20480)
        k8 = at("k8", [NS, HG * DK], F32, o_h + 20480)
        kdT = at("kdT", [P, NCH, HG * DK], F32, o_h + 24576)
        v8 = at("v8", [NS, 1024], F32, o_h + 24576)
        s2 = at("s2", [P, 1024], F32, o_h + 28672)
        o_z = arena(48 * T * 4)
        z = at("z", [P, 48, T], F32, o_z)
        zf = z[:, :, :].rearrange("p a t -> p (a t)")
        f_hi = at("f_hi", [P, KT, T], F32R, o_z)
        f_lo = at("f_lo", [P, KT, T], F32R, o_z + KT * T * 4)
        x_rows = at("x_rows", [P, NCH, D], F32, o_z)
        xs_rows = at("xs_rows", [NS, D], F32, o_z + 16384)
        c_rows = at("c_rows", [NC, D], F32, o_z + 24576)
        va_rows = at("va_rows", [80, P], F32, o_z + 32768)
        vb_rows = at("vb_rows", [VB_ROWS, P], F32, o_z + 33280)
        ba_rows = at("ba_rows", [96, 2, P], F32, o_z + 33792)
        cs_rows = at("cs_rows", [NC, D], F32, o_z + 34816)
        mask_rows = at("mask_rows", [P, LEVELS, CH], I32, o_z + 43008)
        y_rows = at("y_rows", [P, NCH, D], F32, o_z)
        ys_rows = at("ys_rows", [NS, D], F32, o_z + 16384)
        vT_at = {0: o_z + 40 * T * 4, 1: o_z + 32 * T * 4}
        vT = {layer: at(f"vT{layer}", [P, NCH, 1024], F32, vT_at[layer]) for layer in range(2)}
        a_w = at("a_w", [P, KT, 16], F32, o_z + 46 * T * 4)
        pastc = at("pastc", [120, 2, 1024], F32, o_h + 8192)
        pastu = at("pastu", [120, 1024], F32, o_h + 28672)
        AW = KT * 16 + P - 16
        a_hi = at("a_hi", [P, AW], F32R, o_sq)
        a_lo = at("a_lo", [P, AW], F32R, o_sq + AW * 4)
        a_lr = at("a_lr", [16, T], F32, o_sq + 2 * AW * 4)
        tail = sb("tail", [CONV_TAIL, 1024])

        ps = stack.enter_context(nc.psum_tensor("ps", [P, 4, 512], F32))
        pm = stack.enter_context(nc.psum_tensor("pm", [P, 4, 512], F32))

        raw_in = [[sem(f"raw_in{p}{h}") for h in range(2)] for p in range(2)]
        hi_ready = sem("hi_ready")
        lo_ready = sem("lo_ready")
        split_used = sem("split_used")
        evacuated = sem("evacuated")
        turned = sem("turned")
        mod_ready = sem("mod_ready")
        c_in = sem("c_in")
        rows_in = sem("rows_in")
        ident_in = sem("ident_in")
        masks_in = sem("masks_in")
        const_in = sem("const_in")
        c_silu = sem("c_silu")
        c_high = sem("c_high")
        tr_ready = sem("tr_ready")
        tr_taken = sem("tr_taken")
        filled = sem("filled")
        sq_ready = sem("sq_ready")
        ss_done = sem("ss_done")
        x_ready = sem("x_ready")
        gate8_done = sem("gate8_done")
        rstd_ready = sem("rstd_ready")
        t8_ready = sem("t8_ready")
        h8_hi = sem("h8_hi")
        amod_ready = sem("amod_ready")
        hs_even = sem("hs_even")
        hs_odd = sem("hs_odd")
        hh_ready = sem("hh_ready")
        h_ready = sem("h_ready")
        hid_relu = sem("hid_relu")
        hid_sq = sem("hid_sq")
        hid_hi = sem("hid_hi")
        hid_ready = sem("hid_ready")
        mix_hi = sem("mix_hi")
        mix_ready = sem("mix_ready")
        mix_f32 = sem("mix_f32")
        dve_step = sem("dve_step")
        act_step = sem("act_step")
        pool_step = sem("pool_step")
        aw_in = sem("aw_in")
        aw_hi = sem("aw_hi")
        aw_lo = sem("aw_lo")
        alr_psum = sem("alr_psum")
        alr_ready = sem("alr_ready")
        gate_psum = sem("gate_psum")
        gz_ready = sem("gz_ready")
        gl_ready = sem("gl_ready")
        logp_ready = sem("logp_ready")
        q_scaled = sem("q_scaled")
        past_in = sem("past_in")
        past_psum = sem("past_psum")
        past_taken = sem("past_taken")
        tail_psum = sem("tail_psum")
        tail_ready = sem("tail_ready")
        pool_d = sem("pool_d")
        pool_psum = sem("pool_psum")
        pool_taken = sem("pool_taken")
        k_ready = sem("k_ready")
        sig_ready = sem("sig_ready")
        ln_in = sem("ln_in")
        ln_out = sem("ln_out")
        vtr_psum = sem("vtr_psum")
        vtr_ready = sem("vtr_ready")
        dec8_ready = sem("dec8_ready")
        kmask_ready = sem("kmask_ready")
        kv_psum = sem("kv_psum")
        st_in = [sem(f"st_in{i}") for i in range(4)]
        st_ready = sem("st_ready")
        st_out = [sem(f"st_out{i}") for i in range(4)]
        o8_psum = sem("o8_psum")
        o8_taken = sem("o8_taken")
        sc_psum = sem("sc_psum")
        sc_taken = sem("sc_taken")
        prefix_ready = sem("prefix_ready")
        dif_ready = sem("dif_ready")
        exp_ready = sem("exp_ready")
        fac_ready = sem("fac_ready")
        right_ready = sem("right_ready")
        end_ready = sem("end_ready")
        kd_psum = sem("kd_psum")
        kd_ready = sem("kd_ready")
        s1_psum = sem("s1_psum")
        s1_ready = sem("s1_ready")
        kv1_psum = sem("kv1_psum")
        s2_ready = sem("s2_ready")
        o_psum = sem("o_psum")
        o_ready = sem("o_ready")
        osq_ready = sem("osq_ready")
        oss_psum = sem("oss_psum")
        ors_ready = sem("ors_ready")
        silu_ready = sem("silu_ready")
        cw_psum = sem("cw_psum")
        gb_sig = sem("gb_sig")
        cv_in = sem("cv_in")
        conv_step = sem("conv_step")
        ln_psum = sem("ln_psum")
        ln_mean = sem("ln_mean")
        ln_cent = sem("ln_cent")
        ln_sq = sem("ln_sq")
        ln_rstd = sem("ln_rstd")
        ln_done = sem("ln_done")
        cv_ready = sem("cv_ready")
        cv_done = sem("cv_done")
        lb_exp = sem("lb_exp")
        y_ready = sem("y_ready")
        y_psum = sem("y_psum")
        y_taken = sem("y_taken")
        small_out = sem("small_out")
        y_out = sem("y_out")

        HEADS = [dict(layer=0, nv=8, dv=256, q=0, k=4, v=8, bufs=2),
                 dict(layer=1, nv=4, dv=128, q=0, k=8, v=16, bufs=4),
                 dict(layer=1, nv=4, dv=128, q=4, k=12, v=20, bufs=4)]
        SETS = 1 + LEVELS

        def halves(t, w):
            v = t.rearrange("p h (n s w) -> p h n s w", s=2, w=w)
            return v[:, :, :, 0, :], v[:, :, :, 1, :]

        def kv_bank(q, b, o):
            dv = HEADS[q]["dv"]
            return pm[:, o // 512 if dv == 256 else b % 2, o % 512:o % 512 + dv]

        def state(q, b):
            n = HG * HEADS[q]["dv"]
            at_ = (b % HEADS[q]["bufs"]) * n
            return st[:, at_ // 1024, at_ % 1024:at_ % 1024 + n]

        def transfers(q, b):
            i = b % HEADS[q]["bufs"]
            before = sum(len(range(i, NS, HEADS[r]["bufs"])) for r in range(q) if i < HEADS[r]["bufs"])
            return before + b // HEADS[q]["bufs"] + 1

        def bank2(p):
            return ps[:, MT * p:MT * p + MT, 0:T]

        block = stack.enter_context(nc.Block())

        @block.sync
        def _(sp):
            def group(g, p, view, col, k0):
                for h in range(2):
                    if not isinstance(g, int) or g >= 2:
                        sp.wait_ge(lo_ready, NU * (g - 2) + (2 * h + 2))
                    sp.dma_start(raw[:, p, 2 * h:2 * h + 2, :].rearrange("p u (k n) -> p (u k) n", n=GC),
                                 view[:, bass.ds(k0 + 8 * h, 8), bass.ds(col, GC)]).then_inc(raw_in[p][h], 16)

            def phase(count, g, view, col, k0=0, between=None):
                peel = 1 if count == 2 or (isinstance(g, int) and g == 0) else 0
                for i in range(2 * peel):
                    group(g + i, i, view, col(i), k0)
                if between:
                    between()
                if count // 2 > peel:
                    with sp.Fori(0, count // 2 - peel) as j:
                        for p in range(2):
                            i = 2 * j + (2 * peel + p)
                            group(g + i, p, view, col(i), k0)

            def kview(w):
                return w.rearrange("(k p) n -> p k n", p=P)

            def static_phase(name, view, col, k0=0):
                phase(PLAN[name][1], PLAN[name][2], view, col, k0)

            sp.dma_start(c_rows[0:1, :], io["c_prompt"]).then_inc(c_in, 16)
            sp.dma_start(c_rows[1:NC, :], io["c_sample"]).then_inc(c_in, 16)

            sp.dma_start(ident[:, :], io["ident"]).then_inc(ident_in, 16)

            def x_in():
                sp.dma_start(x_rows[:, :, :], io["x_prompt"][0].rearrange("(c p) d -> p c d", p=P)).then_inc(rows_in, 16)
                sp.dma_start(xs_rows[:, :], io["x_sample"].rearrange("b t d -> (b t) d")).then_inc(rows_in, 16)

            ada = [kview(io["w_ada"][l]) for l in range(2)]
            up = [kview(io["mlp_w_up"][l]) for l in range(2)]
            down = [kview(io["mlp_w_down"][l]) for l in range(2)]
            phase(PLAN["ada0a"][1], 0, ada[0], lambda i: i * GC, between=x_in)
            g0 = PLAN["in0"][2]
            w = kview(io["ev_w_in"][0])
            phase(12, g0, w, lambda i: i * GC)
            phase(4, g0 + 12, w, lambda i: (12 + i) * GC + 16)
            static_phase("ada0b", ada[0], lambda i: (16 + i) * GC)
            static_phase("out0", kview(io["ev_w_out"][0]), lambda i: i * GC)

            def mlp_layer(l):
                g0 = PLAN["up0_0" if l == 0 else "up1_0"][2]
                with sp.Fori(0, FF_CHUNKS) as f:
                    g = g0 + CHUNK_GROUPS[l] * f
                    for b in range(2):
                        view, k0 = (up[l], 0) if b == 0 else (down[l], f * KT)
                        col = (lambda i: f * D + i * GC) if b == 0 else (lambda i: i * GC)
                        if l == 0:
                            for i in range(2):
                                group(g + 2 * i, 0, view, col(i), k0)
                                group(g + (2 * i + 1), 1, ada[1], (4 * f + (2 * b + i)) * GC, 0)
                            phase(6, g + 4, view, lambda i: col(i + 2), k0)
                            g = g + 10
                        else:
                            phase(8, g, view, col, k0)
                            g = g + 8

            mlp_layer(0)
            w = kview(io["od_w_in"][0])
            static_phase("glu", w, lambda i: (16 + i) * GC)
            static_phase("in1", w, lambda i: i * GC)
            static_phase("ada1b", ada[1], lambda i: (16 + i) * GC)
            static_phase("out1", kview(io["od_w_out"][0]), lambda i: i * GC)
            mlp_layer(1)
            for r in range(3):
                sp.wait_ge(y_taken, 4 * (r + 1))
                if r < 2:
                    sp.dma_start(out["y_prompt"][0, r * P:(r + 1) * P, :], y_rows[:, r, :]).then_inc(y_out, 16)
                else:
                    sp.dma_start(out["y_sample"].rearrange("b t d -> (b t) d"), ys_rows[:, :]).then_inc(y_out, 16)
            sp.wait_ge(y_out, 48)
            sp.wait_ge(small_out, 16 * SMALL_OUTS)
            for b in range(NS - 4, NS):
                sp.wait_ge(st_out[b % 4], 16 * transfers(2, b))

        @block.gpsimd
        def _(pool):
            steps = Count()

            def step(ins):
                ins.then_inc(pool_step, 1)
                pool.wait_ge(pool_step, steps.next())

            for name, row in VA.items():
                src = io[name]
                n = 16 if name == "norm_final" else 32
                src = src.rearrange("(k p) -> k p", p=P) if name == "norm_final" else src.rearrange("l (k p) -> (l k) p", p=P)
                pool.dma_start(va_rows[row:row + n, :], src).then_inc(const_in, 16)
            for name, row in VB.items():
                src = io[name].rearrange("l (k p) -> (l k) p", p=P)
                pool.dma_start(vb_rows[row:row + src.shape[0], :], src).then_inc(const_in, 16)
            pool.dma_start(ba_rows[:, :, :], io["b_ada"].rearrange("l (m p) -> m l p", p=P)).then_inc(const_in, 16)
            pool.dma_start(mask_rows[:, :, :], io["masks"].rearrange("p (l t) -> p l t", l=LEVELS)).then_inc(masks_in, 16)
            pool.dma_start(inv_count[:, :, :], io["inv_count"].rearrange("p (g t) -> p g t", t=16)).then_inc(masks_in, 16)
            pool.dma_start(gate_up[:, :], io["ev_w_gate_up"][0]).then_inc(aw_in, 16)
            pool.dma_start(pool_w[:, :, :, :], io["ev_pool_w"][0].rearrange("g (c p) e -> p g c e", p=P)).then_inc(aw_in, 16)
            pool.wait_ge(tr_ready, START_BANKS)
            pool.dma_start(a_w[:, :, :], io["ev_w_in"][0][:, 3072:3088].rearrange("(k p) n -> p k n", p=P)).then_inc(aw_in, 16)

            def scales(r):
                pool.wait_ge(amod_ready, r + 1)
                pool.wait_ge(rstd_ready, r + 1)
                pool.wait_ge(x_ready, (0, 8, 40, 48)[r] + 1) if r else pool.wait_ge(tr_taken, START_BANKS)
                for k in range(1, KT, 2):
                    if k >= 5:
                        pool.wait_ge(h_ready, KT * r + k - 3)
                    step(nc.gpsimd.tensor_tensor(hs[:, k % 4, :], x[:, k, 0:TP], rstd[:, 0:TP], ALU.mult))
                    nc.gpsimd.tensor_tensor(hs[:, k % 4, :], hs[:, k % 4, :], amod[:, k, 0:1].broadcast_to([P, TP]),
                                            ALU.mult).then_inc(hs_odd, 1)

            def states(q):
                h = HEADS[q]
                n = HG * h["dv"]
                nb = h["bufs"]
                if h["layer"] == 0:
                    src, dst, hsl = io["state_gla"][0], out["new_gla_sample"][0], slice(0, HG)
                else:
                    src, dst, hsl = io["state_hgrn"][0], out["new_hgrn_sample"][0], slice(h["q"], h["q"] + HG)

                def load(b):
                    pool.dma_start(state(q, b).rearrange("p (h v) -> p h v", h=HG),
                                   src[b, hsl].rearrange("h k v -> k h v")).then_inc(st_in[b % nb], 16)

                pool.wait_ge(vtr_psum, 4 * q + 1)
                for b in range(nb):
                    load(b)
                for b in range(NS):
                    pool.wait_ge(st_ready, NS * q + b + 1)
                    pool.dma_start(dst[b, hsl].rearrange("h k v -> k h v"),
                                   state(q, b).rearrange("p (h v) -> p h v", h=HG)).then_inc(st_out[b % nb], 16)
                    if b + nb < NS:
                        pool.wait_ge(o8_psum, NS * q + b + 1)
                        pool.wait_ge(st_out[b % nb], 16 * transfers(q, b))
                        load(b + nb)

            def level_shares(q):
                zq = HEADS[q]["q"]

                def differ(lv):
                    w = 1 << lv
                    left, _ = halves(logp[:, :, 0:TP], w)
                    dl, _ = halves(dec[:, lv % 2, :, :], w)
                    mid = left[:, :, :, w - 1:w].broadcast_to([P, HG, TP // (2 * w), w])
                    nc.gpsimd.tensor_tensor(dl, mid, left, ALU.subtract).then_inc(dif_ready, 1)

                pool.wait_ge(logp_ready, q + 1)
                pool.wait_ge(dec8_ready, q + 1)
                differ(0)
                pool.wait_ge(o8_psum, NS * (q + 1))
                for b in range(NS - HEADS[q]["bufs"], NS):
                    pool.wait_ge(st_out[b % HEADS[q]["bufs"]], 16 * transfers(q, b))
                for lv in range(LEVELS):
                    w = 1 << lv
                    pool.wait_ge(prefix_ready, LEVELS * q + lv + 1)
                    if lv + 1 < LEVELS:
                        if lv:
                            pool.wait_ge(fac_ready, (LEVELS + 2) * q + lv)
                            pool.wait_ge(right_ready, LEVELS * q + lv)
                        differ(lv + 1)
                    pool.wait_ge(exp_ready, (LEVELS + 2) * q + lv + 1)
                    if lv > 1:
                        pool.wait_ge(sc_psum, SETS * q + lv)
                    _, dr = halves(dec[:, lv % 2, :, :], w)
                    _, fr = halves(fac[:, lv % 2, :, :], w)
                    _, qr = halves(z[:, zq:zq + HG, 0:TP], w)
                    nc.gpsimd.tensor_tensor(fr, qr, dr, ALU.mult).then_inc(right_ready, 1)

            def prompt_state(q):
                h = HEADS[q]
                name, hsl = ("new_gla_prompt", slice(0, HG)) if h["layer"] == 0 else ("new_hgrn_prompt", slice(h["q"], h["q"] + HG))
                pool.wait_ge(s2_ready, q + 1)
                pool.dma_start(out[name][0, 0, hsl].rearrange("h k v -> k h v"),
                               s2[:, 0:HG * h["dv"]].rearrange("p (h v) -> p h v", h=HG)).then_inc(small_out, 16)

            scales(0)
            pool.dma_start(out["new_pool_sample"][0, :, 0:POOL_PAST - 1, :],
                           io["state_pool"][0, :, 1:POOL_PAST, :]).then_inc(small_out, 16)
            pool.dma_start(out["new_conv_sample"][0, :, 0:CONV_PAST - 1, :],
                           io["state_conv"][0, :, 1:CONV_PAST, :]).then_inc(small_out, 16)
            pool.wait_ge(masks_in, 32)
            pool.wait_ge(evacuated, PLAN["in0"][2] + 16)
            pool.wait_ge(alr_psum, 1)
            pool.dma_start(pastu[:, :], io["state_pool"][0].rearrange("b r c -> (b r) c")).then_inc(past_in, 16)
            u = z[:, 24:32, 0:TP]
            for g, w in enumerate(WINDOWS):
                src, width, bufs = u[:, 2 * g:2 * g + 2, :], 1, [pa, pb]
                while width < w:
                    dst = bufs[0]
                    bufs.reverse()
                    nc.gpsimd.tensor_copy(dst[:, :, 0:width], src[:, :, 0:width])
                    step(nc.gpsimd.tensor_tensor(dst[:, :, width:TP], src[:, :, width:TP], src[:, :, 0:TP - width], ALU.add))
                    src, width = dst, 2 * width
                d = z[:, 32 + 2 * g:34 + 2 * g, 0:TP]
                inv = inv_count[:, g:g + 1, :].broadcast_to([P, 2, 16])
                nc.gpsimd.tensor_tensor(d[:, :, 0:16], src[:, :, 0:16], inv, ALU.mult)
                step(nc.gpsimd.tensor_scalar(d[:, :, 16:TP], src[:, :, 16:TP], 1.0 / w, None, ALU.mult))
                nc.gpsimd.tensor_tensor(d, d, u[:, 2 * g:2 * g + 2, :], ALU.subtract).then_inc(pool_d, 1)
            states(0)
            level_shares(0)
            pool.wait_ge(tail_ready, 1)
            pool.dma_start(out["new_pool_prompt"][0, 0], tail[0:POOL_PAST, :]).then_inc(small_out, 16)
            pool.dma_start(out["new_pool_sample"][0, :, POOL_PAST - 1, :], tail[POOL_PAST:POOL_TAIL, :]).then_inc(small_out, 16)
            prompt_state(0)
            scales(1)
            pool.wait_ge(pool_psum, 4)
            pool.dma_start(cw_rows[:, :], io["od_conv_w"][0]).then_inc(aw_in, 16)
            scales(2)
            pool.wait_ge(split_used, NU * (PLAN["in1"][2] + 16))
            pool.dma_start(pastc[:, :, :], io["state_conv"][0].rearrange("(a b) r c -> (b r) a c", b=4)).then_inc(past_in, 16)
            pool.wait_ge(tail_ready, 2)
            pool.dma_start(out["new_conv_prompt"][0, 0], tail[0:CONV_PAST, :]).then_inc(small_out, 16)
            pool.dma_start(out["new_conv_sample"][0, :, CONV_PAST - 1, :], tail[CONV_PAST:CONV_TAIL, :]).then_inc(small_out, 16)
            for q in (1, 2):
                states(q)
                level_shares(q)
                prompt_state(q)
            scales(3)

        @block.tensor
        def _(pe):
            def products(g, p, xh, xl, ready):
                pe.wait_ge(evacuated, g - 1)
                for u in range(NU):
                    ready(u)
                    pe.wait_ge(lo_ready, NU * g + (u + 1))
                    for m in range(MT):
                        acc = ps[:, MT * p + m, 0:T]
                        for kk in range(UK):
                            k = UK * u + kk
                            cols = slice(kk * GC + m * P, kk * GC + (m + 1) * P)
                            nc.tensor.matmul(acc, w_hi[:, u, cols], xh[:, k, :], start=(k == 0), stop=False)
                            nc.tensor.matmul(acc, w_hi[:, u, cols], xl[:, k, :], start=False, stop=False)
                            last = nc.tensor.matmul(acc, w_lo[:, u, cols], xh[:, k, :], start=False, stop=(k == KT - 1))
                    last.then_inc(split_used, 1)

            def clear_sums():
                nc.tensor.matmul(pm[:, 0, 0:T], ones[:, :], zero[:, :].broadcast_to([P, T]), start=True, stop=False,
                                 skip_group_check=True)

            def sums(norm, i, parity):
                pe.wait_ge(sq_ready, norm + i + 1)
                for m in range(MT):
                    last = nc.tensor.matmul(pm[:, 0, 0:T], ones[:, :], sq[:, parity, m, :], start=False,
                                            stop=False, skip_group_check=True)
                last.then_inc(ss_done, 1)

            def gemm(count, g, xh, xl, ready, norm=None):
                if norm is None:
                    with pe.Fori(0, count // 2) as j:
                        for p in range(2):
                            products(g + 2 * j + p, p, xh, xl, ready)
                    return
                for p in range(2):
                    products(g + p, p, xh, xl, ready)
                clear_sums()
                sums(norm, 0, 0)
                with pe.Fori(0, count // 2 - 1) as j:
                    for p in range(2):
                        i = 2 * j + (2 + p)
                        products(g + i, p, xh, xl, ready)
                        sums(norm, i - 1, 1 - p)
                sums(norm, count - 1, 1)

            def mixed(a, g, xh, xl, ready, norm=None):
                def ready_after_ada(u):
                    if u == 0:
                        pe.wait_ge(mod_ready, a + 2)
                    ready(u)

                def ready_and_turn(b, rows):
                    def f(u):
                        ready(u)
                        if u == NU - 1:
                            pe.wait_ge(evacuated, rows)
                            ada_turn(b, 1)
                    return f

                products(g, 0, xh, xl, ready)
                ada_group(a, g + 1, 1, turn_last=False)
                products(g + 2, 0, xh, xl, ready_and_turn(a, g + 2))
                if norm:
                    clear_sums()
                    sums(norm, 0, 0)
                ada_group(a + 1, g + 3, 1, turn_last=False)
                products(g + 4, 0, xh, xl, ready_and_turn(a + 1, g + 4))
                if norm:
                    sums(norm, 1, 1)
                products(g + 5, 1, xh, xl, ready_after_ada)
                if norm:
                    sums(norm, 2, 0)
                with pe.Fori(0, 2) as j:
                    for p in range(2):
                        i = 2 * j + (4 + p)
                        products(g + 2 + i, p, xh, xl, ready)
                        if norm:
                            sums(norm, i - 1, 1 - p)
                if norm:
                    sums(norm, 7, 1)

            def ada_turn(a, p):
                pe.wait_ge(mod_ready, a - 1) if not isinstance(a, int) or a >= 2 else None
                for m in range(MT):
                    last = nc.tensor.matmul(ps[:, MT * p + 1, m * NC:(m + 1) * NC], mod_rows[:, p, m * P:(m + 1) * P],
                                            sel[:, :], start=True, stop=True)
                last.then_inc(turned, 1)

            def ada_group(a, g, p, turn_last=True):
                if not isinstance(g, int) or g >= 2:
                    pe.wait_ge(evacuated, g - 1)
                for u in range(NU):
                    pe.wait_ge(lo_ready, NU * g + (u + 1))
                    for kk in range(UK):
                        k = UK * u + kk
                        rows = c_hl[:, k * CW:k * CW + P]
                        for part, first in ((w_hi, True), (w_lo, False)):
                            last = nc.tensor.matmul(ps[:, MT * p, 0:GC], rows, part[:, u, kk * GC:(kk + 1) * GC],
                                                    start=(k == 0 and first), stop=(k == KT - 1 and not first))
                    last.then_inc(split_used, 1)
                if turn_last:
                    pe.wait_ge(evacuated, g)
                    ada_turn(a - 1, 1 - p)

            def ada_end(a, g):
                pe.wait_ge(evacuated, g)
                ada_turn(a - 1, 1)

            filled_in = Count()

            def fill(point):
                for name, j in fills(filled_in, point):
                    _, count, g0, a0 = PLAN[name]
                    if j:
                        ada_group(a0 + j - 1, g0 + j - 1, (j - 1) % 2, turn_last=j > 1)

            def fill_end(name):
                _, count, g0, a0 = PLAN[name]
                ada_group(a0 + count - 1, g0 + count - 1, 1)
                ada_end(a0 + count, g0 + count)

            def turn(dst, src, rows):
                return nc.tensor.transpose(dst, src, ident[0:rows, 0:rows])

            pe.wait_ge(ident_in, 16)
            pe.wait_ge(c_silu, 1)
            for k in range(KT):
                last = turn(pm[:, 1, k * NC:(k + 1) * NC], cs_rows[:, k * P:(k + 1) * P], NC)
            last.then_inc(tr_ready, 1)
            pe.wait_ge(filled, 1)
            pe.wait_ge(tr_taken, 1)
            ada_group(0, 0, 0, turn_last=False)
            ada_group(1, 1, 1)
            pe.wait_ge(const_in, 16 * CONSTS)
            turn(pm[:, 0, 0:80], va_rows[:, :], 80)
            turn(pm[:, 0, 80:80 + VB_ROWS], vb_rows[:, :], VB_ROWS)
            turn(pm[:, 0, 128:224], ba_rows[:, 0, :], 96)
            turn(pm[:, 0, 224:320], ba_rows[:, 1, :], 96).then_inc(tr_ready, 1)
            pe.wait_ge(rows_in, 32)
            pe.wait_ge(tr_taken, 2)

            def first_squares(r):
                for i in (2 * r, 2 * r + 1):
                    pe.wait_ge(sq_ready, i + 1)
                    for m in range(MT):
                        last = nc.tensor.matmul(pm[:, 0, 0:T], ones[:, :], sq[:, i % 2, m, :], start=(i + m == 0),
                                                stop=(i + m == KT // 2), skip_group_check=True)
                    last.then_inc(ss_done, 1)

            for r in range(4):
                for k in range(4 * r, 4 * r + 4):
                    b = 1 + k % 3
                    if k >= 3:
                        pe.wait_ge(tr_taken, k)
                    for c in range(NCH):
                        turn(pm[:, b, c * P:(c + 1) * P], x_rows[:, c, k * P:(k + 1) * P], P)
                    turn(pm[:, b, TP:T], xs_rows[:, k * P:(k + 1) * P], NS).then_inc(tr_ready, 1)
                ada_group(2 + r, 2 + r, r % 2)
                if r:
                    first_squares(r - 1)
            first_squares(3)
            count = PLAN["ada0a"][1]
            with pe.Fori(0, count // 2 - 3) as j:
                for p in range(2):
                    ada_group(2 * j + (6 + p), 2 * j + (6 + p), p)
            ada_end(count, count)

            def h_wait(n):
                return lambda u: pe.wait_ge(h_ready, KT * n + UK * (u + 1))

            pe.wait_ge(mod_ready, PLAN["ada0b"][3])
            gemm(12, PLAN["in0"][2], h_hi, h_lo, h_wait(0))
            pe.wait_ge(aw_lo, 1)
            pe.wait_ge(rstd_ready, 1)
            for k in range(KT):
                cols = slice(16 * k, 16 * k + P)
                nc.tensor.matmul(pm[:, 0, 0:T], a_hi[:, cols], h_hi[:, k, :], start=(k == 0), stop=False)
                nc.tensor.matmul(pm[:, 0, 0:T], a_hi[:, cols], h_lo[:, k, :], start=False, stop=False)
                last = nc.tensor.matmul(pm[:, 0, 0:T], a_lo[:, cols], h_hi[:, k, :], start=False, stop=(k == KT - 1))
            last.then_inc(alr_psum, 1)
            pe.wait_ge(alr_ready, 1)
            for h in range(HG):
                last = nc.tensor.matmul(pm[:, h, 0:T], gate_up[:, h * DK:(h + 1) * DK], a_lr[:, :], start=True, stop=True)
            last.then_inc(gate_psum, 1)
            gemm(4, PLAN["in0"][2] + 12, h_hi, h_lo, h_wait(0))
            fill("gate")
            pe.wait_ge(evacuated, PLAN["in0"][2] + 16)
            pe.wait_ge(gz_ready, 1)
            for j in range(8):
                last = turn(pm[0:POOL_TAIL, 2 + j // 4, (j % 4) * P:(j % 4 + 1) * P],
                            z[:, 24 + j, T - POOL_TAIL:T], P)
            last.then_inc(tail_psum, 1)
            pe.wait_ge(past_in, 16)
            for j in range(8):
                last = turn(pm[:, j // 4, (j % 4) * 120:(j % 4 + 1) * 120], pastu[:, j * P:(j + 1) * P], 120)
            last.then_inc(past_psum, 1)
            fill("past")
            pe.wait_ge(tail_ready, 1)
            pe.wait_ge(past_taken, 1)

            def recurrence(q):
                hd = HEADS[q]
                nv, dv, zq, zk, zv = hd["nv"], hd["dv"], hd["q"], hd["k"], hd["v"]
                vt = vT[hd["layer"]]

                for c in range(NCH):
                    for j in range(nv):
                        b = c * (nv // 4) + j // 4
                        last = turn(pm[:, b, (j % 4) * P:(j % 4 + 1) * P], z[:, zv + j, c * CH:(c + 1) * CH], P)
                    last.then_inc(vtr_psum, 1)
                pe.wait_ge(vtr_ready, 4 * q + 2)
                for j in range(nv):
                    last = turn(pm[0:NS, j // 4, (j % 4) * P:(j % 4 + 1) * P], z[:, zv + j, TP:T], P)
                last.then_inc(vtr_psum, 1)
                if q:
                    pe.wait_ge(k_ready, q)
                for h in range(HG):
                    last = turn(pm[0:NS, 2, h * P:(h + 1) * P], z[:, zk + h, TP:T], P)
                last.then_inc(vtr_psum, 1)
                fill(f"vt{q}")
                pe.wait_ge(vtr_ready, 4 * q + 4)
                pe.wait_ge(q_scaled, 1)
                def kv(b):
                    if b == NS:
                        return
                    pe.wait_ge(kmask_ready, NS * q + b + 1)
                    earlier = b - ahead
                    if earlier > 0:
                        pe.wait_ge(st_ready, NS * q + earlier)
                    for h in range(HG):
                        o = h * dv
                        last = nc.tensor.matmul(kv_bank(q, b, o), kmask[:, b % 2, h * DK:(h + 1) * DK],
                                                v8[:, o:o + dv], start=True, stop=True)
                    last.then_inc(kv_psum, 1)

                ahead = 0 if dv == 256 else 1
                if ahead:
                    kv(0)
                for b in range(NS):
                    kv(b + ahead)
                    fill(f"kv{q}_{b}")
                    pe.wait_ge(st_ready, NS * q + b + 1)
                    for j in range(nv):
                        last = nc.tensor.matmul(pm[:, 3, j * NS + b:j * NS + b + 1], state(q, b)[:, j * P:(j + 1) * P],
                                                z[:, zq + j * P // dv, TP + b:TP + b + 1], start=True, stop=True)
                    last.then_inc(o8_psum, 1)
                for i in range(SETS):
                    if i == 0:
                        lhs = [[z[:, zk + h, c * CH:(c + 1) * CH] for h in range(HG)] for c in range(NCH)]
                        rhs = [[z[:, zq + h, c * CH:(c + 1) * CH] for h in range(HG)] for c in range(NCH)]
                    else:
                        pe.wait_ge(fac_ready, (LEVELS + 2) * q + i)
                        pe.wait_ge(right_ready, LEVELS * q + i)
                        lhs = rhs = [[fac[:, (i - 1) % 2, h, c * CH:(c + 1) * CH] for h in range(HG)] for c in range(NCH)]
                        if i == 1:
                            pe.wait_ge(o8_taken, q + 1)
                        else:
                            pe.wait_ge(sc_taken, SETS * q + i - 1)
                    for c in range(NCH):
                        for h in range(HG):
                            last = nc.tensor.matmul(pm[:, 2 * (i % 2) + c, h * CH:(h + 1) * CH], lhs[c][h], rhs[c][h],
                                                    start=True, stop=True)
                    last.then_inc(sc_psum, 1)
                    fill(f"lv{q}_{i}")
                pe.wait_ge(fac_ready, (LEVELS + 2) * q + LEVELS + 1)
                pe.wait_ge(sc_taken, SETS * q + SETS - 1)
                for c in range(NCH):
                    for h in range(HG):
                        last = turn(pm[:, c, h * P:(h + 1) * P], fac[:, 1, h, c * CH:(c + 1) * CH], P)
                last.then_inc(kd_psum, 1)
                fill(f"kd{q}")
                pe.wait_ge(kd_ready, q + 1)
                pe.wait_ge(sc_taken, SETS * (q + 1))
                for h in range(HG):
                    o = h * dv
                    last = nc.tensor.matmul(pm[:, 2 + o // 512, o % 512:o % 512 + dv], kdT[:, 0, h * DK:(h + 1) * DK],
                                            vt[:, 0, o:o + dv], start=True, stop=True)
                last.then_inc(s1_psum, 1)
                for h in range(HG):
                    o = h * dv
                    last = nc.tensor.matmul(pm[:, o // 512, o % 512:o % 512 + dv], kdT[:, 1, h * DK:(h + 1) * DK],
                                            vt[:, 1, o:o + dv], start=True, stop=True)
                last.then_inc(kv1_psum, 1)
                pe.wait_ge(s1_ready, q + 1)
                pe.wait_ge(fac_ready, (LEVELS + 2) * (q + 1))
                for jj in range(nv // 2):
                    b0 = 2 if jj % 2 == 0 else 0
                    if jj == 1:
                        pe.wait_ge(s2_ready, q + 1)
                    if jj >= 2:
                        pe.wait_ge(o_ready, OPAIRS[q] + jj - 1)
                    for m in range(2):
                        j = 2 * jj + m
                        h = j * P // dv
                        nc.tensor.matmul(pm[:, b0 + m, 0:CH], vt[:, 0, j * P:(j + 1) * P], scores[:, 0, h, :], start=True, stop=True)
                        nc.tensor.matmul(pm[:, b0 + m, CH:TP], vt[:, 1, j * P:(j + 1) * P], scores[:, 1, h, :], start=True, stop=False)
                        last = nc.tensor.matmul(pm[:, b0 + m, CH:TP], s1[:, j * P:(j + 1) * P], fac[:, 0, h, 0:CH], start=False, stop=True)
                    last.then_inc(o_psum, 1)
                    fill(f"o{q}_{jj}")

            recurrence(0)
            pe.wait_ge(past_taken, 1)
            pe.wait_ge(o_ready, OPAIRS[1])
            for g in range(4):
                pe.wait_ge(pool_d, g + 1)
                if g >= 2:
                    pe.wait_ge(pool_taken, g - 1)
                for e in range(2):
                    for c in range(2):
                        last = nc.tensor.matmul(pm[:, 2 * (g % 2) + e, 0:T], pool_w[:, g, c, e * P:(e + 1) * P],
                                                z[:, 32 + 2 * g + c, :], start=(c == 0), stop=(c == 1))
                last.then_inc(pool_psum, 1)
            fill("pool")
            pe.wait_ge(pool_taken, 4)
            pe.wait_ge(osq_ready, 1)
            for h in range(HG):
                for m in range(2):
                    last = nc.tensor.matmul(pm[:, h, 0:T], ones[:, :], z[:, 2 * h + m, :], start=(m == 0), stop=(m == 1))
            last.then_inc(oss_psum, 1)
            fill("oss")
            fill_end("ada0b")

            def mix_wait(n):
                return lambda u: pe.wait_ge(mix_ready, 4 * n + (3 if u == 0 else 4))

            pe.wait_ge(mod_ready, PLAN["up0_0"][3])
            gemm(8, PLAN["out0"][2], h_hi, h_lo, mix_wait(0), norm=8)

            def mlp_layer(l, hw, norms):
                _, _, g0, a0 = PLAN["up0_0" if l == 0 else "up1_0"]

                def chunk(f, norm):
                    g, a = g0 + CHUNK_GROUPS[l] * f, a0 + 4 * f

                    def hidden(u):
                        pe.wait_ge(hid_ready, 8 * (FF_CHUNKS * l + f) + (2 * (u + 1) + 1))

                    if l == 0:
                        mixed(a, g, h_hi, h_lo, hw)
                        mixed(a + 2, g + 10, f_hi, f_lo, hidden, norm=norm)
                    else:
                        gemm(8, g, h_hi, h_lo, hw)
                        gemm(8, g + 8, f_hi, f_lo, hidden, norm=norm)

                with pe.Fori(0, FF_CHUNKS - 1) as f:
                    chunk(f, None)
                chunk(FF_CHUNKS - 1, norms)

            mlp_layer(0, h_wait(1), 16)
            pe.wait_ge(rstd_ready, 3)
            pe.wait_ge(aw_in, 64)
            for j in range(8):
                last = turn(pm[:, 0, j * TAPS:(j + 1) * TAPS], cw_rows[:, j * P:(j + 1) * P], TAPS)
            last.then_inc(cw_psum, 1)
            gemm(8, PLAN["glu"][2], h_hi, h_lo, h_wait(2))
            gemm(16, PLAN["in1"][2], h_hi, h_lo, h_wait(2))
            pe.wait_ge(evacuated, PLAN["in1"][2] + 16)
            pe.wait_ge(conv_step, 1)
            for j in range(8):
                last = turn(pm[0:CONV_TAIL, 2 + j // 4, (j % 4) * P:(j % 4 + 1) * P],
                            z[:, 32 + j, T - CONV_TAIL:T], P)
            last.then_inc(tail_psum, 1)
            pe.wait_ge(past_in, 32)
            for j in range(8):
                if j >= 2:
                    pe.wait_ge(past_taken, j)
                for a in range(2):
                    last = turn(pm[:, j % 2, a * 120:(a + 1) * 120], pastc[:, a, j * P:(j + 1) * P], 120)
                last.then_inc(past_psum, 1)
            pe.wait_ge(cv_done, 1)
            for j in range(8):
                last = nc.tensor.matmul(pm[:, 0, 0:T], ones[:, :], z[:, 40 + j, :], start=(j == 0), stop=(j == 7))
            last.then_inc(ln_psum, 1)
            fill("ln1")
            pe.wait_ge(ln_sq, 1)
            for j in range(8):
                last = nc.tensor.matmul(pm[:, 1, 0:T], ones[:, :], z[:, 32 + j, :], start=(j == 0), stop=(j == 7))
            last.then_inc(ln_psum, 1)
            fill("ln2")
            pe.wait_ge(ln_rstd, 1)
            pe.wait_ge(tail_ready, 2)
            recurrence(1)
            pe.wait_ge(o_ready, OPAIRS[2])
            fill("gates2")
            recurrence(2)
            pe.wait_ge(o_ready, OPAIRS[3])
            pe.wait_ge(osq_ready, 2)
            for r in range(2):
                if r:
                    pe.wait_ge(ors_ready, 2)
                for h in range(4):
                    last = nc.tensor.matmul(pm[:, h, 0:T], ones[:, :], z[:, 4 * r + h, :], start=True, stop=True)
                last.then_inc(oss_psum, 1)
            fill("oss1")
            fill_end("ada1b")
            pe.wait_ge(mod_ready, 96)
            gemm(8, PLAN["out1"][2], h_hi, h_lo, mix_wait(1), norm=24)
            mlp_layer(1, h_wait(3), 32)
            for r in range(3):
                for b in range(4):
                    i = 4 * r + b
                    if r == 0:
                        pe.wait_ge(y_ready, 4 * b + 4)
                    if i >= 4:
                        pe.wait_ge(y_taken, i - 3)
                    for m in range(4):
                        k = 4 * b + m
                        if r < 2:
                            last = turn(pm[:, b, m * P:(m + 1) * P], x[:, k, r * P:(r + 1) * P], P)
                        else:
                            last = turn(pm[0:NS, b, m * P:(m + 1) * P], x[:, k, TP:T], P)
                    last.then_inc(y_psum, 1)

        @block.scalar
        def _(act):
            steps = Count()

            def step(ins):
                ins.then_inc(act_step, 1)
                act.wait_ge(act_step, steps.next())

            def hi(g, u, p):
                if u % 2 == 0:
                    act.wait_ge(raw_in[p][u // 2], 8 * (g - p) + 16)
                if not isinstance(g, int) or g:
                    act.wait_ge(split_used, NU * g + u - (NU - 1))
                nc.scalar.activation(w_hi[:, u, :], raw[:, p, u, :], ACT.Copy).then_inc(hi_ready, 1)

            def split(g, p):
                for u in range(NU):
                    hi(g, u, p)

            def hi_phase(count, g, after=None, last_next=None):
                def body(i, p, nxt):
                    if nxt is not None:
                        split(nxt, 1 - p)
                    if after:
                        after(i, p)

                with act.Fori(0, count // 2 - 1) as j:
                    for p in range(2):
                        body(2 * j + p, p, g + 2 * j + (p + 1))
                body(count - 2, 0, g + (count - 1))
                body(count - 1, 1, last_next)

            def mixed(g, after, last_next):
                split(g + 1, 1)
                if after:
                    after(0, 0)
                split(g + 2, 0)
                split(g + 3, 1)
                if after:
                    after(1, 1)
                split(g + 4, 0)
                for i in range(2, 8):
                    split(g + (i + 3) if i < 7 else last_next, (i + 1) % 2)
                    if after:
                        after(i, i % 2)

            filled_in = Count()

            def units(point):
                return [(PLAN[name][2] + j, u, j % 2) for name, j in fills(filled_in, point) for u in range(NU)]

            def fill(point, between=None):
                todo = units(point)
                for g, u, p in todo[:2]:
                    hi(g, u, p)
                if between:
                    between()
                for g, u, p in todo[2:]:
                    hi(g, u, p)

            def square(norm, x0):
                def f(i, p):
                    act.wait_ge(x_ready, x0 + i + 2)
                    act.wait_ge(ss_done, norm + i - 1)
                    k = 2 * i
                    nc.scalar.activation(sq[:, p, :, :], x[:, bass.ds(k, 2), :], ACT.Square).then_inc(sq_ready, 1)
                return f

            def rms(r, sums, tail_only=False):
                act.wait_ge(ss_done, sums)
                step(nc.scalar.activation(lnv[:, :], pm[:, 0, 0:T], ACT.Ln, bias=eps_t[:, :], scale=1.0 / D))
                nc.scalar.activation(rstd[:, :], lnv[:, :], ACT.Exp, scale=-0.5).then_inc(rstd_ready, 1)

            def modulate(r, l, sh):
                act.wait_ge(t8_ready, r + 1)
                nc.scalar.activation(h_hi[:, :, TP:T], t8[:, :, :], ACT.Copy).then_inc(h8_hi, 1)
                for k in range(KT):
                    act.wait_ge((hs_even, hs_odd)[k % 2], KT // 2 * r + k // 2 + 1)
                    nc.scalar.activation(h_hi[:, k, 0:TP], hs[:, k % 4, :], ACT.Identity,
                                         bias=mod[:, l, sh + k, 0:1]).then_inc(hh_ready, 1)

            act.wait_ge(c_in, 32)
            nc.scalar.activation(cs_rows[:, :], c_rows[:, :], ACT.Silu).then_inc(c_silu, 1)
            act.preload_act_table_set("natural_log_exp_and_others")
            act.wait_ge(tr_ready, 1)
            nc.scalar.activation(c_hl[:, 0:KT * CW].rearrange("p (k n) -> p k n", n=CW)[:, :, 0:NC],
                                 pm[:, 1, 0:KT * NC].rearrange("p (k n) -> p k n", n=NC), ACT.Copy).then_inc(c_high, 1)
            split(0, 0)
            split(1, 1)
            for r in range(5):
                if r < 4:
                    split(2 + r, r % 2)
                for i in (2 * r - 2, 2 * r - 1) if r else ():
                    act.wait_ge(tr_taken, 2 + 2 * i + 2)
                    if i >= 2:
                        act.wait_ge(ss_done, i - 1)
                    nc.scalar.activation(sq[:, i % 2, :, :], x[:, 2 * i:2 * i + 2, :], ACT.Square).then_inc(sq_ready, 1)
            rms(0, 8)
            act.wait_ge(filled, 2)
            nc.scalar.activation(sm[:, :], lb[:, :], ACT.Exp).then_inc(lb_exp, 1)
            with act.Fori(0, PLAN["ada0a"][1] // 2 - 3) as j:
                for p in range(2):
                    split(2 * j + (6 + p), p)
            g0 = PLAN["in0"][2]
            split(g0, 0)
            modulate(0, 0, SH1)
            act.wait_ge(aw_in, 48)
            act.wait_ge(filled, 3)
            nc.scalar.activation(a_hi[:, 0:KT * 16], a_w[:, :, :].rearrange("p k n -> p (k n)"), ACT.Copy).then_inc(aw_hi, 1)
            hi_phase(12, g0, last_next=g0 + 12)
            act.wait_ge(gz_ready, 2)
            step(nc.scalar.activation(gl[:, :, :], gl[:, :, :], ACT.Exp))
            nc.scalar.activation(gl[:, :, :], gl[:, :, :], ACT.Ln, bias=1.0).then_inc(gl_ready, 1)
            hi_phase(4, g0 + 12)
            fill("gate")
            act.wait_ge(evacuated, g0 + 16)
            nc.scalar.activation(z[:, 0:4, :], z[:, 0:4, :], ACT.Copy, scale=float(DK) ** -0.5).then_inc(q_scaled, 1)
            act.wait_ge(tail_psum, 1)
            nc.scalar.activation(tail[0:POOL_TAIL, :].rearrange("p (a n) -> p a n", a=2), pm[0:POOL_TAIL, 2:4, :],
                                 ACT.Copy).then_inc(tail_ready, 1)
            fill("past")

            def recurrence(q):
                hd = HEADS[q]
                nv, dv, zq, zk, zv = hd["nv"], hd["dv"], hd["q"], hd["k"], hd["v"]
                vt = vT[hd["layer"]]
                nb = nv // 4
                act.wait_ge(logp_ready, q + 1)
                nc.scalar.activation(decay8[:, :, :], logp[:, :, TP:T], ACT.Exp).then_inc(dec8_ready, 1)
                for c in range(NCH):
                    act.wait_ge(vtr_psum, 4 * q + c + 1)
                    nc.scalar.activation(vt[:, c, 0:nv * P].rearrange("p (a n) -> p a n", n=512),
                                         pm[:, c * nb:(c + 1) * nb, :], ACT.Copy).then_inc(vtr_ready, 1)
                act.wait_ge(vtr_psum, 4 * q + 3)
                nc.scalar.activation(v8[:, 0:nv * P].rearrange("p (a n) -> p a n", n=512), pm[0:NS, 0:nb, :],
                                     ACT.Copy).then_inc(vtr_ready, 1)
                act.wait_ge(vtr_psum, 4 * q + 4)
                nc.scalar.activation(k8[:, :], pm[0:NS, 2, :], ACT.Copy).then_inc(vtr_ready, 1)
                act.wait_ge(vtr_ready, 4 * q + 4)
                fill(f"vt{q}")
                for b in range(NS):
                    if b >= 2:
                        act.wait_ge(kv_psum, NS * q + b - 1)
                    nc.scalar.activation(kmask[:, b % 2, :], k8[:, :], ACT.Copy,
                                         scale=ident[0:NS, b:b + 1]).then_inc(kmask_ready, 1)
                    if b:
                        fill(f"kv{q}_{b - 1}")
                fill(f"kv{q}_{NS - 1}")
                def decays(lv):
                    if lv == LEVELS:
                        act.wait_ge(end_ready, q + 1)
                        nc.scalar.activation(dec[:, 1, :, :], dec[:, 1, :, :], ACT.Exp).then_inc(exp_ready, 1)
                        return
                    act.wait_ge(dif_ready, LEVELS * q + lv + 1)
                    w = 1 << lv
                    dl, dr = halves(dec[:, lv % 2, :, :], w)
                    _, pr = halves(logp[:, :, 0:TP], w)
                    nc.scalar.activation(dr, pr, ACT.Exp)
                    nc.scalar.activation(dl, dl, ACT.Exp).then_inc(exp_ready, 1)

                decays(0)
                fill(f"lv{q}_0")
                decays(1)
                for lv in range(1, LEVELS):
                    fill(f"lv{q}_{lv}", lambda: decays(lv + 1))
                act.wait_ge(fac_ready, (LEVELS + 2) * q + LEVELS)
                act.wait_ge(right_ready, LEVELS * (q + 1))
                nc.scalar.activation(dec[:, 0, :, 0:CH], logp[:, :, CH:TP], ACT.Exp).then_inc(exp_ready, 1)
                fill(f"lv{q}_{LEVELS}")
                act.wait_ge(kd_psum, q + 1)
                nc.scalar.activation(kdT[:, :, :], pm[:, 0:2, :], ACT.Copy).then_inc(kd_ready, 1)
                fill(f"kd{q}")
                act.wait_ge(s1_psum, q + 1)
                nc.scalar.activation(s1[:, 0:nv * P].rearrange("p (a n) -> p a n", n=512), pm[:, 2:2 + nb, :],
                                     ACT.Copy).then_inc(s1_ready, 1)
                for jj in range(nv // 2):
                    b0 = 2 if jj % 2 == 0 else 0
                    act.wait_ge(o_psum, OPAIRS[q] + jj + 1)
                    nc.scalar.activation(z[:, zv + 2 * jj:zv + 2 * jj + 2, 0:TP], pm[:, b0:b0 + 2, 0:TP],
                                         ACT.Copy).then_inc(o_ready, 1)
                    fill(f"o{q}_{jj}")

            def mix_high(n, batches):
                for i, (dst, src) in enumerate(batches):
                    if i >= 2:
                        act.wait_ge(mix_f32, n + i - 1)
                    nc.scalar.activation(h_hi[:, dst:dst + 4, :], z[:, src:src + 4, :], ACT.Copy).then_inc(mix_hi, 1)

            recurrence(0)
            for g in range(4):
                act.wait_ge(pool_psum, g + 1)
                for e in range(2):
                    j = 2 * g + e
                    last = nc.scalar.activation(z[:, 40 + j, :], pm[:, 2 * (g % 2) + e, 0:T], ACT.Copy,
                                                scale=vb[:, VB["ev_pool_scale"] + j:VB["ev_pool_scale"] + j + 1])
                last.then_inc(pool_taken, 1)
            act.wait_ge(o_ready, OPAIRS[1])
            act.wait_ge(o8_taken, 1)
            nc.scalar.activation(z[:, 0:8, :], z[:, 8:16, :], ACT.Square).then_inc(osq_ready, 1)
            fill("pool")
            act.wait_ge(oss_psum, 1)
            act.wait_ge(o_ready, OPAIRS[1])
            step(nc.scalar.activation(logp[:, :, :], pm[:, :, 0:T], ACT.Ln, bias=eps_t[:, :], scale=1.0 / 256))
            nc.scalar.activation(logp[:, :, :], logp[:, :, :], ACT.Exp, scale=-0.5).then_inc(ors_ready, 1)
            nc.scalar.activation(z[:, 16:24, :], z[:, 16:24, :], ACT.Silu).then_inc(silu_ready, 1)
            act.preload_act_table_set("natural_log_exp_and_others")
            fill("oss")
            act.wait_ge(pool_taken, 4)
            act.wait_ge(s2_ready, 1)
            act.wait_ge(small_out, 16 * 5)
            mix_high(0, [(8, 40), (12, 44), (0, 8), (4, 12)])
            g1 = PLAN["out0"][2]
            split(g1, 0)
            a1 = PLAN["up0_0"][2]
            hi_phase(8, g1, after=square(8, 0), last_next=a1)
            rms(1, 16)
            modulate(1, 0, SH2)

            def mlp_layer(l, norm, x0, after_next):
                g0 = PLAN["up0_0" if l == 0 else "up1_0"][2]

                def chunk(f, after, next_up):
                    g = g0 + CHUNK_GROUPS[l] * f
                    if l == 0:
                        mixed(g, None, g + 10)
                        mixed(g + 10, after, g + 20 if next_up else after_next)
                    else:
                        hi_phase(8, g, last_next=g + 8)
                        hi_phase(8, g + 8, after=after, last_next=g + 16 if next_up else after_next)

                with act.Fori(0, FF_CHUNKS - 1) as f:
                    chunk(f, None, True)
                chunk(FF_CHUNKS - 1, square(norm, x0), False)

            mlp_layer(0, 16, 32, PLAN["glu"][2])
            rms(2, 24)
            g2 = PLAN["glu"][2]
            modulate(2, 1, SH1)
            hi_phase(8, g2, last_next=g2 + 8)
            act.wait_ge(evacuated, g2 + 8)
            nc.scalar.activation(z[:, 40:48, :], z[:, 40:48, :], ACT.Sigmoid).then_inc(gb_sig, 1)
            act.preload_act_table_set("natural_log_exp_and_others")
            g3 = PLAN["in1"][2]

            def z_evac(i, p):
                act.wait_ge(split_used, NU * (g3 + i) + NU)
                off = 2 * i * T
                nc.scalar.activation(zf[:, bass.ds(off, MT * T)].rearrange("p (a t) -> p a t", a=MT), bank2(p),
                                     ACT.Copy).then_inc(evacuated, 1)

            hi_phase(16, g3, after=z_evac)
            act.wait_ge(tail_psum, 2)
            nc.scalar.activation(tail[0:CONV_TAIL, :].rearrange("p (a n) -> p a n", a=2), pm[0:CONV_TAIL, 2:4, :],
                                 ACT.Copy).then_inc(tail_ready, 1)

            def sigmoids(q):
                zk = HEADS[q]["k"]
                nc.scalar.activation(logp[:, :, :], z[:, zk:zk + 4, :], ACT.Sigmoid)
                nc.scalar.activation(z[:, zk:zk + 4, :], z[:, zk:zk + 4, :], ACT.Sigmoid, scale=-1.0).then_inc(sig_ready, 1)
                act.preload_act_table_set("natural_log_exp_and_others")

            def logs(q):
                act.wait_ge(ln_in, q)
                nc.scalar.activation(gz[:, :, :], gz[:, :, :], ACT.Ln)
                nc.scalar.activation(logp[:, :, :], logp[:, :, :], ACT.Ln).then_inc(ln_out, 1)

            act.wait_ge(evacuated, g3 + 16)
            sigmoids(1)
            logs(1)
            act.wait_ge(ln_psum, 1)
            nc.scalar.activation(mean[:, :], pm[:, 0, 0:T], ACT.Copy, scale=1.0 / 1024).then_inc(ln_mean, 1)
            act.wait_ge(ln_cent, 1)
            act.wait_ge(tail_psum, 2)
            nc.scalar.activation(z[:, 32:40, :], z[:, 40:48, :], ACT.Square).then_inc(ln_sq, 1)
            fill("ln1")
            act.wait_ge(ln_psum, 2)
            step(nc.scalar.activation(lnv[:, :], pm[:, 1, 0:T], ACT.Ln, bias=eps_t[:, :], scale=1.0 / 1024))
            nc.scalar.activation(rstd[:, :], lnv[:, :], ACT.Exp, scale=-0.5).then_inc(ln_rstd, 1)
            fill("ln2")
            act.wait_ge(ln_done, 1)
            nc.scalar.activation(z[:, 40:48, :], z[:, 40:48, :], ACT.Silu).then_inc(cv_ready, 1)
            act.wait_ge(evacuated, g3 + 16)
            nc.scalar.activation(z[:, 24:32, :], z[:, 24:32, :], ACT.Silu).then_inc(silu_ready, 1)
            act.preload_act_table_set("natural_log_exp_and_others")
            recurrence(1)
            act.wait_ge(dec8_ready, 2)
            act.wait_ge(exp_ready, (LEVELS + 2) * 2)
            act.wait_ge(s2_ready, 2)
            sigmoids(2)
            logs(2)
            fill("gates2")
            recurrence(2)
            act.wait_ge(o_ready, OPAIRS[3])
            act.wait_ge(o8_taken, 3)
            nc.scalar.activation(z[:, 0:8, :], z[:, 16:24, :], ACT.Square).then_inc(osq_ready, 1)
            for r in range(2):
                act.wait_ge(oss_psum, 2 + r)
                rs = z[:, 8 + 4 * r:12 + 4 * r, :]
                step(nc.scalar.activation(rs, pm[:, :, 0:T], ACT.Ln, bias=eps_t[:, :], scale=1.0 / 128))
                nc.scalar.activation(rs, rs, ACT.Exp, scale=-0.5).then_inc(ors_ready, 1)
            fill("oss1")
            act.wait_ge(cv_ready, 1)
            act.wait_ge(s2_ready, 3)
            act.wait_ge(small_out, 16 * SMALL_OUTS)
            mix_high(2, [(8, 40), (12, 44), (0, 16), (4, 20)])
            g4 = PLAN["out1"][2]
            split(g4, 0)
            hi_phase(8, g4, after=square(24, 40), last_next=g4 + 8)
            rms(3, 32)
            modulate(3, 1, SH2)
            mlp_layer(1, 32, 72, None)
            rms(4, 40)
            for r in range(3):
                for b in range(4):
                    act.wait_ge(y_psum, 4 * r + b + 1)
                    rows, dst = (P, y_rows[:, r, b * 512:(b + 1) * 512]) if r < 2 else (NS, ys_rows[:, b * 512:(b + 1) * 512])
                    nc.scalar.activation(dst, pm[0:rows, b, :], ACT.Copy).then_inc(y_taken, 1)

        @block.vector
        def _(dve):
            steps = Count()

            def step(ins):
                ins.then_inc(dve_step, 1)
                dve.wait_ge(dve_step, steps.next())

            def lo(n, u, p):
                dve.wait_ge(hi_ready, NU * n + (u + 1))
                nc.vector.tensor_tensor(w_lo[:, u, :], raw[:, p, u, :], w_hi[:, u, :].bitcast(F32),
                                        ALU.subtract).then_inc(lo_ready, 1)

            def split(n, p, work=None):
                for u in range(NU):
                    lo(n, u, p)
                    if work:
                        work(u)

            def lo_phase(count, n, evac, last_next=None, loop_work=None):
                def body(i, p, nxt, work=None):
                    if nxt is not None:
                        split(nxt, 1 - p, work)
                    elif work:
                        for u in range(NU):
                            work(u)
                    if evac:
                        evac(i, p, n + i)

                def work(j, p):
                    return (lambda s: loop_work(j, NU * p + s)) if loop_work else None

                with dve.Fori(0, count // 2 - 1) as j:
                    for p in range(2):
                        i = 2 * j + p
                        body(i, p, n + i + 1, work(j, p))
                i = count - 2
                body(i, 0, n + i + 1, work(i // 2, 0))
                body(i + 1, 1, last_next, work(i // 2, 1))

            def mixed(a, n, evac, last_next):
                def rest(g):
                    for u in range(1, NU):
                        lo(g, u, 0)

                split(n + 1, 1)
                evac(0, 0, n, lambda: lo(n + 2, 0, 0))
                rest(n + 2)
                ada_rows(n + 1, 1)
                split(n + 3, 1)
                ada_add(a, 1)
                evac(1, 0, n + 2, lambda: lo(n + 4, 0, 0))
                rest(n + 4)
                ada_rows(n + 3, 1)
                split(n + 5, 1, lambda u: ada_add(a + 1, 1) if u == NU - 2 else None)
                evac(2, 0, n + 4)
                for i in range(3, 8):
                    split(n + (i + 3) if i < 7 else last_next, (i + 1) % 2)
                    evac(i, i % 2, n + (i + 2))

            def ada_rows(g, p):
                dve.wait_ge(split_used, NU * g + NU)
                nc.vector.tensor_copy(mod_rows[:, p, :], ps[0:CW, MT * p, 0:GC]).then_inc(evacuated, 1)

            def ada_add(a, p):
                dve.wait_ge(turned, a + 1)
                nc.vector.tensor_tensor(modf[:, bass.ds(2 * a, 2), :],
                                        ps[:, MT * p + 1, 0:MT * NC].rearrange("p (m n) -> p m n", n=NC),
                                        badaf[:, bass.ds(2 * a, 2)].unsqueeze(2).broadcast_to([P, 2, NC]),
                                        ALU.add).then_inc(mod_ready, 1)

            def ada_group(a, g, p, before=2):
                split(g, p)
                if before:
                    ada_rows(g - 1, 1 - p)
                if before > 1:
                    ada_add(a - 2, p)

            def ada_end(a, g):
                ada_rows(g - 1, 1)
                ada_add(a - 2, 0)
                ada_add(a - 1, 1)

            filled_in = Count()

            def fill(point):
                for name, j in fills(filled_in, point):
                    _, count, g0, a0 = PLAN[name]
                    ada_group(a0 + j, g0 + j, j % 2, before=min(j, 2))

            def fill_end(name):
                _, count, g0, a0 = PLAN[name]
                ada_end(a0 + count, g0 + count)

            modf = mod[:, :, :, :].rearrange("p l m n -> p (l m) n")
            badaf = bada[:, :, :].rearrange("p l m -> p (l m)")

            def z_evac(z0):
                def f(i, p, g):
                    dve.wait_ge(split_used, NU * g + NU)
                    off = (z0 + 2 * i) * T
                    nc.vector.tensor_copy(zf[:, bass.ds(off, MT * T)].rearrange("p (a t) -> p a t", a=MT),
                                          bank2(p)).then_inc(evacuated, 1)
                return f

            def up_evac(h):
                def f(i, p, g, between=None):
                    dve.wait_ge(split_used, NU * g + NU)
                    dve.wait_ge(hid_ready, h + i + 1)
                    nc.vector.tensor_scalar(hid[:, :, :], bank2(p), 0.0, None, ALU.max).then_inc(evacuated, 1)
                    dve.wait_ge(evacuated, g + 1)
                    if between:
                        between()
                    nc.vector.tensor_tensor(hid[:, :, :], hid[:, :, :], hid[:, :, :], ALU.mult).then_inc(hid_sq, 1)
                    dve.wait_ge(hid_sq, h + i + 1)
                    k = 2 * i
                    nc.vector.tensor_copy(f_hi[:, bass.ds(k, 2), :], hid[:, :, :]).then_inc(hid_hi, 1)
                    dve.wait_ge(hid_hi, h + i + 1)
                    nc.vector.tensor_tensor(f_lo[:, bass.ds(k, 2), :], hid[:, :, :],
                                            f_hi[:, bass.ds(k, 2), :].bitcast(F32), ALU.subtract).then_inc(hid_ready, 1)
                return f

            def res_evac(r, l, gate):
                def f(i, p, g, between=None):
                    dve.wait_ge(split_used, NU * g + NU)
                    dve.wait_ge(x_ready, r + i + 1)
                    k = 2 * i
                    nc.vector.tensor_tensor(g8[:, :, :], bank2(p)[:, :, TP:T], mod[:, l, bass.ds(gate + k, 2), 1:NC],
                                            ALU.mult).then_inc(gate8_done, 1)
                    for m in range(MT):
                        xa = x[:, bass.ds(k + m, 1), 0:TP].rearrange("p a t -> p (a t)")
                        ga = mod[:, l, bass.ds(gate + k + m, 1), 0:1].rearrange("p a t -> p (a t)")
                        last = nc.vector.scalar_tensor_tensor(xa, ps[:, MT * p + m, 0:TP], ga, xa, ALU.mult, ALU.add)
                    last.then_inc(evacuated, 1)
                    dve.wait_ge(gate8_done, r + i + 1)
                    x8 = x[:, bass.ds(k, 2), TP:T]
                    nc.vector.tensor_tensor(x8, x8, g8[:, :, :], ALU.add).then_inc(x_ready, 1)
                    if between:
                        between()
                return f

            def gains(r, l, norm0, sc):
                nc.vector.scalar_tensor_tensor(
                    amod[:, :, :], mod[:, l, sc:sc + KT, :], 1.0,
                    va[:, norm0:norm0 + KT].unsqueeze(2).broadcast_to([P, KT, NC]), ALU.add, ALU.mult).then_inc(amod_ready, 1)
                dve.wait_ge(amod_ready, r + 1)

            def modulate(r, l, sh):
                dve.wait_ge(rstd_ready, r + 1)
                step(nc.vector.tensor_tensor(t8[:, :, :], x[:, :, TP:T], amod[:, :, 1:NC], ALU.mult))
                step(nc.vector.tensor_tensor(t8[:, :, :], t8[:, :, :],
                                             rstd[:, TP:T].unsqueeze(1).broadcast_to([P, KT, NS]), ALU.mult))
                nc.vector.tensor_tensor(t8[:, :, :], t8[:, :, :], mod[:, l, sh:sh + KT, 1:NC], ALU.add).then_inc(t8_ready, 1)

                def scale(k):
                    if k % 2:
                        return
                    nc.vector.scalar_tensor_tensor(hs[:, k % 4, :], x[:, k, 0:TP], amod[:, k, 0:1], rstd[:, 0:TP],
                                                   ALU.mult, ALU.mult).then_inc(hs_even, 1)

                def low(k):
                    dve.wait_ge(hh_ready, KT * r + k + 1)
                    nc.vector.scalar_tensor_tensor(h_lo[:, k, 0:TP], hs[:, k % 4, :], mod[:, l, sh + k, 0:1],
                                                   h_hi[:, k, 0:TP].bitcast(F32), ALU.add, ALU.subtract).then_inc(h_ready, 1)

                for k in range(3):
                    scale(k)
                dve.wait_ge(h8_hi, r + 1)
                nc.vector.tensor_tensor(h_lo[:, :, TP:T], t8[:, :, :], h_hi[:, :, TP:T].bitcast(F32), ALU.subtract)
                for k in range(KT):
                    low(k)
                    if k + 3 < KT:
                        if k:
                            dve.wait_ge(h_ready, KT * r + k)
                        scale(k + 3)

            nc.vector.memset(ones[:, :], 1.0)
            nc.vector.memset(zero[:, :], 0.0)
            nc.vector.memset(c_hl[:, KT * CW:].bitcast(F32), 0.0)
            nc.vector.memset(eps_t[:, :], EPS).then_inc(filled, 1)
            nc.vector.memset(hid[:, :, :], 0.0).then_inc(hid_ready, 1)
            nc.vector.memset(g8[:, :, :], 0.0).then_inc(x_ready, 1)
            dve.wait_ge(c_high, 1)
            c_parts = c_hl[:, 0:KT * CW].rearrange("p (k n) -> p k n", n=CW)
            nc.vector.tensor_tensor(c_parts[:, :, NC:CW], pm[:, 1, 0:KT * NC].rearrange("p (k n) -> p k n", n=NC),
                                    c_parts[:, :, 0:NC].bitcast(F32), ALU.subtract).then_inc(tr_taken, 1)
            nc.vector.tensor_tensor(sel[:, :], ident[0:CW, 0:NC], ident[0:CW, NC:CW], ALU.add)
            ada_group(0, 0, 0, before=0)
            ada_group(1, 1, 1, before=1)
            dve.wait_ge(tr_ready, 2)
            nc.vector.tensor_copy(va[:, :], pm[:, 0, 0:80])
            nc.vector.tensor_copy(vb[:, :], pm[:, 0, 80:80 + VB_ROWS])
            nc.vector.tensor_copy(bada[:, :, :], pm[:, 0, 128:320].rearrange("p (l m) -> p l m", l=2)).then_inc(tr_taken, 1)
            for r in range(4):
                for k in range(4 * r, 4 * r + 4):
                    dve.wait_ge(tr_ready, 3 + k)
                    nc.vector.tensor_copy(x[:, k, :], pm[:, 1 + k % 3, 0:T]).then_inc(tr_taken, 1)
                ada_group(2 + r, 2 + r, r % 2)
            dve.wait_ge(masks_in, 32)
            nc.vector.tensor_copy(masks[:, :, :], mask_rows[:, :, :])
            dve.wait_ge(tr_taken, 2)
            raw_lb = vb[:, VB["od_lb_raw"]:VB["od_lb_raw"] + 8]
            nc.vector.tensor_tensor(lb[:, :], raw_lb, raw_lb, ALU.subtract).then_inc(filled, 1)
            dve.wait_ge(lb_exp, 1)
            step(nc.vector.reciprocal(oml[:, :], sm[:, :]))
            step(nc.vector.tensor_tensor(sm[:, :], sm[:, :], oml[:, :], ALU.mult))
            step(nc.vector.tensor_tensor(lb[:, :], sm[:, :], sm[:, :], ALU.subtract))
            step(nc.vector.tensor_scalar(oml[:, :], lb[:, :], -1.0, 1.0, ALU.mult, ALU.add))
            count = PLAN["ada0a"][1]
            with dve.Fori(0, count // 2 - 3) as j:
                for p in range(2):
                    ada_group(2 * j + (6 + p), 2 * j + (6 + p), p)
            ada_end(count, count)
            dve.wait_ge(mod_ready, count)
            gains(0, 0, VA["norm_mix"], SC1)
            n0 = PLAN["in0"][2]
            split(n0, 0)
            modulate(0, 0, SH1)
            dve.wait_ge(h_ready, KT)
            nc.vector.memset(a_hi[:, KT * 16:AW].bitcast(F32), 0.0)
            nc.vector.memset(a_lo[:, KT * 16:AW].bitcast(F32), 0.0).then_inc(filled, 1)
            dve.wait_ge(aw_hi, 1)
            nc.vector.tensor_tensor(a_lo[:, 0:KT * 16], a_w[:, :, :].rearrange("p k n -> p (k n)"),
                                    a_hi[:, 0:KT * 16].bitcast(F32), ALU.subtract).then_inc(aw_lo, 1)
            lo_phase(12, n0, z_evac(0), last_next=n0 + 12)
            dve.wait_ge(alr_psum, 1)
            nc.vector.tensor_copy(a_lr[:, :], pm[0:16, 0, 0:T]).then_inc(alr_ready, 1)
            dve.wait_ge(gate_psum, 1)
            b0 = VB["ev_b_gate"]
            for h in range(HG):
                last = nc.vector.tensor_scalar(logp[:, h, :], pm[:, h, 0:T], vb[:, b0 + h:b0 + h + 1], None, ALU.add)
            last.then_inc(gz_ready, 1)
            dve.wait_ge(gz_ready, 1)
            gzf = gz[:, :, :].rearrange("p h t -> p (h t)")
            glf = gl[:, :, :].rearrange("p h t -> p (h t)")
            lpf = logp[:, :, :].rearrange("p h t -> p (h t)")
            nc.vector.scalar_tensor_tensor(glf, lpf, -1.0, lpf, ALU.mult, ALU.min).then_inc(gz_ready, 1)
            lo_phase(4, n0 + 12, z_evac(24))
            dve.wait_ge(gl_ready, 1)
            step(nc.vector.scalar_tensor_tensor(lpf, lpf, 0.0, glf, ALU.min, ALU.subtract))
            nc.vector.tensor_scalar(lpf, lpf, 1.0 / 16.0, None, ALU.mult).then_inc(logp_ready, 1)
            fill("gate")
            dve.wait_ge(past_psum, 1)
            dve.wait_ge(evacuated, PLAN["in0"][2] + 16)
            for g, w in enumerate(WINDOWS):
                b = g // 2
                c0 = (g % 2) * 240
                past = pm[:, b, c0:c0 + 240].rearrange("p (j b r) -> p j b r", j=2, r=POOL_PAST)
                u8 = z[:, 24 + 2 * g:26 + 2 * g, TP:T]
                d8 = z[:, 32 + 2 * g:34 + 2 * g, TP:T]
                step(nc.vector.tensor_reduce(wsum[:, :, :], past[:, :, :, POOL_PAST - w + 1:POOL_PAST], AX.X, ALU.add))
                step(nc.vector.tensor_tensor(wsum[:, :, :], wsum[:, :, :], u8, ALU.add))
                last = nc.vector.scalar_tensor_tensor(d8, wsum[:, :, :], 1.0 / w, u8, ALU.mult, ALU.subtract)
                if g < 3:
                    step(last)
            last.then_inc(past_taken, 1)
            fill("past")

            def recurrence(q):
                hd = HEADS[q]
                nv, dv, zq, zk, zv = hd["nv"], hd["dv"], hd["q"], hd["k"], hd["v"]

                fill(f"vt{q}")
                dve.wait_ge(dec8_ready, q + 1)
                for b in range(NS):
                    dve.wait_ge(kv_psum, NS * q + b + 1)
                    dve.wait_ge(st_in[b % hd["bufs"]], 16 * transfers(q, b))
                    for h in range(HG):
                        o = h * dv
                        s_ = state(q, b)[:, o:o + dv]
                        last = nc.vector.scalar_tensor_tensor(s_, s_, decay8[:, h, b:b + 1],
                                                              kv_bank(q, b, o), ALU.mult, ALU.add)
                    last.then_inc(st_ready, 1)
                    fill(f"kv{q}_{b}")
                dve.wait_ge(o8_psum, NS * (q + 1))
                nc.vector.tensor_copy(z[:, zv:zv + nv, TP:T], pm[:, 3, 0:nv * NS].rearrange("p (j b) -> p j b", b=NS)).then_inc(o8_taken, 1)
                for b in range(NS - hd["bufs"], NS):
                    dve.wait_ge(st_out[b % hd["bufs"]], 16 * transfers(q, b))

                def take(i):
                    dve.wait_ge(sc_psum, SETS * q + i + 1)
                    if i:
                        dve.wait_ge(sc_taken, SETS * q + i)
                    for c in range(NCH):
                        prod = pm[:, 2 * (i % 2) + c, :].rearrange("p (h t) -> p h t", h=HG)
                        if i == 0:
                            last = nc.vector.tensor_tensor(scores[:, c, :, :], prod,
                                                           ident[:, :].unsqueeze(1).broadcast_to([P, HG, CH]), ALU.mult)
                        else:
                            last = nc.vector.copy_predicated(scores[:, c, :, :],
                                                             masks[:, i - 1, :].unsqueeze(1).broadcast_to([P, HG, CH]), prod)
                    last.then_inc(sc_taken, 1)

                take(0)
                fill(f"lv{q}_0")
                for lv in range(LEVELS):
                    w = 1 << lv
                    dve.wait_ge(exp_ready, (LEVELS + 2) * q + lv + 1)
                    dl, _ = halves(dec[:, lv % 2, :, :], w)
                    fl, _ = halves(fac[:, lv % 2, :, :], w)
                    kl, _ = halves(z[:, zk:zk + HG, 0:TP], w)
                    left, right = halves(logp[:, :, 0:TP], w)
                    mid = left[:, :, :, w - 1:w].broadcast_to([P, HG, TP // (2 * w), w])
                    nc.vector.tensor_tensor(right, right, mid, ALU.add).then_inc(prefix_ready, 1)
                    nc.vector.tensor_tensor(fl, kl, dl, ALU.mult).then_inc(fac_ready, 1)
                    dve.wait_ge(prefix_ready, LEVELS * q + lv + 1)
                    if lv + 1 == LEVELS:
                        dve.wait_ge(right_ready, LEVELS * (q + 1) - 1)
                        dve.wait_ge(fac_ready, (LEVELS + 2) * q + LEVELS - 1)
                        lp = logp[:, :, 0:TP].rearrange("p h (c t) -> p h c t", c=NCH)
                        end = lp[:, :, :, CH - 1:CH].broadcast_to([P, HG, NCH, CH])
                        nc.vector.tensor_tensor(dec[:, 1, :, :].rearrange("p h (c t) -> p h c t", c=NCH), end, lp,
                                                ALU.subtract).then_inc(end_ready, 1)
                    if lv:
                        take(lv)
                        fill(f"lv{q}_{lv}")
                dve.wait_ge(exp_ready, (LEVELS + 2) * q + LEVELS + 1)
                nc.vector.tensor_tensor(fac[:, 1, :, :], z[:, zk:zk + HG, 0:TP], dec[:, 1, :, :], ALU.mult).then_inc(fac_ready, 1)
                take(LEVELS)
                fill(f"lv{q}_{LEVELS}")
                dve.wait_ge(exp_ready, (LEVELS + 2) * (q + 1))
                nc.vector.tensor_tensor(fac[:, 0, :, 0:CH], z[:, zq:zq + HG, CH:TP], dec[:, 0, :, 0:CH], ALU.mult).then_inc(fac_ready, 1)
                fill(f"kd{q}")
                dve.wait_ge(kv1_psum, q + 1)
                dve.wait_ge(s1_ready, q + 1)
                if q == 2:
                    dve.wait_ge(small_out, 16 * (SMALL_OUTS - 1))
                for h in range(HG):
                    o = h * dv
                    last = nc.vector.scalar_tensor_tensor(s2[:, o:o + dv], s1[:, o:o + dv], dec[:, 0, h, CH - 1:CH],
                                                          pm[:, o // 512, o % 512:o % 512 + dv], ALU.mult, ALU.add)
                last.then_inc(s2_ready, 1)
                for jj in range(nv // 2):
                    fill(f"o{q}_{jj}")

            def mix_low(n, batches):
                for i, (dst, src) in enumerate(batches):
                    dve.wait_ge(mix_hi, n + i + 1)
                    nc.vector.tensor_tensor(h_lo[:, dst:dst + 4, :], z[:, src:src + 4, :],
                                            h_hi[:, dst:dst + 4, :].bitcast(F32), ALU.subtract).then_inc(mix_ready, 1)

            recurrence(0)
            fill("pool")
            dve.wait_ge(ors_ready, 1)
            gn = VB["ev_gla_norm"]
            for m in range(2):
                o_ = z[:, 8 + m:16:2, :]
                last = nc.vector.scalar_tensor_tensor(o_, o_, vb[:, gn + m:gn + m + 1], logp[:, :, :], ALU.mult, ALU.mult)
            step(last)
            dve.wait_ge(silu_ready, 1)
            for i in range(2):
                a = 8 + 4 * i
                nc.vector.tensor_tensor(z[:, a:a + 4, :], z[:, a:a + 4, :], z[:, a + 8:a + 12, :], ALU.mult).then_inc(mix_f32, 1)
            fill("oss")
            fill_end("ada0b")
            mix_low(0, [(8, 40), (12, 44), (0, 8), (4, 12)])
            n1 = PLAN["out0"][2]
            split(n1, 0)
            a1, m1 = PLAN["up0_0"][2:4]
            dve.wait_ge(mod_ready, m1)
            lo_phase(8, n1, res_evac(0, 0, G1), last_next=a1)
            gains(1, 0, VA["norm_mlp"], SC2)
            modulate(1, 0, SH2)

            def mlp_layer(l, r0, after_next):
                _, _, g0, a0 = PLAN["up0_0" if l == 0 else "up1_0"]

                def chunk(f, last_chunk):
                    g, a = g0 + CHUNK_GROUPS[l] * f, a0 + 4 * f
                    up_e, down_e = up_evac(8 * (FF_CHUNKS * l + f)), res_evac(r0 + 8 * f, l, G2)
                    if l == 0:
                        mixed(a, g, up_e, g + 10)
                        mixed(a + 2, g + 10, down_e, after_next if last_chunk else g + 20)
                    else:
                        lo_phase(8, g, up_e, last_next=g + 8)
                        lo_phase(8, g + 8, down_e, last_next=after_next if last_chunk else g + 16)

                with dve.Fori(0, FF_CHUNKS - 1) as f:
                    chunk(f, False)
                chunk(FF_CHUNKS - 1, True)

            mlp_layer(0, 8, PLAN["glu"][2])
            gains(2, 1, VA["norm_mix"] + KT, SC1)
            n2 = PLAN["glu"][2]
            modulate(2, 1, SH1)
            dve.wait_ge(cw_psum, 1)
            nc.vector.tensor_copy(conv_w[:, :, :], pm[:, 0, 0:8 * TAPS].rearrange("p (j r) -> p j r", r=TAPS)).then_inc(conv_step, 1)
            n3 = PLAN["in1"][2]
            lo_phase(8, n2, z_evac(32), last_next=n3)
            dve.wait_ge(gb_sig, 1)
            dve.wait_ge(conv_step, 1)
            nc.vector.tensor_tensor(z[:, 32:40, :], z[:, 32:40, :], z[:, 40:48, :], ALU.mult).then_inc(cv_in, 1)
            dve.wait_ge(cv_in, 1)

            PER_BLOCK = TAPS + 1

            def conv(j, s):
                src = zf[:, bass.ds((32 + j) * T, TP)]
                acc = [zf[:, bass.ds((40 + j) * T, TP)], acc1[:, :]]
                base = 1 + PER_BLOCK * j
                for shift in range(4 * s, min(4 * s + 4, TAPS)):
                    tap = TAPS - 1 - shift
                    wt = conv_w[:, bass.ds(j, 1), tap:tap + 1].rearrange("p a t -> p (a t)")
                    a = acc[shift % 2]
                    if shift == 0:
                        bias = vb[:, bass.ds(VB["od_conv_b"] + j, 1)]
                        ins = nc.vector.tensor_scalar(a, src, wt, bias, ALU.mult, ALU.add)
                    elif shift == 1:
                        dve.wait_ge(conv_step, base)
                        nc.vector.memset(a[:, 0:1], 0.0)
                        ins = nc.vector.tensor_scalar(a[:, 1:TP], src[:, 0:TP - 1], wt, None, ALU.mult)
                    else:
                        dve.wait_ge(conv_step, base + (shift - 1))
                        ins = nc.vector.scalar_tensor_tensor(a[:, shift:TP], src[:, 0:TP - shift], wt, a[:, shift:TP],
                                                             ALU.mult, ALU.add)
                    ins.then_inc(conv_step, 1)
                if s == 7:
                    dve.wait_ge(conv_step, base + TAPS)
                    nc.vector.tensor_tensor(acc[0], acc[0], acc[1], ALU.add).then_inc(conv_step, 1)

            lo_phase(16, n3, None, loop_work=conv)
            dve.wait_ge(evacuated, n3 + 16)
            for j in range(8):
                dve.wait_ge(past_psum, 2 + j)
                wj = conv_w[:, j, 0:CONV_PAST].unsqueeze(1).broadcast_to([P, NS, CONV_PAST])
                past = pm[:, j % 2, 0:NS * CONV_PAST].rearrange("p (b r) -> p b r", r=CONV_PAST)
                nc.vector.tensor_tensor(cprod[:, :, :], past, wj, ALU.mult).then_inc(past_taken, 1)
                dve.wait_ge(past_taken, 2 + j)
                step(nc.vector.tensor_reduce(t8[:, j, :], cprod[:, :, :], AX.X, ALU.add))
            new, cb = t8[:, 8:16, :], VB["od_conv_b"]
            step(nc.vector.tensor_tensor(new, z[:, 32:40, TP:T], conv_w[:, :, TAPS - 1:TAPS].broadcast_to([P, 8, NS]), ALU.mult))
            step(nc.vector.tensor_tensor(new, new, t8[:, 0:8, :], ALU.add))
            nc.vector.tensor_tensor(z[:, 40:48, TP:T], new, vb[:, cb:cb + 8].unsqueeze(2).broadcast_to([P, 8, NS]),
                                    ALU.add).then_inc(cv_done, 1)

            def gate_inputs(q):
                zk = HEADS[q]["k"]
                dve.wait_ge(sig_ready, q)
                for h in range(HG):
                    c = HEADS[q]["q"] + h
                    nc.vector.tensor_scalar(z[:, zk + h, :], z[:, zk + h, :], oml[:, c:c + 1], None, ALU.mult)
                    last = nc.vector.tensor_scalar(logp[:, h, :], logp[:, h, :], oml[:, c:c + 1], lb[:, c:c + 1], ALU.mult, ALU.add)
                last.then_inc(k_ready, 1)
                dve.wait_ge(k_ready, q)
                nc.vector.tensor_scalar(gzf, lpf, MIN_GATE, 1.0 / TWO60, ALU.max, ALU.max)
                step(nc.vector.tensor_scalar(lpf, lpf, MIN_GATE, TWO60, ALU.max, ALU.mult))
                nc.vector.tensor_scalar(lpf, lpf, 1.0, None, ALU.min).then_inc(ln_in, 1)

            def log_decays(q):
                dve.wait_ge(ln_out, q)
                nc.vector.tensor_tensor(lpf, lpf, gzf, ALU.add).then_inc(logp_ready, 1)
                dve.wait_ge(logp_ready, q + 1)

            gate_inputs(1)
            dve.wait_ge(ln_mean, 1)
            dve.wait_ge(conv_step, 1 + 8 * PER_BLOCK)
            cvz = z[:, 40:48, :]
            nc.vector.tensor_tensor(cvz, cvz, mean[:, :].unsqueeze(1).broadcast_to([P, 8, T]), ALU.subtract).then_inc(ln_cent, 1)
            log_decays(1)
            fill("ln1")
            dve.wait_ge(ln_rstd, 1)
            step(nc.vector.tensor_tensor(cvz, cvz, rstd[:, :].unsqueeze(1).broadcast_to([P, 8, T]), ALU.mult))
            for j in range(8):
                g_, b_ = VB["od_ln_g"] + j, VB["od_ln_b"] + j
                last = nc.vector.tensor_scalar(z[:, 40 + j, :], z[:, 40 + j, :], vb[:, g_:g_ + 1], vb[:, b_:b_ + 1], ALU.mult, ALU.add)
            last.then_inc(ln_done, 1)
            fill("ln2")
            recurrence(1)
            gate_inputs(2)
            log_decays(2)
            fill("gates2")
            recurrence(2)
            dve.wait_ge(ors_ready, 3)
            hn = VB["od_hgrn_norm"]
            step(nc.vector.scalar_tensor_tensor(z[:, 16:24, :], z[:, 16:24, :], vb[:, hn:hn + 1], z[:, 8:16, :], ALU.mult, ALU.mult))
            dve.wait_ge(silu_ready, 2)
            for i in range(2):
                a = 16 + 4 * i
                nc.vector.tensor_tensor(z[:, a:a + 4, :], z[:, a:a + 4, :], z[:, a + 8:a + 12, :], ALU.mult).then_inc(mix_f32, 1)
            fill("oss1")
            fill_end("ada1b")
            mix_low(4, [(8, 40), (12, 44), (0, 16), (4, 20)])
            n4 = PLAN["out1"][2]
            split(n4, 0)
            dve.wait_ge(mod_ready, 96)
            lo_phase(8, n4, res_evac(40, 1, G1), last_next=n4 + 8)
            gains(3, 1, VA["norm_mlp"] + KT, SC2)
            modulate(3, 1, SH2)
            mlp_layer(1, 48, None)
            dve.wait_ge(rstd_ready, 5)
            for k in range(KT):
                c = VA["norm_final"] + k
                nc.vector.scalar_tensor_tensor(x[:, k, :], x[:, k, :], va[:, c:c + 1], rstd[:, :], ALU.mult, ALU.mult).then_inc(y_ready, 1)


INPUTS = ["x_prompt", "x_sample", "c_prompt", "c_sample", "state_gla", "state_pool", "state_hgrn", "state_conv",
          "w_ada", "b_ada", "norm_mix", "norm_mlp", "norm_final", "ev_w_in", "ev_w_gate_up", "ev_b_gate",
          "ev_gla_norm", "ev_pool_w", "ev_pool_scale", "ev_w_out", "od_w_in", "od_lb_raw", "od_hgrn_norm",
          "od_conv_w", "od_conv_b", "od_ln_g", "od_ln_b", "od_w_out", "mlp_w_up", "mlp_w_down"]
OUTPUTS = [("y_prompt", (1, 256, 2048)), ("y_sample", (8, 1, 2048)),
           ("new_gla_prompt", (1, 1, 4, 128, 256)), ("new_pool_prompt", (1, 1, 15, 1024)),
           ("new_hgrn_prompt", (1, 1, 8, 128, 128)), ("new_conv_prompt", (1, 1, 30, 1024)),
           ("new_gla_sample", (1, 8, 4, 128, 256)), ("new_pool_sample", (1, 8, 15, 1024)),
           ("new_hgrn_sample", (1, 8, 8, 128, 128)), ("new_conv_sample", (1, 8, 30, 1024))]


def kernel(**inputs):
    import concourse.bacc as bacc
    from concourse.bass_utils import run_bass_kernel_spmd

    nc = bacc.Bacc("TRN2", target_bir_lowering=False, num_devices=1)
    arrays, io, out = {}, {}, {}
    for name, a in list((n, inputs[n]) for n in INPUTS) + list(constants().items()):
        a = np.ascontiguousarray(a)
        arrays[f"in_{name}"] = a
        io[name] = nc.dram_tensor(f"in_{name}", a.shape, mybir.dt.from_np(a.dtype), kind="ExternalInput").ap()
    for name, shape in OUTPUTS:
        out[name] = nc.dram_tensor(f"out_{name}", shape, F32, kind="ExternalOutput").ap()
    build(nc, io, out)
    r = run_bass_kernel_spmd(nc, [arrays], core_ids=[0])
    return tuple(r.results[0][f"out_{name}"] for name, _ in OUTPUTS)
```
